# Optimizing a Trainium2 kernel written in Bass

```python
import jax, jax.numpy as jnp
from jax import lax
import numpy as np

D_MODEL = 1024
BATCH = 1
SEQ = 256
DEPTH = 2

GRID_W = 64
CTX_LEN = 256

N_HEADS = 8
QK_NOPE = 64
QK_ROPE = 32
V_DIM = 64
Q_RANK = 384
KV_RANK = 256
QK_DIM = QK_NOPE + QK_ROPE
ROPE_BASE = 10000.0
Q_BLOCK = 128
CONV_WIDTH = 512
CONV_K = 3
FOURIER_GROUPS = 4
FOURIER_GROUP_CH = 128
FOURIER_WIDTH = FOURIER_GROUPS * FOURIER_GROUP_CH
N_EXPERTS = 32
TOP_K = 4
F_EXPERT = 256
F_SHARED = 256
ROUTED_SCALE = 2.5
N_BRANCHES = 3
EPS = 1e-6

KV_END = KV_RANK + QK_ROPE
Q_END = KV_END + Q_RANK
CB_END = Q_END + CONV_WIDTH
CC_END = CB_END + CONV_WIDTH
CX_END = CC_END + CONV_WIDTH
FOUR_END = CX_END + FOURIER_WIDTH
PROJ_WIDTH = FOUR_END + N_BRANCHES * D_MODEL

kernel_name = "hybrid_mla_conv_fourier_moe_dit"

def rms_norm(x, g):
    xf = x.astype(jnp.float32)
    y = xf * lax.rsqrt(jnp.mean(xf * xf, axis=-1, keepdims=True) + EPS)
    return (y * g.astype(jnp.float32)).astype(x.dtype)

def modulate(h, shift, scale):
    return h * (1 + scale) + shift

def rope_tables(n):
    rows = n // GRID_W
    r, col = jnp.meshgrid(jnp.arange(rows), jnp.arange(GRID_W), indexing="ij")
    r = r.reshape(-1).astype(jnp.float32)
    col = col.reshape(-1).astype(jnp.float32)
    pairs = QK_ROPE // 4
    inv = ROPE_BASE ** (-jnp.arange(pairs, dtype=jnp.float32) / pairs)
    ang = jnp.concatenate([r[:, None] * inv, col[:, None] * inv], axis=-1)
    return jnp.cos(ang), jnp.sin(ang)

def apply_rope(x, cos, sin):
    half = QK_ROPE // 2
    xf = x.astype(jnp.float32)
    x1, x2 = xf[..., :half], xf[..., half:]
    return jnp.concatenate([x1 * cos - x2 * sin, x2 * cos + x1 * sin], axis=-1).astype(x.dtype)

def mla_kv(p_kv, g_kv, w_ukv, rope):
    B, N, _ = p_kv.shape
    ckv = rms_norm(p_kv[..., :KV_RANK], g_kv)
    k_pe = p_kv[..., KV_RANK:]
    if rope is not None:
        k_pe = apply_rope(k_pe, rope[0], rope[1])
    kv = (ckv @ w_ukv).reshape(B, N, N_HEADS, QK_NOPE + V_DIM)
    k_nope, v = kv[..., :QK_NOPE], kv[..., QK_NOPE:]
    k_pe = jnp.broadcast_to(k_pe[:, :, None, :], (B, N, N_HEADS, QK_ROPE))
    return jnp.concatenate([k_nope, k_pe], axis=-1), v

def mla_q(p_q, g_q, w_uq, rope):
    B, N, _ = p_q.shape
    cq = rms_norm(p_q, g_q)
    q = (cq @ w_uq).reshape(B, N, N_HEADS, QK_DIM)
    if rope is not None:
        q_pe = apply_rope(q[..., QK_NOPE:], rope[0][:, None, :], rope[1][:, None, :])
        q = jnp.concatenate([q[..., :QK_NOPE], q_pe], axis=-1)
    return q

def attention(q, k, v):
    B, N, H, _ = q.shape
    nb = N // Q_BLOCK
    qb = q.reshape(B, nb, Q_BLOCK, H, QK_DIM).swapaxes(0, 1)
    scale = QK_DIM ** -0.5

    def one_block(qblk):
        s = jnp.einsum("bqhd,bkhd->bhqk", qblk, k).astype(jnp.float32) * scale
        p = jax.nn.softmax(s, axis=-1)
        return jnp.einsum("bhqk,bkhv->bqhv", p.astype(v.dtype), v)

    o = lax.map(one_block, qb)
    return o.swapaxes(0, 1).reshape(B, N, H * V_DIM)

def short_conv(b_gate, c_gate, u, w_conv):
    N = u.shape[1]
    pad = CONV_K // 2
    inner = jnp.pad(c_gate * u, ((0, 0), (pad, pad), (0, 0)))
    y = sum(inner[:, j:j + N] * w_conv[j] for j in range(CONV_K))
    return b_gate * y

def fourier_mix(u):
    B, N, _ = u.shape
    ug = u.astype(jnp.float32).reshape(B, N, FOURIER_GROUPS, FOURIER_GROUP_CH)
    f = jnp.fft.fft2(ug, axes=(1, 3), norm="ortho").real
    return f.reshape(B, N, FOURIER_WIDTH).astype(u.dtype)

def mix_stream(proj, k_read, v_read, rope, prm):
    q = mla_q(proj[..., KV_END:Q_END], prm["g_q"], prm["w_uq"], rope)
    y_attn = attention(q, k_read, v_read) @ prm["w_mla_out"]
    y_conv = short_conv(proj[..., Q_END:CB_END], proj[..., CB_END:CC_END],
                        proj[..., CC_END:CX_END], prm["conv_w"]) @ prm["w_conv_out"]
    y_four = fourier_mix(proj[..., CX_END:FOUR_END]) @ prm["w_four_out"]
    gates = jax.nn.sigmoid(proj[..., FOUR_END:] + prm["b_gate"])
    g_a, g_c, g_f = jnp.split(gates, N_BRANCHES, axis=-1)
    return (g_a * y_attn + g_c * y_conv + g_f * y_four) @ prm["w_out"]

def moe(h, prm):
    B, N, D = h.shape
    t = h.reshape(B * N, D)
    scores = jax.nn.sigmoid((t @ prm["w_router"]).astype(jnp.float32))
    _, idx = lax.top_k(scores + prm["b_router"].astype(jnp.float32), TOP_K)
    sel = jnp.take_along_axis(scores, idx, axis=-1)
    w = sel / jnp.sum(sel, axis=-1, keepdims=True) * ROUTED_SCALE
    comb = jnp.sum(jax.nn.one_hot(idx, N_EXPERTS, dtype=jnp.float32) * w[..., None], axis=1)
    gate = jnp.einsum("td,edf->tef", t, prm["w_gate_e"])
    up = jnp.einsum("td,edf->tef", t, prm["w_up_e"])
    act = jax.nn.silu(gate) * up * comb[..., None].astype(t.dtype)
    routed = jnp.einsum("tef,efd->td", act, prm["w_down_e"])
    shared = (jax.nn.silu(t @ prm["w_gate_s"]) * (t @ prm["w_up_s"])) @ prm["w_down_s"]
    return (routed + shared).reshape(B, N, D)

def layer(x, ctx, ada_x, ada_c, prm, rope, ctx_out):
    sh1x, sc1x, g1x, sh2x, sc2x, g2x = jnp.split(ada_x[:, None, :], 6, axis=-1)
    sh1c, sc1c, g1c, sh2c, sc2c, g2c = jnp.split(ada_c, 6, axis=-1)
    hx = modulate(rms_norm(x, prm["g_pre_mix"]), sh1x, sc1x)
    hc = modulate(rms_norm(ctx, prm["g_pre_mix"]), sh1c, sc1c)
    px = hx @ prm["w_in"]
    if ctx_out:
        pc = hc @ prm["w_in"]
        pc_kv = pc[..., :KV_END]
    else:
        pc_kv = hc @ prm["w_in"][:, :KV_END]
    kc, vc = mla_kv(pc_kv, prm["g_kv"], prm["w_ukv"], None)
    kx, vx = mla_kv(px[..., :KV_END], prm["g_kv"], prm["w_ukv"], rope)
    k_all = jnp.concatenate([kc, kx], axis=1)
    v_all = jnp.concatenate([vc, vx], axis=1)
    yx = mix_stream(px, k_all, v_all, rope, prm)
    x = x + g1x * rms_norm(yx, prm["g_post_mix"])
    hx2 = modulate(rms_norm(x, prm["g_pre_ffn"]), sh2x, sc2x)
    x = x + g2x * rms_norm(moe(hx2, prm), prm["g_post_ffn"])
    if ctx_out:
        yc = mix_stream(pc, kc, vc, None, prm)
        ctx = ctx + g1c * rms_norm(yc, prm["g_post_mix"])
        hc2 = modulate(rms_norm(ctx, prm["g_pre_ffn"]), sh2c, sc2c)
        ctx = ctx + g2c * rms_norm(moe(hc2, prm), prm["g_post_ffn"])
    return x, ctx

def setup_inputs(seed: int = 0) -> dict:
    key = jax.random.key(seed)
    ks = jax.random.split(key, 29)
    f32 = jnp.float32

    def nrm(k, shape, scale):
        return jax.random.normal(k, shape, f32) * scale

    D, L = D_MODEL, DEPTH
    return {
        "x": nrm(ks[0], (BATCH, SEQ, D), 1.0),
        "c": nrm(ks[1], (BATCH, D), 1.0),
        "ctx": nrm(ks[2], (BATCH, CTX_LEN, D), 1.0),
        "c_ctx": nrm(ks[3], (D,), 1.0),
        "w_ada": nrm(ks[4], (L, D, 6 * D), 0.5 * D ** -0.5),
        "b_ada": nrm(ks[5], (L, 6 * D), 0.02),
        "g_pre_mix": 1.0 + nrm(ks[6], (L, D), 0.02),
        "g_post_mix": 1.0 + nrm(ks[7], (L, D), 0.02),
        "g_pre_ffn": 1.0 + nrm(ks[8], (L, D), 0.02),
        "g_post_ffn": 1.0 + nrm(ks[9], (L, D), 0.02),
        "w_in": nrm(ks[10], (L, D, PROJ_WIDTH), D ** -0.5),
        "b_gate": nrm(ks[11], (L, N_BRANCHES * D), 0.02),
        "g_q": 1.0 + nrm(ks[12], (L, Q_RANK), 0.02),
        "w_uq": nrm(ks[13], (L, Q_RANK, N_HEADS * QK_DIM), Q_RANK ** -0.5),
        "g_kv": 1.0 + nrm(ks[14], (L, KV_RANK), 0.02),
        "w_ukv": nrm(ks[15], (L, KV_RANK, N_HEADS * (QK_NOPE + V_DIM)), KV_RANK ** -0.5),
        "w_mla_out": nrm(ks[16], (L, N_HEADS * V_DIM, D), (N_HEADS * V_DIM) ** -0.5),
        "conv_w": nrm(ks[17], (L, CONV_K, CONV_WIDTH), CONV_K ** -0.5),
        "w_conv_out": nrm(ks[18], (L, CONV_WIDTH, D), CONV_WIDTH ** -0.5),
        "w_four_out": nrm(ks[19], (L, FOURIER_WIDTH, D), FOURIER_WIDTH ** -0.5),
        "w_out": nrm(ks[20], (L, D, D), D ** -0.5),
        "w_router": nrm(ks[21], (L, D, N_EXPERTS), D ** -0.5),
        "b_router": nrm(ks[22], (L, N_EXPERTS), 0.01),
        "w_gate_e": nrm(ks[23], (L, N_EXPERTS, D, F_EXPERT), D ** -0.5),
        "w_up_e": nrm(ks[24], (L, N_EXPERTS, D, F_EXPERT), D ** -0.5),
        "w_down_e": nrm(ks[25], (L, N_EXPERTS, F_EXPERT, D), F_EXPERT ** -0.5),
        "w_gate_s": nrm(ks[26], (L, D, F_SHARED), D ** -0.5),
        "w_up_s": nrm(ks[27], (L, D, F_SHARED), D ** -0.5),
        "w_down_s": nrm(ks[28], (L, F_SHARED, D), F_SHARED ** -0.5),
    }

def reference(x, c, ctx, c_ctx, w_ada, b_ada, g_pre_mix, g_post_mix, g_pre_ffn, g_post_ffn,
              w_in, b_gate, g_q, w_uq, g_kv, w_ukv, w_mla_out, conv_w, w_conv_out, w_four_out,
              w_out, w_router, b_router, w_gate_e, w_up_e, w_down_e, w_gate_s, w_up_s, w_down_s):
    rope = rope_tables(x.shape[1])
    for l in range(DEPTH):
        prm = {
            "g_pre_mix": g_pre_mix[l], "g_post_mix": g_post_mix[l],
            "g_pre_ffn": g_pre_ffn[l], "g_post_ffn": g_post_ffn[l],
            "w_in": w_in[l], "b_gate": b_gate[l],
            "g_q": g_q[l], "w_uq": w_uq[l], "g_kv": g_kv[l], "w_ukv": w_ukv[l],
            "w_mla_out": w_mla_out[l], "conv_w": conv_w[l], "w_conv_out": w_conv_out[l],
            "w_four_out": w_four_out[l], "w_out": w_out[l],
            "w_router": w_router[l], "b_router": b_router[l],
            "w_gate_e": w_gate_e[l], "w_up_e": w_up_e[l], "w_down_e": w_down_e[l],
            "w_gate_s": w_gate_s[l], "w_up_s": w_up_s[l], "w_down_s": w_down_s[l],
        }
        ada_x = jax.nn.silu(c) @ w_ada[l] + b_ada[l]
        ada_c = jax.nn.silu(c_ctx) @ w_ada[l] + b_ada[l]
        x, ctx = layer(x, ctx, ada_x, ada_c, prm, rope, l < DEPTH - 1)
    return x


_drawn_inputs = setup_inputs


def setup_inputs(seed=0):
    import zlib

    import numpy as np

    out = dict(_drawn_inputs(seed))
    spreads = {}
    factors = {'g_post_ffn': 4.169, 'b_gate': 3.202, 'g_q': 8.0, 'g_kv': 8.0}
    for name, (base, spread) in spreads.items():
        noise = np.random.default_rng([zlib.crc32(name.encode()), seed]).standard_normal(out[name].shape)
        drawn = base * np.exp(spread * noise) if base else spread * noise
        out[name] = __import__('jax').numpy.asarray(drawn.astype(out[name].dtype))
    for name, factor in factors.items():
        out[name] = (out[name] * factor).astype(out[name].dtype)
    return out
```

```python
import numpy as np
import concourse.bass as bass
from concourse import mybir
from concourse.alu_op_type import AluOpType as ALU
from contextlib import ExitStack

DM, DEPTH, GRID_W = 1024, 2, 64
H, NOPE, ROPE, VD = 8, 64, 32, 64
QK = NOPE + ROPE
QR, KVR = 384, 256
CONV = 512
FG, FC = 4, 128
NE, TOPK, FE = 32, 4, 256
ROUTED_SCALE, EPS = 2.5, 1e-6
ROPE_BASE = 10000.0
P = 128
KC = DM // P
NTILE = 4
SEQ = 256
KV_END = KVR + ROPE
Q_END = KV_END + QR
FOUR_END = Q_END + 3 * CONV + FG * FC
SLOTS = 4
BANKS = 8
ATT_SCALE = QK ** -0.5
ACTIVE = [NTILE, 2]


class Groups:

    def __init__(self):
        self.at, self.count, self.emptied_at = {}, {"act": 0, "dve": 0}, []

    def add(self, owner, *key):
        self.at[key] = len(self.emptied_at)
        self.count[owner] += 1
        self.emptied_at.append((owner, self.count[owner]))


def attention_units(l):
    return [(h, s) for h in range(H) for s in range(ACTIVE[l] // 2)]


def plan():
    g = Groups()
    alternate = lambda k: "act" if k % 2 else "dve"
    for l in range(DEPTH):
        act = ACTIVE[l]
        for r in range(3):
            g.add("dve", l, "ada", r)
        for r in range(3):
            g.add("act", l, "adaT", r)
        for n in (1, 2):
            for s in range(act // 2):
                for j in range(2):
                    g.add("dve", l, "gaterow", n, s, j)
        for k in range(KC):
            g.add(alternate(k), l, "h", 1, k)
        for t in range(NTILE):
            g.add("act", l, "kv", t)
            if t < act:
                g.add("act", l, "q", t)
        for name, owner in (("b", "act"), ("c", "act"), ("u", "dve"), ("f", "act")):
            for f in range(4):
                g.add(owner, l, name, f)
        for c in range(2):
            g.add("dve", l, "ckvT", c)
        for c in range(3):
            g.add("act", l, "cqT", c)
        for t in range(NTILE):
            for j in range(2):
                g.add("act", l, "kvup", t, j)
        for t in range(act):
            for j in range(2):
                g.add("dve", l, "qup", t, j)
        for f in range(FG):
            for s in range(act // 2):
                g.add("act", l, "four1", f, s)
        for f in range(FG):
            g.add("dve", l, "four2", f)
        units = attention_units(l)
        for u in range(len(units) + 1):
            if u < len(units):
                h, s = units[u]
                if s == 0:
                    g.add("dve", l, "kT", h)
                    g.add("act", l, "qT", h)
                for t in range(2):
                    g.add("act", l, "S", h, s, t)
            if u >= 1:
                h, s = units[u - 1]
                for t in range(2):
                    g.add(alternate(t), l, "PT", h, s, t)
                g.add("dve", l, "O", h, s)
        for b in range(3):
            for dc in range(KC):
                g.add("act", l, "g", b, dc)
                g.add("dve", l, "y", b, dc)
        for t in range(act):
            for j in range(2):
                g.add("act", l, "out", t, j)
        for k in range(KC):
            g.add(alternate(k), l, "h", 2, k)
        for t in range(act):
            g.add("act", l, "rt", t)
    return g


def hybrid_layers(nc, I, C, out):
    f32, u32 = mybir.dt.float32, mybir.dt.uint32
    ACT, AX = mybir.ActivationFunctionType, mybir.AxisListType.X
    G = plan()
    ctx = ExitStack()

    def sb(name, shape, dt=f32):
        return ctx.enter_context(nc.sbuf_tensor(name, shape, dt))

    def one(name):
        return ctx.enter_context(nc.semaphore(name))

    def by_layer(name):
        return [one(f"{name}_{l}") for l in range(DEPTH)]

    with ctx:
        xres = sb("xres", [P, NTILE, DM])
        hT = sb("hT", [P, KC, NTILE * P])
        ring = sb("ring", [P, SLOTS, 4096])
        bT = sb("bT", [P, 4, 512])
        cT = sb("cT", [P, 4, 512])
        fT = sb("fT", [P, 4, 512])
        tmp2 = sb("tmp2", [P, 2, 512])
        qkv = sb("qkv", [P, 8192])
        head = sb("head", [P, 2048])
        probs_b = sb("probs_b", [P, 2048])
        probsT_b = sb("probsT_b", [P, 2048])
        oT_b = sb("oT_b", [P, 2048])
        Grow = sb("Grow", [P, 2, 2, DM])
        ident = sb("ident", [P, P])
        rope_t = sb("rope_t", [P, 2, 2, 16])
        wr = sb("wr", [P, KC, NE])
        small = sb("small", [P, 400])
        used = [0]

        def part(n):
            used[0] += n
            assert used[0] <= 400
            return small[:, used[0] - n:used[0]]

        cs = part(16).rearrange("p (s k) -> p s k", s=2)
        gains = part(16).rearrange("p (n k) -> p n k", k=KC)
        scaleT = part(32).rearrange("p (n s k) -> p n s k", n=2, s=2)
        shiftT = part(32).rearrange("p (n s k) -> p n s k", n=2, s=2)
        gqk = part(5)
        convw = part(12).rearrange("p (j f) -> p j f", j=3)
        bgate = part(24).rearrange("p (b k) -> p b k", b=3)
        ssq = part(24)
        rstd = part(24)
        brow = part(NE)
        iota = part(NE)
        smax, nmax, ssum, sinv = part(4), part(4), part(4), part(4)
        rden = part(4)
        m8 = part(32).rearrange("p (t k) -> p t k", k=8)
        idx8 = part(32).bitcast(u32).rearrange("p (t k) -> p t k", k=8)
        idxf = part(32).rearrange("p (t k) -> p t k", k=8)

        ada_bias = probs_b[:, 0:1536].rearrange("p (r c) -> p r c", r=3)
        ada_row = probsT_b[:, 0:1536].rearrange("p (r c) -> p r c", r=3)
        gpost = oT_b[:, :].rearrange("p (n d) -> p n d", n=2)
        ca32 = head[:, 0:256].rearrange("p (k c) -> p k c", c=32)
        adaT = head[:, 256:352].rearrange("p (r b j s) -> p r b j s", r=3, b=4, j=4)
        dft_c = head[:, 0:256]
        dft_n = head[:, 256:1280].rearrange("p (a c n) -> p a c n", a=2, c=2)
        ropek = head[:, 1280:1408].rearrange("p (t d) -> p t d", t=NTILE)
        rt1 = head[:, 1408:1664].rearrange("p (t h d) -> p t h d", t=2, h=H)
        rt2 = head[:, 1664:1920].rearrange("p (t h d) -> p t h d", t=2, h=H)
        kvlat = probs_b[:, 0:4 * KV_END].rearrange("p (t c) -> p t c", t=4)
        qlat = probsT_b[:, 0:4 * QR].rearrange("p (t c) -> p t c", t=4)
        ckvT = qkv[:, 0:1024].rearrange("p (c t) -> p c t", c=2)
        cqT = oT_b[:, 0:1536].rearrange("p (c t) -> p c t", c=3)
        four_ab = [b[:, 512 * i:512 * i + 512] for b in (probs_b, probsT_b) for i in range(4)]
        qtok = qkv[:, 0:3072].rearrange("p (t h d) -> p t h d", t=4, h=H)
        ktok = qkv[:, 3072:6144].rearrange("p (t h d) -> p t h d", t=4, h=H)
        vtok = qkv[:, 6144:8192].rearrange("p (t h d) -> p t h d", t=4, h=H)
        headT = head[:, :].rearrange("p (b a t) -> p b a t", b=2, a=2)
        probs = probs_b[:, :].rearrange("p (b t k) -> p b t k", b=2, t=2)
        probsT = probsT_b[:, :].rearrange("p (b k t) -> p b k t", b=2, k=4)
        oT = oT_b[:, :].rearrange("p (c t) -> p c t", c=4)
        xn = qkv[:, 4096:8192].rearrange("p (t d) -> p t d", t=NTILE)
        mT = qkv[:, 0:4096].rearrange("p (k t) -> p k t", k=KC)
        ytmp = head[:, 0:1024].rearrange("p (b t) -> p b t", b=2)
        rows = oT_b[:, :].rearrange("p (n d) -> p n d", n=2)
        junk = tmp2[:, :, :].rearrange("p a b -> p (a b)")
        score = bT[:, 0, 0:NTILE * NE].rearrange("p (t e) -> p t e", e=NE)
        biased = bT[:, 1, 0:NTILE * NE].rearrange("p (t e) -> p t e", e=NE)
        comb = bT[:, 2, 0:NTILE * NE].rearrange("p (t e) -> p t e", e=NE)
        onehot = bT[:, 3, :].rearrange("p (t k e) -> p t k e", t=NTILE, k=TOPK)
        silu, actT = cT, fT
        acc = qkv[:, 0:4096].rearrange("p (t d) -> p t d", t=NTILE)
        gu = [ring[:, i, :].rearrange("p (k n) -> p k n", k=KC) for i in range(2)]
        dn = [ring[:, 2 + i, 0:2048].rearrange("p (k n) -> p k n", k=2) for i in range(2)]
        ps = ctx.enter_context(nc.psum_tensor("ps", [P, BANKS * 512], f32))

        psum_full = one("psum_full")
        emptied = {"act": one("emptied_by_act"), "dve": one("emptied_by_dve")}
        x_loaded, consts_loaded, out_stored = one("x_loaded"), one("consts_loaded"), one("out_stored")
        slot_loaded = [one(f"slot_loaded_{i}") for i in range(SLOTS)]
        gu_loaded = [one(f"gu_loaded_{i}") for i in range(2)]
        dn_loaded = [one(f"dn_loaded_{i}") for i in range(2)]
        params_loaded = by_layer("params_loaded")
        adab_zero = by_layer("adab_zero")
        adab_loaded = by_layer("adab_loaded")
        dft_loaded = by_layer("dft_loaded")
        ca_ready = by_layer("ca_ready")
        ssq_ready = by_layer("ssq_ready")
        ms_ready = by_layer("ms_ready")
        root_ready = by_layer("root_ready")
        xn_ready = by_layer("xn_ready")
        coef_ready = by_layer("coef_ready")
        lat_ready = by_layer("lat_ready")
        conv_ready = by_layer("conv_ready")
        kpe_ready = by_layer("kpe_ready")
        qrope_ready = by_layer("qrope_ready")
        max_ready = by_layer("max_ready")
        prob_ready = by_layer("prob_ready")
        merged = by_layer("merged")
        x_updated = by_layer("x_updated")
        comb_ready = by_layer("comb_ready")
        gu_full = by_layer("gu_full")
        silu_ready = by_layer("silu_ready")
        act_ready = by_layer("act_ready")
        dn_full = by_layer("dn_full")
        dn_taken = by_layer("dn_taken")
        dve_step = one("dve_step")

        def wait_full(eng, *key):
            eng.wait_ge(psum_full, G.at[key] + 1)

        def wait_emptied(eng, *key):
            owner, n = G.emptied_at[G.at[key]]
            eng.wait_ge(emptied[owner], n)

        def bank(*key):
            b = G.at[key] % BANKS
            return ps[:, 512 * b:512 * b + 512]

        stream, last_reader = [], []
        for l in range(DEPTH):
            at = lambda w, k0, k1: w[l].rearrange("(k p) n -> p k n", p=P)[:, :, k0:k1]
            last = ACTIVE[l] - 1

            def item(reader, name, chunks, src):
                stream.append(((l, *name), chunks, src.shape[2], src))
                last_reader.append((l, *reader))

            for c in range(12):
                item(("ada", c // 4), ("ada", c), KC, at(I["w_ada"], 512 * c, 512 * c + 512))
            item(("kv", NTILE - 1) if last < NTILE - 1 else ("q", last), ("kv",), KC, at(I["w_in"], 0, KV_END))
            item(("kv", NTILE - 1) if last < NTILE - 1 else ("q", last), ("q",), KC, at(I["w_in"], KV_END, Q_END))
            for n, name in enumerate("bcuf"):
                item((name, 3), (name,), KC, at(I["w_in"], Q_END + CONV * n, Q_END + CONV * (n + 1)))
            item(("kvup", NTILE - 1, 1), ("ukv",), 2, at(I["w_ukv"], 0, 1024))
            item(("qup", last, 1), ("uq",), 3, at(I["w_uq"], 0, 768))
            for b, name in enumerate(["w_mla_out", "w_conv_out", "w_four_out"]):
                item(("y", b, KC - 1), ("branch", b), 4, at(I[name], 0, DM))
                for j in range(2):
                    c0 = FOUR_END + b * DM + 512 * j
                    item(("g", b, 4 * j + 3), ("gate", b, j), KC, at(I["w_in"], c0, c0 + 512))
            for j in range(2):
                item(("out", last, 1), ("out", j), KC, at(I["w_out"], 512 * j, 512 * j + 512))
        item_at = {key: n for n, (key, *_) in enumerate(stream)}
        per_layer = len(stream) // DEPTH

        def slot(*key):
            n = item_at[key]
            _, k, cols, _ = stream[n]
            return ring[:, n % SLOTS, 0:k * cols].rearrange("p (k n) -> p k n", k=k)

        block = ctx.enter_context(nc.Block())

        @block.sync
        def _(sp):
            rows_of = lambda a: a.rearrange("(t p) d -> p t d", p=P)
            sp.dma_start(xres[:, 0:2, :], rows_of(I["x"][0])).then_inc(x_loaded, 16)
            sp.dma_start(xres[:, 2:4, :], rows_of(I["ctx"][0])).then_inc(x_loaded, 16)
            for l in range(DEPTH):
                downs = 2 * ACTIVE[l]
                for n in range(l * per_layer, (l + 1) * per_layer):
                    key, _, _, src = stream[n]
                    if n == l * per_layer and l:
                        sp.wait_ge(dn_full[l - 1], 2 * ACTIVE[l - 1] * (NE + 1))
                    if n - l * per_layer >= SLOTS:
                        wait_full(sp, *last_reader[n - SLOTS])
                    sp.dma_start(slot(*key), src).then_inc(slot_loaded[n % SLOTS], 16)
                wait_full(sp, *last_reader[(l + 1) * per_layer - 1])
                chunks = lambda w: w.rearrange("(k p) n -> p k n", p=P)
                sp.dma_start(gu[0][:, :, 0:FE], chunks(I["w_gate_s"][l])).then_inc(gu_loaded[0], 16)
                sp.dma_start(gu[0][:, :, FE:2 * FE], chunks(I["w_up_s"][l])).then_inc(gu_loaded[0], 16)
                sp.dma_start(dn[0], chunks(I["w_down_s"][l])).then_inc(dn_loaded[0], 16)

                def load_expert(n1, i):
                    j = n1 % 2
                    one_of = lambda w: w[l][bass.ds(2 * i + (n1 - 1), 1)].rearrange("a (k p) n -> p (a k) n", p=P)
                    if n1 > 1:
                        sp.wait_ge(gu_full[l], 4 * i + 2 * (n1 - 1))
                    sp.dma_start(gu[j][:, :, 0:FE], one_of(I["w_gate_e"])).then_inc(gu_loaded[j], 16)
                    sp.dma_start(gu[j][:, :, FE:2 * FE], one_of(I["w_up_e"])).then_inc(gu_loaded[j], 16)
                    if n1 > 1:
                        sp.wait_ge(dn_full[l], 2 * downs * i + downs * (n1 - 1))
                    sp.dma_start(dn[j], one_of(I["w_down_e"])).then_inc(dn_loaded[j], 16)

                load_expert(1, 0)
                with nc.sync.Fori(0, NE // 2 - 1) as i:
                    load_expert(2, i)
                    load_expert(3, i)
                load_expert(NE, 0)
            sp.wait_ge(x_updated[DEPTH - 1], 2 * ACTIVE[DEPTH - 1])
            sp.dma_start(rows_of(out[0]), xres[:, 0:2, :]).then_inc(out_stored, 16)
            sp.wait_ge(out_stored, 16)

        @block.gpsimd
        def _(pool):
            pool.dma_start(ident[:, :], C["ident"]).then_inc(consts_loaded, 16)
            pool.dma_start(rope_t[:, :, :, :], C["rope"]).then_inc(consts_loaded, 16)
            pool.dma_start(iota, C["iota"]).then_inc(consts_loaded, 16)
            col = lambda a: a.rearrange("(k p) -> p k", p=P)
            for l in range(DEPTH):
                act = ACTIVE[l]
                if l:
                    pool.wait_ge(x_updated[l - 1], 2 * ACTIVE[l - 1])
                with nc.allow_non_contiguous_dma("one small vector a partition"):
                    vectors = [(cs[:, 0, :], col(I["c"][0])), (cs[:, 1, :], col(I["c_ctx"])),
                               (gains[:, 0, :], col(I["g_pre_mix"][l])), (gains[:, 1, :], col(I["g_pre_ffn"][l])),
                               (gqk[:, 0:2], col(I["g_kv"][l])), (gqk[:, 2:5], col(I["g_q"][l])),
                               (bgate, I["b_gate"][l].rearrange("(b k p) -> p b k", p=P, b=3)),
                               (wr[:, :, :], I["w_router"][l].rearrange("(k p) e -> p k e", p=P)),
                               (brow, I["b_router"][l:l + 1, :].to_broadcast([P, NE])),
                               (gpost[:, 0, :], I["g_post_mix"][l:l + 1, :].to_broadcast([P, DM])),
                               (gpost[:, 1, :], I["g_post_ffn"][l:l + 1, :].to_broadcast([P, DM]))]
                    vectors += [(convw[:, j, :], col(I["conv_w"][l][j])) for j in range(3)]
                    assert len(vectors) == 14
                    for dst, src in vectors:
                        pool.dma_start(dst, src).then_inc(params_loaded[l], 16)
                nc.gpsimd.memset(ca32, 0.0).then_inc(adab_zero[l], 1)
                nc.gpsimd.memset(ada_bias, 0.0).then_inc(adab_zero[l], 1)
                pool.wait_ge(adab_zero[l], 2)
                for j in range(4):
                    src = I["b_ada"][l].rearrange("(r j c) -> j r c", j=4, c=512)[j:j + 1]
                    for s in range(2):
                        pool.dma_start(ada_bias[32 * j + s:32 * j + s + 1], src).then_inc(adab_loaded[l], 16)
                pool.wait_ge(coef_ready[l], 1)
                pool.dma_start(head[:, 0:1280], C["dft"]).then_inc(dft_loaded[l], 16)
                for b in (1, 2):
                    for dc in range(KC):
                        n = (b - 1) * KC + dc
                        wait_emptied(pool, l, "y", b, dc)
                        if b == 2:
                            pool.wait_ge(merged[l], n - KC + 1)
                        nc.gpsimd.tensor_tensor(mT[:, dc, 0:P * act], mT[:, dc, 0:P * act],
                                                ytmp[:, n % 2, 0:P * act], ALU.add).then_inc(merged[l], 1)

        @block.scalar
        def _(act_e):
            act = None

            for l in range(DEPTH):
                act = ACTIVE[l]
                n_tok = P * act
                roots, squares = [0], [0]

                def square(src, into, width):
                    act_e.wait_ge(ssq_ready[l], squares[0])
                    squares[0] += 1
                    nc.scalar.activation(junk[:, 0:width], src, ACT.Square, accum_out=ssq[:, into:into + 1])\
                        .then_inc(ssq_ready[l], 1)

                def root(c0, c1):
                    roots[0] += 1
                    act_e.wait_ge(ms_ready[l], roots[0])
                    nc.scalar.activation(rstd[:, c0:c1], ssq[:, c0:c1], ACT.Sqrt).then_inc(root_ready[l], 1)

                if l:
                    act_e.wait_ge(ssq_ready[l - 1], last_squares)
                act_e.wait_ge(params_loaded[l], 16 * 14)
                act_e.wait_ge(adab_zero[l], 2)
                nc.scalar.activation(ca32[:, :, 0:2], cs.rearrange("p s k -> p k s"), ACT.Silu).then_inc(ca_ready[l], 1)
                if l == 0:
                    act_e.wait_ge(x_loaded, 32)
                else:
                    act_e.wait_ge(x_updated[l - 1], 2 * ACTIVE[l - 1])
                for t in range(NTILE):
                    square(xres[:, t, :], t, DM)
                root(0, 4)
                for r in range(3):
                    wait_full(act_e, l, "adaT", r)
                    src = bank(l, "adaT", r).rearrange("p (b j m) -> p b j m", b=4, j=4)[:, :, :, 0:2]
                    nc.scalar.activation(adaT[:, r], src, ACT.Copy).then_inc(emptied["act"], 1)

                def modulate(n):
                    act_e.wait_ge(coef_ready[l], 1)
                    for k in range(1, KC, 2):
                        wait_full(act_e, l, "h", n, k)
                        for s in range(2 if n == 1 else act // 2):
                            ins = nc.scalar.activation(hT[:, k, SEQ * s:SEQ * s + SEQ], bank(l, "h", n, k)[:, SEQ * s:SEQ * s + SEQ],
                                                       ACT.Identity, scale=scaleT[:, n - 1, s, k:k + 1],
                                                       bias=shiftT[:, n - 1, s, k:k + 1])
                        ins.then_inc(emptied["act"], 1)

                modulate(1)
                for t in range(NTILE):
                    wait_full(act_e, l, "kv", t)
                    square(bank(l, "kv", t)[:, 0:KVR], 4 + t, KVR)
                    nc.scalar.activation(kvlat[:, t, :], bank(l, "kv", t)[:, 0:KV_END], ACT.Copy).then_inc(emptied["act"], 1)
                    if t < act:
                        wait_full(act_e, l, "q", t)
                        square(bank(l, "q", t)[:, 0:QR], 8 + t, QR)
                        nc.scalar.activation(qlat[:, t, :], bank(l, "q", t)[:, 0:QR], ACT.Copy).then_inc(emptied["act"], 1)
                root(4, 8 + act)
                for name, dst in (("b", bT), ("c", cT)):
                    for f in range(4):
                        wait_full(act_e, l, name, f)
                        nc.scalar.activation(dst[:, f, 0:n_tok], bank(l, name, f)[:, 0:n_tok], ACT.Copy).then_inc(emptied["act"], 1)
                for f in range(4):
                    wait_full(act_e, l, "f", f)
                    nc.scalar.activation(fT[:, f, 0:n_tok], bank(l, "f", f)[:, 0:n_tok], ACT.Copy).then_inc(emptied["act"], 1)
                for c in range(3):
                    wait_full(act_e, l, "cqT", c)
                    nc.scalar.activation(cqT[:, c, 0:n_tok], bank(l, "cqT", c)[:, 0:n_tok], ACT.Identity,
                                         scale=gqk[:, 2 + c:3 + c]).then_inc(emptied["act"], 1)
                for t in range(NTILE):
                    for j in range(2):
                        wait_full(act_e, l, "kvup", t, j)
                        src = bank(l, "kvup", t, j).rearrange("p (h d) -> p h d", h=4)
                        nc.scalar.activation(ktok[:, t, 4 * j:4 * j + 4, 0:NOPE], src[:, :, 0:NOPE], ACT.Copy)
                        nc.scalar.activation(vtok[:, t, 4 * j:4 * j + 4, :], src[:, :, NOPE:], ACT.Copy).then_inc(emptied["act"], 1)
                n = 0
                for f in range(FG):
                    for s in range(act // 2):
                        wait_full(act_e, l, "four1", f, s)
                        nc.scalar.activation(four_ab[n], bank(l, "four1", f, s), ACT.Copy).then_inc(emptied["act"], 1)
                        n += 1
                units = attention_units(l)
                for u in range(len(units) + 1):
                    if u < len(units):
                        h, s = units[u]
                        keys = 512 if s == 0 else 256
                        if s == 0:
                            wait_full(act_e, l, "qT", h)
                            nc.scalar.activation(headT[0:QK, h % 2, 0, 0:n_tok], bank(l, "qT", h)[0:QK, 0:n_tok],
                                                 ACT.Copy).then_inc(emptied["act"], 1)
                        for t in range(2):
                            act_e.wait_ge(max_ready[l], 2 * u + t + 1)
                            if u >= 2:
                                wait_full(act_e, l, "PT", *units[u - 2], t)
                            c = 2 * (u % 2) + t
                            nc.scalar.activation(probs[:, u % 2, t, 0:keys], bank(l, "S", h, s, t)[:, 0:keys], ACT.Exp,
                                                 scale=ATT_SCALE, bias=nmax[:, c:c + 1],
                                                 accum_out=ssum[:, c:c + 1]).then_inc(emptied["act"], 1)
                    if u >= 1:
                        h, s = units[u - 1]
                        nk = 4 if s == 0 else 2
                        wait_full(act_e, l, "PT", h, s, 1)
                        nc.scalar.activation(probsT[:, (u - 1) % 2, 0:nk, P:2 * P],
                                             bank(l, "PT", h, s, 1)[:, 0:P * nk].rearrange("p (k q) -> p k q", q=P),
                                             ACT.Copy).then_inc(emptied["act"], 1)
                for b in range(3):
                    for dc in range(KC):
                        n = b * KC + dc
                        wait_full(act_e, l, "g", b, dc)
                        if n >= 2:
                            wait_emptied(act_e, l, "y", (n - 2) // KC, (n - 2) % KC)
                        nc.scalar.activation(tmp2[:, n % 2, 0:n_tok], bank(l, "g", b, dc)[:, 0:n_tok], ACT.Sigmoid,
                                             bias=bgate[:, b, dc:dc + 1]).then_inc(emptied["act"], 1)
                wait_emptied(act_e, l, "y", 2, KC - 1)
                for t in range(act):
                    if t >= 2:
                        act_e.wait_ge(x_updated[l], t - 1)
                    for j in range(2):
                        wait_full(act_e, l, "out", t, j)
                        square(bank(l, "out", t, j), 12 + 2 * t + j, 512)
                        nc.scalar.activation(rows[:, t % 2, 512 * j:512 * j + 512], bank(l, "out", t, j), ACT.Copy)\
                            .then_inc(emptied["act"], 1)
                    root(12 + 2 * t, 13 + 2 * t)
                act_e.wait_ge(x_updated[l], act)
                for t in range(act):
                    square(xres[:, t, :], t, DM)
                root(0, act)
                modulate(2)
                for t in range(act):
                    wait_full(act_e, l, "rt", t)
                    nc.scalar.activation(score[:, t, :], bank(l, "rt", t)[:, 0:NE], ACT.Sigmoid).then_inc(emptied["act"], 1)

                def silus(n1, i):
                    for f in range(2):
                        act_e.wait_ge(gu_full[l], 4 * i + 2 * n1 + f + 1)
                        nc.scalar.activation(silu[:, 2 * (n1 % 2) + f, 0:n_tok], ps[:, 512 * f:512 * f + n_tok],
                                             ACT.Silu).then_inc(silu_ready[l], 1)

                silus(0, 0)
                with nc.scalar.Fori(0, NE // 2) as i:
                    for n1 in (1, 2):
                        silus(n1, i)
                act_e.wait_ge(dn_taken[l], 2 * act * (NE + 1))
                for t in range(act):
                    square(acc[:, t, :], t, DM)
                root(0, act)
                last_squares = squares[0]

        @block.tensor
        def _(pe):
            opened = [0]

            def group(*key):
                n = G.at[key]
                assert n == opened[0]
                opened[0] += 1
                if n >= BANKS:
                    owner, count = G.emptied_at[n - BANKS]
                    pe.wait_ge(emptied[owner], count)
                return bank(*key)

            def arrived(*key):
                n = item_at[key]
                pe.wait_ge(slot_loaded[n % SLOTS], 16 * (n // SLOTS + 1))
                return slot(*key)

            def chain(dst, pairs):
                for n, (a, b) in enumerate(pairs):
                    ins = nc.tensor.matmul(dst, a, b, start=n == 0, stop=n == len(pairs) - 1)
                return ins

            for l in range(DEPTH):
                act = ACTIVE[l]
                n_tok = P * act
                tile = lambda t: slice(P * t, P * t + P)
                if l == 0:
                    pe.wait_ge(consts_loaded, 48)
                else:
                    pe.wait_ge(dn_taken[l - 1], 2 * ACTIVE[l - 1] * (NE + 1))
                pe.wait_ge(ca_ready[l], 1)
                for r in range(3):
                    dst = group(l, "ada", r)
                    w = [arrived(l, "ada", 4 * r + j) for j in range(4)]
                    for k in range(KC):
                        for j in range(4):
                            ins = nc.tensor.matmul(dst[32 * j:32 * j + 32, :], ca32[:, k, :], w[j][:, k, :],
                                                   start=k == 0, stop=k == KC - 1, skip_group_check=True)
                    ins.then_inc(psum_full, 1)
                for r in range(3):
                    dst = group(l, "adaT", r)
                    wait_emptied(pe, l, "ada", r)
                    for b in range(4):
                        ins = nc.tensor.transpose(dst[:, tile(b)], ada_row[:, r, tile(b)], ident[:, :])
                    ins.then_inc(psum_full, 1)
                for n in (1, 2):
                    for s in range(act // 2):
                        for j in range(2):
                            dst = group(l, "gaterow", n, s, j)
                            src_j = j if n == 1 else 2 + j
                            pick = ident[:, 32 * src_j + s:32 * src_j + s + 1].to_broadcast([P, P])
                            nc.tensor.matmul(dst, pick, ada_row[:, n, :], start=True, stop=True).then_inc(psum_full, 1)

                def transpose_h(n, tiles):
                    for k in range(KC):
                        dst = group(l, "h", n, k)
                        for t in range(tiles):
                            if k == 0:
                                pe.wait_ge(xn_ready[l], (0 if n == 1 else NTILE) + t + 1)
                            ins = nc.tensor.transpose(dst[:, tile(t)], xn[:, t, tile(k)], ident[:, :])
                        ins.then_inc(psum_full, 1)

                transpose_h(1, NTILE)
                wkv, wq = None, None
                for t in range(NTILE):
                    dst = group(l, "kv", t)
                    wkv = arrived(l, "kv")
                    if t == 0:
                        wait_emptied(pe, l, "h", 1, KC - 2)
                        wait_emptied(pe, l, "h", 1, KC - 1)
                    chain(dst[:, 0:KV_END], [(hT[:, k, tile(t)], wkv[:, k, :]) for k in range(KC)]).then_inc(psum_full, 1)
                    if t < act:
                        dst = group(l, "q", t)
                        wq = arrived(l, "q")
                        chain(dst[:, 0:QR], [(hT[:, k, tile(t)], wq[:, k, :]) for k in range(KC)]).then_inc(psum_full, 1)
                for name in "bcuf":
                    for f in range(4):
                        dst = group(l, name, f)
                        w = arrived(l, name)
                        chain(dst[:, 0:n_tok], [(w[:, k, tile(f)], hT[:, k, 0:n_tok]) for k in range(KC)]).then_inc(psum_full, 1)
                pe.wait_ge(lat_ready[l], 1)
                for c in range(2):
                    dst = group(l, "ckvT", c)
                    for t in range(NTILE):
                        ins = nc.tensor.transpose(dst[:, tile(t)], kvlat[:, t, tile(c)], ident[:, :])
                    ins.then_inc(psum_full, 1)
                for c in range(3):
                    dst = group(l, "cqT", c)
                    for t in range(act):
                        ins = nc.tensor.transpose(dst[:, tile(t)], qlat[:, t, tile(c)], ident[:, :])
                    ins.then_inc(psum_full, 1)
                for t in range(NTILE):
                    for j in range(2):
                        dst = group(l, "kvup", t, j)
                        w = arrived(l, "ukv")
                        wait_emptied(pe, l, "ckvT", 1)
                        chain(dst, [(ckvT[:, c, tile(t)], w[:, c, 512 * j:512 * j + 512]) for c in range(2)]).then_inc(psum_full, 1)
                for t in range(act):
                    for j in range(2):
                        dst = group(l, "qup", t, j)
                        w = arrived(l, "uq")
                        wait_emptied(pe, l, "cqT", 2)
                        chain(dst[:, 0:4 * QK], [(cqT[:, c, tile(t)], w[:, c, 4 * QK * j:4 * QK * (j + 1)]) for c in range(3)])\
                            .then_inc(psum_full, 1)
                pe.wait_ge(dft_loaded[l], 16)
                for f in range(FG):
                    wait_emptied(pe, l, "f", f)
                    for s in range(act // 2):
                        dst = group(l, "four1", f, s)
                        for t in range(2):
                            ins = nc.tensor.matmul(dst[:, 256 * t:256 * t + 256], fT[:, f, tile(2 * s + t)], dft_c,
                                                   start=True, stop=True)
                        ins.then_inc(psum_full, 1)
                for f in range(FG):
                    dst = group(l, "four2", f)
                    for s in range(act // 2):
                        n = f * (act // 2) + s
                        wait_emptied(pe, l, "four1", f, s)
                        ab = four_ab[n].rearrange("p (t a c) -> p t a c", t=2, a=2)
                        ins = chain(dst[:, SEQ * s:SEQ * s + SEQ],
                                    [(ab[:, t, a, :], dft_n[:, a, t, :]) for t in range(2) for a in range(2)])
                    ins.then_inc(psum_full, 1)
                wait_emptied(pe, l, "kvup", NTILE - 1, 1)
                pe.wait_ge(kpe_ready[l], 1)
                pe.wait_ge(qrope_ready[l], 1)
                units = attention_units(l)
                for u in range(len(units) + 1):
                    if u < len(units):
                        h, s = units[u]
                        if s == 0:
                            dst = group(l, "kT", h)
                            for t in range(NTILE):
                                ins = nc.tensor.transpose(dst[0:QK, tile(t)], ktok[:, t, h, :], ident[:, :])
                            ins.then_inc(psum_full, 1)
                            dst = group(l, "qT", h)
                            for t in range(act):
                                ins = nc.tensor.transpose(dst[0:QK, tile(t)], qtok[:, t, h, :], ident[:, :])
                            ins.then_inc(psum_full, 1)
                            wait_emptied(pe, l, "kT", h)
                            wait_emptied(pe, l, "qT", h)
                        k0 = 0 if s == 0 else SEQ
                        for t in range(2):
                            dst = group(l, "S", h, s, t)
                            nc.tensor.matmul(dst[:, 0:512 - k0], headT[0:QK, h % 2, 0, tile(2 * s + t)],
                                             headT[0:QK, h % 2, 1, k0:512], start=True, stop=True).then_inc(psum_full, 1)
                    if u >= 1:
                        h, s = units[u - 1]
                        nk = 4 if s == 0 else 2
                        for t in range(2):
                            dst = group(l, "PT", h, s, t)
                            pe.wait_ge(prob_ready[l], 2 * (u - 1) + t + 1)
                            for k in range(nk):
                                ins = nc.tensor.transpose(dst[:, tile(k)], probs[:, (u - 1) % 2, t, tile(k)], ident[:, :])
                            ins.then_inc(psum_full, 1)
                        dst = group(l, "O", h, s)
                        for t in range(2):
                            wait_emptied(pe, l, "PT", h, s, t)
                        half = slice(VD * (h % 2), VD * (h % 2) + VD)
                        chain(dst[half, 0:SEQ], [(vtok[:, (NTILE - nk) + k, h, :], probsT[:, (u - 1) % 2, k, :]) for k in range(nk)])\
                            .then_inc(psum_full, 1)
                wait_emptied(pe, l, "O", *units[-1])
                branch = [oT, bT, fT]
                for b in range(3):
                    for dc in range(KC):
                        if b == 1 and dc == 0:
                            pe.wait_ge(conv_ready[l], 4)
                        if b == 2 and dc == 0:
                            wait_emptied(pe, l, "four2", FG - 1)
                        dst = group(l, "g", b, dc)
                        wo = arrived(l, "branch", b)
                        w = arrived(l, "gate", b, dc // 4)
                        chain(dst[:, 0:n_tok], [(w[:, k, tile(dc % 4)], hT[:, k, 0:n_tok]) for k in range(KC)]).then_inc(psum_full, 1)
                        dst = group(l, "y", b, dc)
                        chain(dst[:, 0:n_tok], [(wo[:, c, tile(dc)], branch[b][:, c, 0:n_tok]) for c in range(4)])\
                            .then_inc(psum_full, 1)
                pe.wait_ge(merged[l], 2 * KC)
                wo2 = [arrived(l, "out", j) for j in range(2)]
                for t in range(act):
                    for j in range(2):
                        dst = group(l, "out", t, j)
                        chain(dst, [(mT[:, k, tile(t)], wo2[j][:, k, :]) for k in range(KC)]).then_inc(psum_full, 1)
                transpose_h(2, act)
                wait_emptied(pe, l, "h", 2, KC - 2)
                wait_emptied(pe, l, "h", 2, KC - 1)
                for t in range(act):
                    dst = group(l, "rt", t)
                    chain(dst[:, 0:NE], [(hT[:, k, tile(t)], wr[:, k, :]) for k in range(KC)]).then_inc(psum_full, 1)
                wait_emptied(pe, l, "rt", act - 1)
                downs = 2 * act

                def expert(n1, i):
                    j = n1 % 2
                    uses = (NE // 2 + (1 - j)) * l + (1 if n1 != 0 else 0) + (1 if n1 == 2 else 0)
                    if n1 == 0:
                        uses += 1
                    pe.wait_ge(gu_loaded[j], 32 * i + 32 * uses)
                    if n1:
                        pe.wait_ge(act_ready[l], 4 * i + 2 * n1)
                    for f in range(2):
                        for a in range(2):
                            b = f + 2 * a
                            ins = chain(ps[:, 512 * b:512 * b + n_tok],
                                        [(gu[j][:, k, FE * a + P * f:FE * a + P * f + P], hT[:, k, 0:n_tok]) for k in range(KC)])
                        ins.then_inc(gu_full[l], 1)
                    pe.wait_ge(dn_loaded[j], 16 * i + 16 * uses)
                    pe.wait_ge(act_ready[l], 4 * i + 2 * n1 + 2)
                    for g in range(downs):
                        t, hf = g // 2, g % 2
                        b = 4 + g % 4
                        if n1 or g >= 4:
                            pe.wait_ge(dn_taken[l], 2 * downs * i + downs * n1 + g - 3)
                        chain(ps[:, 512 * b:512 * b + 512],
                              [(actT[:, 2 * j + f, tile(t)], dn[j][:, f, 512 * hf:512 * hf + 512]) for f in range(2)])\
                            .then_inc(dn_full[l], 1)

                expert(0, 0)
                with nc.tensor.Fori(0, NE // 2) as i:
                    for n1 in (1, 2):
                        expert(n1, i)

        @block.vector
        def _(dve):
            steps = [0]

            def link(ins):
                steps[0] += 1
                ins.then_inc(dve_step, 1)
                dve.wait_ge(dve_step, steps[0])

            V = nc.vector
            dve.wait_ge(consts_loaded, 48)
            for l in range(DEPTH):
                act = ACTIVE[l]
                n_tok = P * act
                counts = {"ssq": 0, "root": 0}

                def mean_square(count, pieces):
                    counts["ssq"] += count
                    dve.wait_ge(ssq_ready[l], counts["ssq"])
                    for c0, c1, width in pieces:
                        ins = V.tensor_scalar(ssq[:, c0:c1], ssq[:, c0:c1], 1.0 / width, EPS, ALU.mult, ALU.add)
                    ins.then_inc(ms_ready[l], 1)

                def inverse_root(c0, c1):
                    counts["root"] += 1
                    dve.wait_ge(root_ready[l], counts["root"])
                    link(V.reciprocal(rstd[:, c0:c1], rstd[:, c0:c1]))

                mean_square(NTILE, [(0, 4, DM)])
                inverse_root(0, 4)
                for t in range(NTILE):
                    V.tensor_scalar(xn[:, t, :], xres[:, t, :], rstd[:, t:t + 1], None, ALU.mult).then_inc(xn_ready[l], 1)
                dve.wait_ge(adab_loaded[l], 16 * 8)
                dve.wait_ge(params_loaded[l], 16 * 14)
                for r in range(3):
                    wait_full(dve, l, "ada", r)
                    V.tensor_tensor(ada_row[:, r, :], bank(l, "ada", r), ada_bias[:, r, :], ALU.add).then_inc(emptied["dve"], 1)
                wait_emptied(dve, l, "adaT", 2)
                halves = {0: (0, 0), 1: (0, 2), 3: (1, 2), 4: (2, 0)}
                for n, (shift, scale) in enumerate(((0, 1), (3, 4))):
                    for s in range(2):
                        (r, j) = halves[scale]
                        V.scalar_tensor_tensor(scaleT[:, n, s, :].rearrange("p (j b) -> p j b", j=2),
                                               adaT[:, r, :, j:j + 2, s].rearrange("p b j -> p j b"), 1.0,
                                               gains[:, n, :].rearrange("p (j b) -> p j b", j=2), ALU.add, ALU.mult)
                        (r, j) = halves[shift]
                        ins = V.tensor_copy(shiftT[:, n, s, :].rearrange("p (j b) -> p j b", j=2),
                                            adaT[:, r, :, j:j + 2, s].rearrange("p b j -> p j b"))
                ins.then_inc(coef_ready[l], 1)
                for n in (1, 2):
                    for s in range(act // 2):
                        for j in range(2):
                            wait_full(dve, l, "gaterow", n, s, j)
                            V.tensor_tensor(Grow[:, n - 1, s, 512 * j:512 * j + 512], bank(l, "gaterow", n, s, j),
                                            gpost[:, n - 1, 512 * j:512 * j + 512], ALU.mult).then_inc(emptied["dve"], 1)

                def modulate(n):
                    dve.wait_ge(coef_ready[l], 1)
                    for k in range(0, KC, 2):
                        wait_full(dve, l, "h", n, k)
                        for s in range(2 if n == 1 else act // 2):
                            ins = V.tensor_scalar(hT[:, k, SEQ * s:SEQ * s + SEQ], bank(l, "h", n, k)[:, SEQ * s:SEQ * s + SEQ],
                                                  scaleT[:, n - 1, s, k:k + 1], shiftT[:, n - 1, s, k:k + 1], ALU.mult, ALU.add)
                        ins.then_inc(emptied["dve"], 1)

                modulate(1)
                mean_square(NTILE + act, [(4, 8, KVR), (8, 8 + act, QR)])
                inverse_root(4, 8 + act)
                wait_emptied(dve, l, "kv", NTILE - 1)
                wait_emptied(dve, l, "q", act - 1)
                for t in range(NTILE):
                    V.tensor_scalar(kvlat[:, t, 0:KVR], kvlat[:, t, 0:KVR], rstd[:, 4 + t:5 + t], None, ALU.mult)
                for t in range(act):
                    ins = V.tensor_scalar(qlat[:, t, :], qlat[:, t, :], rstd[:, 8 + t:9 + t], None, ALU.mult)
                ins.then_inc(lat_ready[l], 1)
                cos, sin = rope_t[:, :, 0, :], rope_t[:, :, 1, :]
                x1, x2 = kvlat[:, 0:2, KVR:KVR + 16], kvlat[:, 0:2, KVR + 16:KV_END]
                t1, t2, t3, t4 = rt1[:, :, 0, :], rt1[:, :, 1, :], rt1[:, :, 2, :], rt1[:, :, 3, :]
                V.tensor_tensor(t1, x1, cos, ALU.mult)
                V.tensor_tensor(t2, x2, sin, ALU.mult)
                V.tensor_tensor(t3, x2, cos, ALU.mult)
                V.tensor_copy(ropek[:, 2:4, :], kvlat[:, 2:4, KVR:KV_END])
                link(V.tensor_tensor(t4, x1, sin, ALU.mult))
                V.tensor_tensor(ropek[:, 0:2, 0:16], t1, t2, ALU.subtract)
                link(V.tensor_tensor(ropek[:, 0:2, 16:32], t3, t4, ALU.add))
                wait_full(dve, l, "kv", 0)
                for t in range(NTILE):
                    ins = V.tensor_copy(ktok[:, t, :, NOPE:QK], ropek[:, t:t + 1, :].to_broadcast([P, H, ROPE]))
                ins.then_inc(kpe_ready[l], 1)
                for f in range(4):
                    wait_full(dve, l, "u", f)
                    wait_emptied(dve, l, "c", f)
                    V.tensor_tensor(cT[:, f, 0:n_tok], bank(l, "u", f)[:, 0:n_tok], cT[:, f, 0:n_tok], ALU.mult)\
                        .then_inc(emptied["dve"], 1)
                    wait_emptied(dve, l, "u", f)
                    inner = cT[:, f, 0:n_tok].rearrange("p (s n) -> p s n", n=SEQ)
                    y = tmp2[:, f % 2, 0:n_tok].rearrange("p (s n) -> p s n", n=SEQ)
                    link(V.tensor_scalar(y, inner, convw[:, 1, f:f + 1], None, ALU.mult))
                    link(V.scalar_tensor_tensor(y[:, :, 1:SEQ], inner[:, :, 0:SEQ - 1], convw[:, 0, f:f + 1],
                                                y[:, :, 1:SEQ], ALU.mult, ALU.add))
                    link(V.scalar_tensor_tensor(y[:, :, 0:SEQ - 1], inner[:, :, 1:SEQ], convw[:, 2, f:f + 1],
                                                y[:, :, 0:SEQ - 1], ALU.mult, ALU.add))
                    wait_emptied(dve, l, "b", f)
                    V.tensor_tensor(bT[:, f, 0:n_tok], bT[:, f, 0:n_tok], tmp2[:, f % 2, 0:n_tok], ALU.mult).then_inc(conv_ready[l], 1)
                for c in range(2):
                    wait_full(dve, l, "ckvT", c)
                    V.tensor_scalar(ckvT[:, c, :], bank(l, "ckvT", c), gqk[:, c:c + 1], None, ALU.mult).then_inc(emptied["dve"], 1)
                for t in range(act):
                    for j in range(2):
                        wait_full(dve, l, "qup", t, j)
                        V.tensor_copy(qtok[:, t, 4 * j:4 * j + 4, :], bank(l, "qup", t, j)[:, 0:4 * QK].rearrange("p (h d) -> p h d", h=4))\
                            .then_inc(emptied["dve"], 1)
                wait_emptied(dve, l, "qup", act - 1, 1)
                for t in range(2):
                    q1, q2 = qtok[:, t, :, NOPE:NOPE + 16], qtok[:, t, :, NOPE + 16:QK]
                    c_ = rope_t[:, t, 0:1, :].to_broadcast([P, H, 16])
                    s_ = rope_t[:, t, 1:2, :].to_broadcast([P, H, 16])
                    a1, a2 = rt1[:, 0], rt1[:, 1]
                    b1, b2 = rt2[:, 0], rt2[:, 1]
                    V.tensor_tensor(a1, q1, c_, ALU.mult)
                    V.tensor_tensor(a2, q2, s_, ALU.mult)
                    V.tensor_tensor(b1, q2, c_, ALU.mult)
                    link(V.tensor_tensor(b2, q1, s_, ALU.mult))
                    V.tensor_tensor(q1, a1, a2, ALU.subtract)
                    ins = V.tensor_tensor(q2, b1, b2, ALU.add)
                    if t == 0:
                        link(ins)
                ins.then_inc(qrope_ready[l], 1)
                for f in range(FG):
                    wait_full(dve, l, "four2", f)
                    V.tensor_copy(fT[:, f, 0:n_tok], bank(l, "four2", f)[:, 0:n_tok]).then_inc(emptied["dve"], 1)
                units = attention_units(l)
                for u in range(len(units) + 1):
                    if u < len(units):
                        h, s = units[u]
                        keys = 512 if s == 0 else 256
                        if s == 0:
                            wait_full(dve, l, "kT", h)
                            V.tensor_copy(headT[0:QK, h % 2, 1, :], bank(l, "kT", h)[0:QK, :]).then_inc(emptied["dve"], 1)
                        for t in range(2):
                            c = 2 * (u % 2) + t
                            wait_full(dve, l, "S", h, s, t)
                            link(V.reduce_max(smax[:, c:c + 1], bank(l, "S", h, s, t)[:, 0:keys], AX))
                            V.tensor_scalar(nmax[:, c:c + 1], smax[:, c:c + 1], -ATT_SCALE, None, ALU.mult).then_inc(max_ready[l], 1)
                    if u >= 1:
                        h, s = units[u - 1]
                        nk = 4 if s == 0 else 2
                        wait_full(dve, l, "PT", h, s, 0)
                        V.tensor_copy(probsT[:, (u - 1) % 2, 0:nk, 0:P],
                                      bank(l, "PT", h, s, 0)[:, 0:P * nk].rearrange("p (k q) -> p k q", q=P)).then_inc(emptied["dve"], 1)
                        wait_full(dve, l, "O", h, s)
                        half = slice(VD * (h % 2), VD * (h % 2) + VD)
                        V.tensor_copy(oT[half, h // 2, SEQ * s:SEQ * s + SEQ], bank(l, "O", h, s)[half, 0:SEQ]).then_inc(emptied["dve"], 1)
                    if u < len(units):
                        h, s = units[u]
                        keys = 512 if s == 0 else 256
                        for t in range(2):
                            c = 2 * (u % 2) + t
                            wait_emptied(dve, l, "S", h, s, t)
                            link(V.reciprocal(sinv[:, c:c + 1], ssum[:, c:c + 1]))
                            V.tensor_scalar(probs[:, u % 2, t, 0:keys], probs[:, u % 2, t, 0:keys], sinv[:, c:c + 1], None,
                                            ALU.mult).then_inc(prob_ready[l], 1)
                for b in range(3):
                    for dc in range(KC):
                        n = b * KC + dc
                        wait_full(dve, l, "y", b, dc)
                        wait_emptied(dve, l, "g", b, dc)
                        if b == 0:
                            dst = mT[:, dc, 0:n_tok]
                        else:
                            m = n - KC
                            if m >= 2:
                                dve.wait_ge(merged[l], m - 1)
                            dst = ytmp[:, m % 2, 0:n_tok]
                        V.tensor_tensor(dst, bank(l, "y", b, dc)[:, 0:n_tok], tmp2[:, n % 2, 0:n_tok], ALU.mult)\
                            .then_inc(emptied["dve"], 1)
                for t in range(act):
                    c = 12 + 2 * t
                    dve.wait_ge(ssq_ready[l], counts["ssq"] + 2)
                    link(V.tensor_tensor(ssq[:, c:c + 1], ssq[:, c:c + 1], ssq[:, c + 1:c + 2], ALU.add))
                    mean_square(2, [(c, c + 1, DM)])
                    inverse_root(c, c + 1)
                    wait_emptied(dve, l, "out", t, 1)
                    link(V.scalar_tensor_tensor(rows[:, t % 2, :], rows[:, t % 2, :], rstd[:, c:c + 1], Grow[:, 0, t // 2, :],
                                                ALU.mult, ALU.mult))
                    V.tensor_tensor(xres[:, t, :], xres[:, t, :], rows[:, t % 2, :], ALU.add).then_inc(x_updated[l], 1)
                mean_square(act, [(0, act, DM)])
                inverse_root(0, act)
                for t in range(act):
                    V.tensor_scalar(xn[:, t, :], xres[:, t, :], rstd[:, t:t + 1], None, ALU.mult).then_inc(xn_ready[l], 1)
                modulate(2)
                wait_emptied(dve, l, "rt", act - 1)
                sc, bi, cb, oh = score[:, 0:act], biased[:, 0:act], comb[:, 0:act], onehot[:, 0:act]
                link(V.tensor_tensor(bi, sc, brow.rearrange("p (a e) -> p a e", a=1).to_broadcast([P, act, NE]), ALU.add))
                for t in range(act):
                    link(V.max(m8[:, t, :], biased[:, t, :]))
                    link(V.max_index(idx8[:, t, :], m8[:, t, :], biased[:, t, :]))
                link(V.tensor_copy(idxf[:, 0:act, :], idx8[:, 0:act, :]))
                for t in range(act):
                    ins = V.tensor_tensor(oh[:, t], iota.rearrange("p (a e) -> p a e", a=1).to_broadcast([P, TOPK, NE]),
                                          idxf[:, t, 0:TOPK].rearrange("p (k a) -> p k a", a=1).to_broadcast([P, TOPK, NE]),
                                          ALU.is_equal)
                link(ins)
                link(V.tensor_reduce(cb, oh.rearrange("p t k e -> p t e k"), AX, ALU.add))
                link(V.tensor_tensor(cb, cb, sc, ALU.mult))
                link(V.tensor_reduce(rden[:, 0:act], cb, AX, ALU.add))
                link(V.reciprocal(rden[:, 0:act], rden[:, 0:act]))
                for t in range(act):
                    ins = V.tensor_scalar(cb[:, t, :], cb[:, t, :], rden[:, t:t + 1], ROUTED_SCALE, ALU.mult, ALU.mult)
                link(ins)
                downs = 2 * act

                def expert(n1, i, shared=False):
                    for f in range(2):
                        dve.wait_ge(silu_ready[l], 4 * i + 2 * n1 + f + 1)
                        b = 2 + f
                        V.tensor_tensor(actT[:, 2 * (n1 % 2) + f, 0:n_tok], ps[:, 512 * b:512 * b + n_tok],
                                        silu[:, 2 * (n1 % 2) + f, 0:n_tok], ALU.mult).then_inc(act_ready[l], 1)
                    for g in range(downs):
                        t, hf = g // 2, g % 2
                        b = 4 + g % 4
                        dve.wait_ge(dn_full[l], 2 * downs * i + downs * n1 + g + 1)
                        dst = acc[:, t, 512 * hf:512 * hf + 512]
                        if shared:
                            V.tensor_copy(dst, ps[:, 512 * b:512 * b + 512]).then_inc(dn_taken[l], 1)
                        else:
                            dve.wait_ge(dn_taken[l], 2 * downs * i + downs * (n1 - 1) + g + 1)
                            V.scalar_tensor_tensor(dst, ps[:, 512 * b:512 * b + 512], comb[:, t, bass.ds(2 * i + (n1 - 1), 1)],
                                                   dst, ALU.mult, ALU.add).then_inc(dn_taken[l], 1)

                expert(0, 0, shared=True)
                with nc.vector.Fori(0, NE // 2) as i:
                    for n1 in (1, 2):
                        expert(n1, i)
                dve.wait_ge(dn_taken[l], downs * (NE + 1))
                mean_square(act, [(0, act, DM)])
                inverse_root(0, act)
                for t in range(act):
                    link(V.scalar_tensor_tensor(acc[:, t, :], acc[:, t, :], rstd[:, t:t + 1], Grow[:, 1, t // 2, :],
                                                ALU.mult, ALU.mult))
                    V.tensor_tensor(xres[:, t, :], xres[:, t, :], acc[:, t, :], ALU.add).then_inc(x_updated[l], 1)


_INS = ["x", "c", "ctx", "c_ctx", "w_ada", "b_ada", "g_pre_mix", "g_post_mix", "g_pre_ffn", "g_post_ffn", "w_in",
        "b_gate", "g_q", "w_uq", "g_kv", "w_ukv", "w_mla_out", "conv_w", "w_conv_out", "w_four_out", "w_out",
        "w_router", "b_router", "w_gate_e", "w_up_e", "w_down_e", "w_gate_s", "w_up_s", "w_down_s"]


def shape_tables():
    pos = np.arange(SEQ)
    pairs = ROPE // 4
    inv = (ROPE_BASE ** (-np.arange(pairs, dtype=np.float32) / pairs)).astype(np.float32)
    ang = np.concatenate([(pos // GRID_W)[:, None].astype(np.float32) * inv,
                          (pos % GRID_W)[:, None].astype(np.float32) * inv], axis=1).astype(np.float64)
    rope = np.stack([np.cos(ang), np.sin(ang)], axis=1).reshape(2, P, 2, ROPE // 2).transpose(1, 0, 2, 3)
    a = 2 * np.pi * (np.outer(np.arange(FC), np.arange(FC)) % FC) / FC
    chan = np.concatenate([np.cos(a), np.sin(a)], axis=1) / np.sqrt(FC)
    b = 2 * np.pi * (np.outer(pos, pos) % SEQ) / SEQ
    seq = (np.stack([np.cos(b), -np.sin(b)]) / np.sqrt(SEQ)).reshape(2, 2, P, SEQ).transpose(2, 0, 1, 3).reshape(P, 1024)
    return {"ident": np.eye(P, dtype=np.float32),
            "iota": np.tile(np.arange(NE, dtype=np.float32), (P, 1)),
            "rope": np.ascontiguousarray(rope, dtype=np.float32),
            "dft": np.ascontiguousarray(np.concatenate([chan, seq], axis=1), dtype=np.float32)}


def kernel(**inputs):
    import concourse.bacc as _bacc
    from concourse.bass_utils import run_bass_kernel_spmd as _run

    nc = _bacc.Bacc("TRN2", target_bir_lowering=False, num_devices=1)
    arrays, I, C = {}, {}, {}
    for group, into in (({n: inputs[n] for n in _INS}, I), (shape_tables(), C)):
        for name, a in group.items():
            a = np.ascontiguousarray(a)
            arrays[f"in_{name}"] = a
            into[name] = nc.dram_tensor(f"in_{name}", a.shape, mybir.dt.from_np(a.dtype), kind="ExternalInput").ap()
    out = nc.dram_tensor("out_0", (1, SEQ, DM), mybir.dt.float32, kind="ExternalOutput").ap()
    hybrid_layers(nc, I, C, out)
    r = _run(nc, [arrays], core_ids=[0])
    return r.results[0]["out_0"]
```

```python
import numpy as np
import concourse.bass as bass
from concourse import mybir
from concourse.alu_op_type import AluOpType as ALU
from contextlib import ExitStack

DM, DEPTH, GRID_W = 1024, 2, 64
H, NOPE, ROPE, VD = 8, 64, 32, 64
QK = NOPE + ROPE
QR, KVR = 384, 256
CONV = 512
FG, FC = 4, 128
NE, TOPK, FE = 32, 4, 256
ROUTED_SCALE, EPS = 2.5, 1e-6
ROPE_BASE = 10000.0
P = 128
KC = DM // P
NTILE = 4
SEQ = 256
KV_END = KVR + ROPE
Q_END = KV_END + QR
FOUR_END = Q_END + 3 * CONV + FG * FC
SLOTS = 4
BANKS = 8
ATT_SCALE = QK ** -0.5
ACTIVE = [NTILE, 2]
CAP = [P, P // 2]
ROUNDS = 4
MAX_ITEMS = 48
UNROLL = 4
BLOCKS = NE // UNROLL
ABSENT = 65535


class Groups:

    def __init__(self):
        self.at, self.count, self.emptied_at = {}, {"act": 0, "dve": 0}, []

    def add(self, owner, *key):
        self.at[key] = len(self.emptied_at)
        self.count[owner] += 1
        self.emptied_at.append((owner, self.count[owner]))


def attention_units(l):
    return [(h, s) for h in range(H) for s in range(ACTIVE[l] // 2)]


def plan():
    g = Groups()
    alternate = lambda k: "act" if k % 2 else "dve"
    for l in range(DEPTH):
        act = ACTIVE[l]
        for r in range(3):
            g.add("dve", l, "ada", r)
        g.add("act", l, "adaT")
        g.add("act", l, "adaP")
        for n in (1, 2):
            for s in range(act // 2):
                for j in range(2):
                    g.add("dve", l, "gaterow", n, s, j)
        for k in range(KC):
            g.add(alternate(k), l, "h", 1, k)
        for t in range(NTILE):
            g.add("act", l, "kv", t)
            if t < act:
                g.add("act", l, "q", t)
        for name, owner in (("b", "act"), ("c", "act"), ("u", "dve"), ("f", "act")):
            for f in range(4):
                g.add(owner, l, name, f)
        for c in range(2):
            g.add("dve", l, "ckvT", c)
        for c in range(3):
            g.add("act", l, "cqT", c)
        for t in range(NTILE):
            for j in range(2):
                g.add("act", l, "kvup", t, j)
        for t in range(act):
            for j in range(2):
                g.add("dve", l, "qup", t, j)
        for f in range(FG):
            for s in range(act // 2):
                g.add("act", l, "four1", f, s)
        for f in range(FG):
            g.add("dve", l, "four2", f)
        units = attention_units(l)
        for u in range(len(units) + 1):
            if u < len(units):
                h, s = units[u]
                if s == 0:
                    g.add("dve", l, "kT", h)
                    g.add("act", l, "qT", h)
                for t in range(2):
                    g.add("act", l, "S", h, s, t)
            if u >= 1:
                h, s = units[u - 1]
                for t in range(2):
                    g.add(alternate(t), l, "PT", h, s, t)
                g.add("dve", l, "O", h, s)
        for b in range(3):
            for dc in range(KC):
                g.add("act", l, "g", b, dc)
                g.add("dve", l, "y", b, dc)
        for t in range(act):
            for j in range(2):
                g.add("act", l, "out", t, j)
        for k in range(KC):
            g.add(alternate(k), l, "h", 2, k)
        for t in range(act):
            g.add("act", l, "rt", t)
        for t in range(act):
            for j in range(2):
                g.add("act", l, "hrow", t, j)
        for name in ("rank", "turn", "items"):
            g.add("dve", l, name)
    return g


def hybrid_layers(nc, I, C, out):
    f32, u32 = mybir.dt.float32, mybir.dt.uint32
    ACT, AX = mybir.ActivationFunctionType, mybir.AxisListType.X
    G = plan()
    ctx = ExitStack()

    def sb(name, shape, dt=f32):
        return ctx.enter_context(nc.sbuf_tensor(name, shape, dt))

    def one(name):
        return ctx.enter_context(nc.semaphore(name))

    def by_layer(name):
        return [one(f"{name}_{l}") for l in range(DEPTH)]

    with ctx:
        xres = sb("xres", [P, NTILE, DM])
        hT = sb("hT", [P, KC, NTILE * P])
        ring = sb("ring", [P, SLOTS, 4096])
        bT = sb("bT", [P, 4, 512])
        cT = sb("cT", [P, 4, 512])
        fT = sb("fT", [P, 4, 512])
        tmp2 = sb("tmp2", [P, 2, 512])
        qkv = sb("qkv", [P, 8192])
        head = sb("head", [P, 2048])
        probs_b = sb("probs_b", [P, 2048])
        probsT_b = sb("probsT_b", [P, 2048])
        oT_b = sb("oT_b", [P, 2048])
        Grow = sb("Grow", [P, 2, 2, DM])
        ident = sb("ident", [P, P])
        rope_t = sb("rope_t", [P, 2, 2, 16])
        wr = sb("wr", [P, KC, NE])
        small = sb("small", [P, 480])
        used = [0]

        def part(n):
            used[0] += n
            assert used[0] <= 480
            return small[:, used[0] - n:used[0]]

        cs = part(16).rearrange("p (s k) -> p s k", s=2)
        gains = part(16).rearrange("p (n k) -> p n k", k=KC)
        scaleT = part(32).rearrange("p (n s k) -> p n s k", n=2, s=2)
        shiftT = part(32).rearrange("p (n s k) -> p n s k", n=2, s=2)
        gqk = part(5)
        convw = part(12).rearrange("p (j f) -> p j f", j=3)
        bgate = part(24).rearrange("p (b k) -> p b k", b=3)
        ssq = part(24)
        rstd = part(24)
        brow = part(NE)
        iota = part(MAX_ITEMS)
        smax, nmax, ssum, sinv = part(4), part(4), part(4), part(4)
        rden = part(4)
        m8 = part(32).rearrange("p (t k) -> p t k", k=8)
        idx8 = part(32).bitcast(u32).rearrange("p (t k) -> p t k", k=8)
        idxf = part(32).rearrange("p (t k) -> p t k", k=8)
        pick_w = part(16).rearrange("p (t k) -> p t k", k=TOPK)
        pos = part(16).rearrange("p (t k) -> p t k", k=TOPK)
        posu = part(16).bitcast(u32).rearrange("p (t k) -> p t k", k=TOPK)
        pick_id = part(16).bitcast(u32).rearrange("p (t k) -> p t k", k=TOPK)
        item_t = part(8)
        needed, over = part(1), part(4)
        half_id = part(1)
        held = part(1)
        more_f, more_u = part(1), part(1).bitcast(u32)
        now_g, now_y = part(4).bitcast(u32), part(4).bitcast(u32)

        ada_bias = probs_b[:, 0:1536].rearrange("p (r c) -> p r c", r=3)
        ada_row = probsT_b[:, 0:1536].rearrange("p (r c) -> p r c", r=3)
        gpost = oT_b[:, :].rearrange("p (n d) -> p n d", n=2)
        ca32 = head[:, 0:256].rearrange("p (k c) -> p k c", c=32)
        adaT = head[:, 256:288].rearrange("p (b j s) -> p b j s", b=4, j=4)
        adaP = head[:, 288:320].rearrange("p (n k s) -> p n k s", n=2, k=KC)
        dft_c = head[:, 0:256]
        dft_n = head[:, 256:1280].rearrange("p (a c n) -> p a c n", a=2, c=2)
        ropek = head[:, 1280:1408].rearrange("p (t d) -> p t d", t=NTILE)
        rt1 = head[:, 1408:1664].rearrange("p (t h d) -> p t h d", t=2, h=H)
        rt2 = head[:, 1664:1920].rearrange("p (t h d) -> p t h d", t=2, h=H)
        kvlat = probs_b[:, 0:4 * KV_END].rearrange("p (t c) -> p t c", t=4)
        qlat = probsT_b[:, 0:4 * QR].rearrange("p (t c) -> p t c", t=4)
        ckvT = qkv[:, 0:1024].rearrange("p (c t) -> p c t", c=2)
        cqT = oT_b[:, 0:1536].rearrange("p (c t) -> p c t", c=3)
        four_ab = [b[:, 512 * i:512 * i + 512] for b in (probs_b, probsT_b) for i in range(4)]
        qtok = qkv[:, 0:3072].rearrange("p (t h d) -> p t h d", t=4, h=H)
        ktok = qkv[:, 3072:6144].rearrange("p (t h d) -> p t h d", t=4, h=H)
        vtok = qkv[:, 6144:8192].rearrange("p (t h d) -> p t h d", t=4, h=H)
        headT = head[:, :].rearrange("p (b a t) -> p b a t", b=2, a=2)
        probs = probs_b[:, :].rearrange("p (b t k) -> p b t k", b=2, t=2)
        probsT = probsT_b[:, :].rearrange("p (b k t) -> p b k t", b=2, k=4)
        oT = oT_b[:, :].rearrange("p (c t) -> p c t", c=4)
        xn = qkv[:, 4096:8192].rearrange("p (t d) -> p t d", t=NTILE)
        mT = qkv[:, 0:4096].rearrange("p (k t) -> p k t", k=KC)
        ytmp = head[:, 0:1024].rearrange("p (b t) -> p b t", b=2)
        rows = oT_b[:, :].rearrange("p (n d) -> p n d", n=2)
        junk = tmp2[:, :, :].rearrange("p a b -> p (a b)")
        route = bT[:, 2:4, :].rearrange("p a b -> p (a b)")
        cols = lambda a, b: route[:, a:b].rearrange("p (t e) -> p t e", e=NE)
        score, biased, mask = cols(0, 128), cols(128, 256), cols(256, 384)
        onehot = route[:, 384:896].rearrange("p (t k e) -> p t k e", t=NTILE, k=TOPK)
        tri = qkv[:, 0:256]
        oh_tmp = tmp2[:, 0, :].rearrange("p (t k e) -> p t k e", t=NTILE, k=TOPK)
        turn = qkv[:, 384:384 + MAX_ITEMS]
        place = qkv[:, 256:384].rearrange("p (t e) -> p t e", e=NE)
        silu_s, act_s = tmp2, bT[:, 0:2, :]
        dn_s = head[:, :].rearrange("p (k n) -> p k n", k=2)
        acc = qkv[:, 0:4096].rearrange("p (t d) -> p t d", t=NTILE)
        hrow = [(probs_b if t < 2 else probsT_b)[:, DM * (t % 2):DM * (t % 2) + DM] for t in range(NTILE)]
        tab = wr[:, :, :].rearrange("p k e -> p (k e)").bitcast(u32)
        row_y, row_g = tab[:, 0:P + 1], head[:, 1536:1537 + P].bitcast(u32)
        item_col, item_expert = tab[0:1, 136:136 + MAX_ITEMS], tab[0:1, 184:184 + MAX_ITEMS]
        wide = [DM, DM // 2]
        xg = [(probs_b if u < 2 else probsT_b)[:, DM * (u % 2):DM * (u % 2) + DM] for u in range(4)]
        xT = [oT_b[:, DM * j:DM * j + DM] for j in range(2)]
        silu_e = [head[:, 256 * j:256 * j + 256] for j in range(2)]
        a_e = [head[:, 512 + 256 * j:768 + 256 * j] for j in range(2)]
        aT_e = [head[:, 1024 + 256 * j:1280 + 256 * j] for j in range(2)]
        y_e = [bT[:, 2 * j:2 * j + 2, :].rearrange("p a b -> p (a b)") for j in range(2)]
        gu = [ring[:, u, :].rearrange("p (k n) -> p k n", k=KC) for u in range(UNROLL)]
        dn = [w.rearrange("p (k n) -> p k n", k=2) for w in
              (cT[:, :, :].rearrange("p a b -> p (a b)"), fT[:, :, :].rearrange("p a b -> p (a b)"),
               qkv[:, 4096:6144], qkv[:, 6144:8192])]
        picked = [hT[:, :, :].rearrange("p a b -> p (a b)"), qkv[:, 4096:8192]]
        scratch = lambda name, shape, dt: [nc.dram_tensor(f"{name}_{l}", shape(l), dt, kind="Internal").ap()
                                           for l in range(DEPTH)]
        h_rows = scratch("h_rows", lambda l: (P * ACTIVE[l], DM), f32)
        slots_d = scratch("slot_table", lambda l: (P * ACTIVE[l] * NE, 1), u32)
        y_rows = scratch("y_rows", lambda l: (P * ACTIVE[l] * TOPK, DM), f32)
        ps = ctx.enter_context(nc.psum_tensor("ps", [P, BANKS * 512], f32))

        psum_full = one("psum_full")
        emptied = {"act": one("emptied_by_act"), "dve": one("emptied_by_dve")}
        x_loaded, consts_loaded, out_stored = one("x_loaded"), one("consts_loaded"), one("out_stored")
        slot_loaded = [one(f"slot_loaded_{i}") for i in range(SLOTS)]
        by_buffer = lambda name: [[one(f"{name}_{l}_{u}") for u in range(UNROLL)] for l in range(DEPTH)]
        gu_loaded, dn_loaded = by_buffer("gu_loaded"), by_buffer("dn_loaded")
        x_gathered, y_stored = by_buffer("x_gathered"), by_buffer("y_stored")
        params_loaded = by_layer("params_loaded")
        adab_zero = by_layer("adab_zero")
        adab_loaded = by_layer("adab_loaded")
        dft_loaded = by_layer("dft_loaded")
        ca_ready = by_layer("ca_ready")
        ssq_ready = by_layer("ssq_ready")
        ms_ready = by_layer("ms_ready")
        root_ready = by_layer("root_ready")
        xn_ready = by_layer("xn_ready")
        coef_ready = by_layer("coef_ready")
        lat_ready = by_layer("lat_ready")
        conv_ready = by_layer("conv_ready")
        kpe_ready = by_layer("kpe_ready")
        qrope_ready = by_layer("qrope_ready")
        max_ready = by_layer("max_ready")
        prob_ready = by_layer("prob_ready")
        merged = by_layer("merged")
        x_updated = by_layer("x_updated")
        mask_ready = by_layer("mask_ready")
        tri_loaded = by_layer("tri_loaded")
        table_clear = by_layer("table_clear")
        pos_ready = by_layer("pos_ready")
        needed_ready = by_layer("needed_ready")
        turn_ready = by_layer("turn_ready")
        table_filled = by_layer("table_filled")
        table_read = by_layer("table_read")
        rows_ready = by_layer("rows_ready")
        now_ready = by_layer("now_ready")
        h_stored = by_layer("h_stored")
        sgu_full = by_layer("sgu_full")
        ssilu_ready = by_layer("ssilu_ready")
        sact_ready = by_layer("sact_ready")
        sdn_loaded = by_layer("sdn_loaded")
        sdn_full = by_layer("sdn_full")
        sdn_taken = by_layer("sdn_taken")
        xt_full = by_layer("xt_full")
        gu_full = by_layer("gu_full")
        at_full = by_layer("at_full")
        y_full = by_layer("y_full")
        xt_act, xt_dve = by_layer("xt_act"), by_layer("xt_dve")
        silu_ready = by_layer("silu_ready")
        a_ready = by_layer("a_ready")
        at_ready = by_layer("at_ready")
        y_act, y_dve = by_layer("y_act"), by_layer("y_dve")
        picked_loaded = [by_layer(f"picked_loaded_{i}") for i in range(2)]
        combined = by_layer("combined")
        held_set, dve_step = one("held_set"), one("dve_step")

        def wait_full(eng, *key):
            eng.wait_ge(psum_full, G.at[key] + 1)

        def wait_emptied(eng, *key):
            owner, n = G.emptied_at[G.at[key]]
            eng.wait_ge(emptied[owner], n)

        def bank(*key):
            b = G.at[key] % BANKS
            return ps[:, 512 * b:512 * b + 512]

        stream, last_reader = [], []
        for l in range(DEPTH):
            at = lambda w, k0, k1: w[l].rearrange("(k p) n -> p k n", p=P)[:, :, k0:k1]
            last = ACTIVE[l] - 1

            def item(reader, name, chunks, src):
                stream.append(((l, *name), chunks, src.shape[2] if src else 512, src))
                last_reader.append(reader and (l, *reader))

            for c in range(12):
                item(("ada", c // 4), ("ada", c), KC, at(I["w_ada"], 512 * c, 512 * c + 512))
            item(("kv", NTILE - 1) if last < NTILE - 1 else ("q", last), ("kv",), KC, at(I["w_in"], 0, KV_END))
            item(("kv", NTILE - 1) if last < NTILE - 1 else ("q", last), ("q",), KC, at(I["w_in"], KV_END, Q_END))
            for n, name in enumerate("bcuf"):
                item((name, 3), (name,), KC, at(I["w_in"], Q_END + CONV * n, Q_END + CONV * (n + 1)))
            item(("kvup", NTILE - 1, 1), ("ukv",), 2, at(I["w_ukv"], 0, 1024))
            item(("qup", last, 1), ("uq",), 3, at(I["w_uq"], 0, 768))
            for b, name in enumerate(["w_mla_out", "w_conv_out", "w_four_out"]):
                item(("y", b, KC - 1), ("branch", b), 4, at(I[name], 0, DM))
                for j in range(2):
                    c0 = FOUR_END + b * DM + 512 * j
                    item(("g", b, 4 * j + 3), ("gate", b, j), KC, at(I["w_in"], c0, c0 + 512))
            for j in range(2):
                item(("out", last, 1), ("out", j), KC, at(I["w_out"], 512 * j, 512 * j + 512))
            item(None, ("shared",), KC, None)
        item_at = {key: n for n, (key, *_) in enumerate(stream)}
        per_layer = len(stream) // DEPTH
        assert per_layer % SLOTS == 0 and SLOTS == UNROLL

        def slot(*key):
            n = item_at[key]
            _, k, cols, _ = stream[n]
            return ring[:, n % SLOTS, 0:k * cols].rearrange("p (k n) -> p k n", k=k)

        block = ctx.enter_context(nc.Block())

        @block.sync
        def _(sp):
            rows_of = lambda a: a.rearrange("(t p) d -> p t d", p=P)
            sp.dma_start(xres[:, 0:2, :], rows_of(I["x"][0])).then_inc(x_loaded, 16)
            sp.dma_start(xres[:, 2:4, :], rows_of(I["ctx"][0])).then_inc(x_loaded, 16)
            more = None
            for l in range(DEPTH):
                act = ACTIVE[l]
                for n in range(l * per_layer, (l + 1) * per_layer):
                    key, _, _, src = stream[n]
                    m = n - l * per_layer
                    if l and m < SLOTS:
                        sp.wait_ge(gu_full[l - 1], more * UNROLL + (NE - SLOTS + 1 + m))
                    elif m >= SLOTS:
                        wait_full(sp, *last_reader[n - SLOTS])
                    if src is not None:
                        sp.dma_start(slot(*key), src).then_inc(slot_loaded[n % SLOTS], 16)
                by_p = lambda w: w.rearrange("(p k) n -> p k n", k=KC)
                w = slot(l, "shared")
                sp.dma_start(w[:, :, 0:FE], by_p(I["w_gate_s"][l])).then_inc(slot_loaded[SLOTS - 1], 16)
                sp.dma_start(w[:, :, FE:2 * FE], by_p(I["w_up_s"][l])).then_inc(slot_loaded[SLOTS - 1], 16)
                sp.wait_ge(merged[l], 2 * KC)
                sp.dma_start(dn_s, I["w_down_s"][l].rearrange("(k p) n -> p k n", p=P)).then_inc(sdn_loaded[l], 16)
                wait_full(sp, l, "out", act - 1, 1)
                sp.dma_start(tri, C["tri"]).then_inc(tri_loaded[l], 16)

                def load_expert(u, b, first=False):
                    e = u if first else sp.value_load(item_expert[:, bass.ds(4 * b + u, 1)], min_val=0, max_val=NE - 1)
                    one_of = lambda w, how, **kw: w[l][bass.ds(e, 1)].rearrange(how, **kw)
                    if not first:
                        sp.wait_ge(gu_full[l], 4 * b + u - 3)
                    elif u < 3:
                        wait_full(sp, *last_reader[(l + 1) * per_layer - SLOTS + u])
                    else:
                        sp.wait_ge(sgu_full[l], 2)
                    how = "a (p k) n -> p (a k) n"
                    sp.dma_start(gu[u][:, :, 0:FE], one_of(I["w_gate_e"], how, k=KC)).then_inc(gu_loaded[l][u], 16)
                    sp.dma_start(gu[u][:, :, FE:2 * FE], one_of(I["w_up_e"], how, k=KC)).then_inc(gu_loaded[l][u], 16)
                    if not first:
                        sp.wait_ge(y_full[l], 4 * b + u - 3)
                    elif u < 2:
                        wait_full(sp, l, "y", 2, KC - 1)
                    else:
                        wait_full(sp, l, "h", 2, KC - 1)
                    sp.dma_start(dn[u], one_of(I["w_down_e"], "a (k p) n -> p (a k) n", p=P)).then_inc(dn_loaded[l][u], 16)

                for u in range(UNROLL):
                    load_expert(u, 0, first=True)
                wait_emptied(sp, l, "items")
                more = sp.value_load(more_u[0:1, 0:1], min_val=0, max_val=4)
                with nc.sync.Fori(1, more + BLOCKS) as b:
                    for u in range(UNROLL):
                        load_expert(u, b)
                for u in range(UNROLL):
                    sp.wait_ge(y_stored[l][u], more * 16 + 16 * BLOCKS)
                for t in range(act):
                    if t >= 2:
                        sp.wait_ge(combined[l], t - 1)
                    sp.dma_start(picked[t % 2].rearrange("p (k d) -> p k d", k=TOPK),
                                 y_rows[l].rearrange("(t p k) d -> t p k d", p=P, k=TOPK)[t]).then_inc(picked_loaded[t % 2][l], 16)
            sp.wait_ge(x_updated[DEPTH - 1], 2 * ACTIVE[DEPTH - 1])
            sp.dma_start(rows_of(out[0]), xres[:, 0:2, :]).then_inc(out_stored, 16)
            sp.wait_ge(out_stored, 16)

        @block.gpsimd
        def _(pool):
            pool.dma_start(ident[:, :], C["ident"]).then_inc(consts_loaded, 16)
            pool.dma_start(rope_t[:, :, :, :], C["rope"]).then_inc(consts_loaded, 16)
            pool.dma_start(iota, C["iota"]).then_inc(consts_loaded, 16)
            pool.dma_start(pick_id, C["pick_id"]).then_inc(consts_loaded, 16)
            pool.dma_start(item_t, C["item_t"]).then_inc(consts_loaded, 16)
            pool.dma_start(half_id, C["half_id"]).then_inc(consts_loaded, 16)
            col = lambda a: a.rearrange("(k p) -> p k", p=P)
            nc.gpsimd.memset(held, 0.0).then_inc(held_set, 1)
            pool.wait_ge(held_set, 1)
            for l in range(DEPTH):
                act = ACTIVE[l]
                if l:
                    pool.wait_ge(x_updated[l - 1], 2 * ACTIVE[l - 1])
                with nc.allow_non_contiguous_dma("one small vector a partition"):
                    vectors = [(cs[:, 0, :], col(I["c"][0])), (cs[:, 1, :], col(I["c_ctx"])),
                               (gains[:, 0, :], col(I["g_pre_mix"][l])), (gains[:, 1, :], I["g_pre_ffn"][l].rearrange("(p k) -> p k", k=KC)),
                               (gqk[:, 0:2], col(I["g_kv"][l])), (gqk[:, 2:5], col(I["g_q"][l])),
                               (bgate, I["b_gate"][l].rearrange("(b k p) -> p b k", p=P, b=3)),
                               (wr[:, :, :], I["w_router"][l].rearrange("(p k) e -> p k e", k=KC)),
                               (brow, I["b_router"][l:l + 1, :].to_broadcast([P, NE])),
                               (gpost[:, 0, :], I["g_post_mix"][l:l + 1, :].to_broadcast([P, DM])),
                               (gpost[:, 1, :], I["g_post_ffn"][l:l + 1, :].to_broadcast([P, DM]))]
                    vectors += [(convw[:, j, :], col(I["conv_w"][l][j])) for j in range(3)]
                    assert len(vectors) == 14
                    for dst, src in vectors:
                        pool.dma_start(dst, src).then_inc(params_loaded[l], 16)
                nc.gpsimd.memset(ca32, 0.0).then_inc(adab_zero[l], 1)
                nc.gpsimd.memset(ada_bias, 0.0).then_inc(adab_zero[l], 1)
                pool.wait_ge(adab_zero[l], 2)
                for j in range(4):
                    src = I["b_ada"][l].rearrange("(r j c) -> j r c", j=4, c=512)[j:j + 1]
                    for s in range(2):
                        pool.dma_start(ada_bias[32 * j + s:32 * j + s + 1], src).then_inc(adab_loaded[l], 16)
                pool.wait_ge(coef_ready[l], 1)
                pool.dma_start(head[:, 0:1280], C["dft"]).then_inc(dft_loaded[l], 16)
                for b in (1, 2):
                    for dc in range(KC):
                        n = (b - 1) * KC + dc
                        wait_emptied(pool, l, "y", b, dc)
                        if b == 2:
                            pool.wait_ge(merged[l], n - KC + 1)
                        nc.gpsimd.tensor_tensor(mT[:, dc, 0:P * act], mT[:, dc, 0:P * act],
                                                ytmp[:, n % 2, 0:P * act], ALU.add).then_inc(merged[l], 1)
                pool.dma_start(slots_d[l], C["absent"][0:P * act * NE]).then_inc(table_clear[l], 16)
                pool.wait_ge(table_clear[l], 16)
                pool.wait_ge(pos_ready[l], 1)
                for t in range(act):
                    for k in range(TOPK):
                        pool.indirect_dma_start(out=slots_d[l], out_offset=bass.IndirectOffsetOnAxis(ap=posu[:, t, k:k + 1], axis=0),
                                                in_=pick_id[:, t, k:k + 1], in_offset=None,
                                                bounds_check=P * act * NE - 1, oob_is_err=False).then_inc(table_filled[l], 16)
                pool.wait_ge(table_filled[l], 16 * act * TOPK)
                for p0 in range(0, P, CAP[l]):
                    pool.dma_start(row_y[p0:p0 + CAP[l], 0:P], slots_d[l].rearrange("(r j e) a -> j r (e a)", e=NE, j=CAP[l]))\
                        .then_inc(table_read[l], 16)
                pool.dma_start(row_y[:, P:P + 1], C["absent"][0:P]).then_inc(table_read[l], 16)
                pool.wait_ge(h_stored[l], 16 * act)
                pool.wait_ge(rows_ready[l], 1)
                wait_emptied(pool, l, "items")
                more = pool.value_load(more_u[0:1, 0:1], min_val=0, max_val=4)
                split = P // CAP[l]
                source = h_rows[l].rearrange("t (a d) -> (t a) d", a=split)
                target = y_rows[l].rearrange("t (a d) -> (t a) d", a=split)
                n_g = P * act * split - 1
                n_y = P * act * TOPK * split - 1

                def column(u, b):
                    return pool.value_load(item_col[:, bass.ds(4 * b + u, 1)], min_val=0, max_val=P)

                def copied(count):
                    pool.wait_ge(now_ready[l], count)
                    nc.gpsimd.tensor_tensor(held, held, held, ALU.mult).then_inc(now_ready[l], 1)

                def gather(u, b, first=False):
                    n = u if first else column(u, b)
                    if not first:
                        pool.wait_ge(xt_full[l], 4 * b + u - 3)
                    pool.wait_ge(rows_ready[l], 1)
                    nc.gpsimd.tensor_copy(now_g[:, u:u + 1], row_g[:, bass.ds(n, 1)]).then_inc(now_ready[l], 1)
                    copied((16 * b + 4 * u - 7) if not first else 2 * u + 1)
                    pool.indirect_dma_start(out=xg[u][:, 0:wide[l]], out_offset=None, in_=source,
                                            in_offset=bass.IndirectOffsetOnAxis(ap=now_g[:, u:u + 1], axis=0),
                                            bounds_check=n_g, oob_is_err=False).then_inc(x_gathered[l][u], 16)

                def store(u, b, copies):
                    n = column(u, b)
                    pool.wait_ge(y_act[l], 4 * b + u + 1)
                    if l == 0:
                        pool.wait_ge(y_dve[l], 4 * b + u + 1)
                    nc.gpsimd.tensor_copy(now_y[:, u:u + 1], row_y[:, bass.ds(n, 1)]).then_inc(now_ready[l], 1)
                    copied(copies)
                    pool.indirect_dma_start(out=target, out_offset=bass.IndirectOffsetOnAxis(ap=now_y[:, u:u + 1], axis=0),
                                            in_=y_e[u % 2][:, 0:wide[l]], in_offset=None,
                                            bounds_check=n_y, oob_is_err=False).then_inc(y_stored[l][u], 16)

                for u in range(UNROLL):
                    gather(u, 0, first=True)
                with nc.gpsimd.Fori(1, more + BLOCKS) as b:
                    for u in range(UNROLL):
                        gather(u, b)
                        store(u, b - 1, 16 * b + 4 * u - 5)
                for u in range(UNROLL):
                    store(u, more + (BLOCKS - 1), more * (4 * UNROLL) + (4 * NE - 7 + 2 * u))

        @block.scalar
        def _(act_e):
            act = None

            for l in range(DEPTH):
                act = ACTIVE[l]
                n_tok = P * act
                roots, squares = [0], [0]

                def square(src, into, width):
                    act_e.wait_ge(ssq_ready[l], squares[0])
                    squares[0] += 1
                    nc.scalar.activation(junk[:, 0:width], src, ACT.Square, accum_out=ssq[:, into:into + 1])\
                        .then_inc(ssq_ready[l], 1)

                def root(c0, c1):
                    roots[0] += 1
                    act_e.wait_ge(ms_ready[l], roots[0])
                    nc.scalar.activation(rstd[:, c0:c1], ssq[:, c0:c1], ACT.Sqrt).then_inc(root_ready[l], 1)

                if l:
                    act_e.wait_ge(ssq_ready[l - 1], last_squares)
                act_e.wait_ge(params_loaded[l], 16 * 14)
                act_e.wait_ge(adab_zero[l], 2)
                nc.scalar.activation(ca32[:, :, 0:2], cs.rearrange("p s k -> p k s"), ACT.Silu).then_inc(ca_ready[l], 1)
                if l == 0:
                    act_e.wait_ge(x_loaded, 32)
                else:
                    act_e.wait_ge(x_updated[l - 1], 2 * ACTIVE[l - 1])
                for t in range(NTILE):
                    square(xres[:, t, :], t, DM)
                root(0, 4)
                wait_full(act_e, l, "adaT")
                src = bank(l, "adaT").rearrange("p (b j m) -> p b j m", b=4, j=4)[:, :, :, 0:2]
                nc.scalar.activation(adaT, src, ACT.Copy).then_inc(emptied["act"], 1)
                wait_full(act_e, l, "adaP")
                nc.scalar.activation(adaP, bank(l, "adaP")[:, 0:32].rearrange("p (n k s) -> p n k s", n=2, k=KC),
                                     ACT.Copy).then_inc(emptied["act"], 1)

                def modulate(n):
                    act_e.wait_ge(coef_ready[l], 1)
                    for k in range(1, KC, 2):
                        wait_full(act_e, l, "h", n, k)
                        for s in range(2 if n == 1 else act // 2):
                            ins = nc.scalar.activation(hT[:, k, SEQ * s:SEQ * s + SEQ], bank(l, "h", n, k)[:, SEQ * s:SEQ * s + SEQ],
                                                       ACT.Identity, scale=scaleT[:, n - 1, s, k:k + 1],
                                                       bias=shiftT[:, n - 1, s, k:k + 1])
                        ins.then_inc(emptied["act"], 1)

                modulate(1)
                for t in range(NTILE):
                    wait_full(act_e, l, "kv", t)
                    square(bank(l, "kv", t)[:, 0:KVR], 4 + t, KVR)
                    nc.scalar.activation(kvlat[:, t, :], bank(l, "kv", t)[:, 0:KV_END], ACT.Copy).then_inc(emptied["act"], 1)
                    if t < act:
                        wait_full(act_e, l, "q", t)
                        square(bank(l, "q", t)[:, 0:QR], 8 + t, QR)
                        nc.scalar.activation(qlat[:, t, :], bank(l, "q", t)[:, 0:QR], ACT.Copy).then_inc(emptied["act"], 1)
                root(4, 8 + act)
                for name, dst in (("b", bT), ("c", cT)):
                    for f in range(4):
                        wait_full(act_e, l, name, f)
                        nc.scalar.activation(dst[:, f, 0:n_tok], bank(l, name, f)[:, 0:n_tok], ACT.Copy).then_inc(emptied["act"], 1)
                for f in range(4):
                    wait_full(act_e, l, "f", f)
                    nc.scalar.activation(fT[:, f, 0:n_tok], bank(l, "f", f)[:, 0:n_tok], ACT.Copy).then_inc(emptied["act"], 1)
                for c in range(3):
                    wait_full(act_e, l, "cqT", c)
                    nc.scalar.activation(cqT[:, c, 0:n_tok], bank(l, "cqT", c)[:, 0:n_tok], ACT.Identity,
                                         scale=gqk[:, 2 + c:3 + c]).then_inc(emptied["act"], 1)
                for t in range(NTILE):
                    for j in range(2):
                        wait_full(act_e, l, "kvup", t, j)
                        src = bank(l, "kvup", t, j).rearrange("p (h d) -> p h d", h=4)
                        nc.scalar.activation(ktok[:, t, 4 * j:4 * j + 4, 0:NOPE], src[:, :, 0:NOPE], ACT.Copy)
                        nc.scalar.activation(vtok[:, t, 4 * j:4 * j + 4, :], src[:, :, NOPE:], ACT.Copy).then_inc(emptied["act"], 1)
                n = 0
                for f in range(FG):
                    for s in range(act // 2):
                        wait_full(act_e, l, "four1", f, s)
                        nc.scalar.activation(four_ab[n], bank(l, "four1", f, s), ACT.Copy).then_inc(emptied["act"], 1)
                        n += 1
                units = attention_units(l)
                for u in range(len(units) + 1):
                    if u < len(units):
                        h, s = units[u]
                        keys = 512 if s == 0 else 256
                        if s == 0:
                            wait_full(act_e, l, "qT", h)
                            nc.scalar.activation(headT[0:QK, h % 2, 0, 0:n_tok], bank(l, "qT", h)[0:QK, 0:n_tok],
                                                 ACT.Copy).then_inc(emptied["act"], 1)
                        for t in range(2):
                            act_e.wait_ge(max_ready[l], 2 * u + t + 1)
                            if u >= 2:
                                wait_full(act_e, l, "PT", *units[u - 2], t)
                            c = 2 * (u % 2) + t
                            nc.scalar.activation(probs[:, u % 2, t, 0:keys], bank(l, "S", h, s, t)[:, 0:keys], ACT.Exp,
                                                 scale=ATT_SCALE, bias=nmax[:, c:c + 1],
                                                 accum_out=ssum[:, c:c + 1]).then_inc(emptied["act"], 1)
                    if u >= 1:
                        h, s = units[u - 1]
                        nk = 4 if s == 0 else 2
                        wait_full(act_e, l, "PT", h, s, 1)
                        nc.scalar.activation(probsT[:, (u - 1) % 2, 0:nk, P:2 * P],
                                             bank(l, "PT", h, s, 1)[:, 0:P * nk].rearrange("p (k q) -> p k q", q=P),
                                             ACT.Copy).then_inc(emptied["act"], 1)
                for b in range(3):
                    for dc in range(KC):
                        n = b * KC + dc
                        wait_full(act_e, l, "g", b, dc)
                        if n >= 2:
                            wait_emptied(act_e, l, "y", (n - 2) // KC, (n - 2) % KC)
                        nc.scalar.activation(tmp2[:, n % 2, 0:n_tok], bank(l, "g", b, dc)[:, 0:n_tok], ACT.Sigmoid,
                                             bias=bgate[:, b, dc:dc + 1]).then_inc(emptied["act"], 1)
                wait_emptied(act_e, l, "y", 2, KC - 1)
                for t in range(act):
                    if t >= 2:
                        act_e.wait_ge(x_updated[l], t - 1)
                    for j in range(2):
                        wait_full(act_e, l, "out", t, j)
                        square(bank(l, "out", t, j), 12 + 2 * t + j, 512)
                        nc.scalar.activation(rows[:, t % 2, 512 * j:512 * j + 512], bank(l, "out", t, j), ACT.Copy)\
                            .then_inc(emptied["act"], 1)
                    root(12 + 2 * t, 13 + 2 * t)
                act_e.wait_ge(x_updated[l], act)
                for t in range(act):
                    square(xres[:, t, :], t, DM)
                root(0, act)
                modulate(2)
                for t in range(act):
                    wait_full(act_e, l, "rt", t)
                    nc.scalar.activation(score[:, t, :], bank(l, "rt", t)[:, 0:NE], ACT.Sigmoid).then_inc(emptied["act"], 1)
                for t in range(act):
                    for j in range(2):
                        wait_full(act_e, l, "hrow", t, j)
                        nc.scalar.activation(hrow[t][:, 512 * j:512 * j + 512], bank(l, "hrow", t, j), ACT.Copy)\
                            .then_inc(emptied["act"], 1)
                    wait_emptied(act_e, l, "hrow", t, 1)
                    act_e.dma_start(h_rows[l].rearrange("(t p) d -> t p d", p=P)[t], hrow[t]).then_inc(h_stored[l], 16)
                act_e.wait_ge(pos_ready[l], 1)
                for f in range(2):
                    act_e.wait_ge(sgu_full[l], f + 1)
                    nc.scalar.activation(silu_s[:, f, 0:n_tok], ps[:, 512 * f:512 * f + n_tok], ACT.Silu).then_inc(ssilu_ready[l], 1)
                wait_emptied(act_e, l, "items")
                more = nc.scalar.value_load(more_u[0:1, 0:1], min_val=0, max_val=4)
                half = wide[l] // 2
                fw = CAP[l] * 2

                def take_x(u, b, n=None):
                    act_e.wait_ge(xt_full[l], 4 * b + u + 1)
                    if n is None or n >= 2:
                        act_e.wait_ge(gu_full[l], 4 * b + u - 1)
                    nc.scalar.activation(xT[u % 2][:, 0:half], ps[:, 1024:1024 + half], ACT.Copy).then_inc(xt_act[l], 1)

                def silus(u, b, n=None):
                    act_e.wait_ge(gu_full[l], 4 * b + u + 1)
                    if n is None or n >= 2:
                        act_e.wait_ge(a_ready[l], 4 * b + u - 1)
                    nc.scalar.activation(silu_e[u % 2][:, 0:fw], ps[:, 512 * (u % 2):512 * (u % 2) + fw], ACT.Silu)\
                        .then_inc(silu_ready[l], 1)

                def take_y(u, b, n=None):
                    act_e.wait_ge(y_full[l], 4 * b + u + 1)
                    if n is None or n >= 2:
                        act_e.wait_ge(y_stored[l][(u - 2) % 4], 16 * b + (16 if u >= 2 else 0))
                    nc.scalar.activation(y_e[u % 2][:, 0:512], ps[:, 2560:3072], ACT.Copy).then_inc(y_act[l], 1)

                for n in range(UNROLL):
                    take_x(n, 0, n)
                    if n >= 1:
                        silus(n - 1, 0, n - 1)
                    if n >= 2:
                        take_y(n - 2, 0, n - 2)
                with nc.scalar.Fori(1, more + BLOCKS) as b:
                    for u in range(UNROLL):
                        take_x(u, b)
                        silus((u - 1) % 4, b - (u < 1))
                        take_y((u - 2) % 4, b - (u < 2))
                silus(3, more + (BLOCKS - 1))
                take_y(2, more + (BLOCKS - 1))
                take_y(3, more + (BLOCKS - 1))
                for t in range(act):
                    act_e.wait_ge(combined[l], t + 1)
                    square(acc[:, t, :], t, DM)
                root(0, act)
                last_squares = squares[0]

        @block.tensor
        def _(pe):
            opened = [0]

            def group(*key):
                n = G.at[key]
                assert n == opened[0]
                opened[0] += 1
                if n >= BANKS:
                    owner, count = G.emptied_at[n - BANKS]
                    pe.wait_ge(emptied[owner], count)
                return bank(*key)

            def arrived(*key):
                n = item_at[key]
                more_dmas = n // per_layer if n % SLOTS == SLOTS - 1 else 0
                pe.wait_ge(slot_loaded[n % SLOTS], 16 * (n // SLOTS + 1 + more_dmas))
                return slot(*key)

            def chain(dst, pairs):
                for n, (a, b) in enumerate(pairs):
                    ins = nc.tensor.matmul(dst, a, b, start=n == 0, stop=n == len(pairs) - 1)
                return ins

            for l in range(DEPTH):
                act = ACTIVE[l]
                n_tok = P * act
                tile = lambda t: slice(P * t, P * t + P)
                if l == 0:
                    pe.wait_ge(consts_loaded, 96)
                else:
                    pe.wait_ge(combined[l - 1], 1)
                pe.wait_ge(ca_ready[l], 1)
                for r in range(3):
                    dst = group(l, "ada", r)
                    w = [arrived(l, "ada", 4 * r + j) for j in range(4)]
                    for k in range(KC):
                        for j in range(4):
                            ins = nc.tensor.matmul(dst[32 * j:32 * j + 32, :], ca32[:, k, :], w[j][:, k, :],
                                                   start=k == 0, stop=k == KC - 1, skip_group_check=True)
                    ins.then_inc(psum_full, 1)
                dst = group(l, "adaT")
                wait_emptied(pe, l, "ada", 0)
                for b in range(4):
                    ins = nc.tensor.transpose(dst[:, tile(b)], ada_row[:, 0, tile(b)], ident[:, :])
                ins.then_inc(psum_full, 1)
                dst = group(l, "adaP")
                wait_emptied(pe, l, "ada", 2)
                for n, (r, j) in enumerate(((1, 2), (2, 0))):
                    for k in range(KC):
                        for a in range(2):
                            c = 2 * (KC * n + k)
                            ins = nc.tensor.matmul(dst[64 * a:64 * a + 64, c:c + 2],
                                                   ada_row[:, r, :].rearrange("p (q k) -> p k q", k=KC)[:, k, :],
                                                   ident[:, 32 * (j + a):32 * (j + a) + 2], start=True, stop=True,
                                                   skip_group_check=True)
                ins.then_inc(psum_full, 1)
                for n in (1, 2):
                    for s in range(act // 2):
                        for j in range(2):
                            dst = group(l, "gaterow", n, s, j)
                            src_j = j if n == 1 else 2 + j
                            pick = ident[:, 32 * src_j + s:32 * src_j + s + 1].to_broadcast([P, P])
                            nc.tensor.matmul(dst, pick, ada_row[:, n, :], start=True, stop=True).then_inc(psum_full, 1)

                def transpose_h(n, tiles):
                    for k in range(KC):
                        dst = group(l, "h", n, k)
                        for t in range(tiles):
                            if k == 0:
                                pe.wait_ge(xn_ready[l], (0 if n == 1 else NTILE) + t + 1)
                            cols = xn[:, t, tile(k)] if n == 1 else xn[:, t, :].rearrange("p (q k) -> p k q", k=KC)[:, k, :]
                            ins = nc.tensor.transpose(dst[:, tile(t)], cols, ident[:, :])
                        ins.then_inc(psum_full, 1)

                transpose_h(1, NTILE)
                wkv, wq = None, None
                for t in range(NTILE):
                    dst = group(l, "kv", t)
                    wkv = arrived(l, "kv")
                    if t == 0:
                        wait_emptied(pe, l, "h", 1, KC - 2)
                        wait_emptied(pe, l, "h", 1, KC - 1)
                    chain(dst[:, 0:KV_END], [(hT[:, k, tile(t)], wkv[:, k, :]) for k in range(KC)]).then_inc(psum_full, 1)
                    if t < act:
                        dst = group(l, "q", t)
                        wq = arrived(l, "q")
                        chain(dst[:, 0:QR], [(hT[:, k, tile(t)], wq[:, k, :]) for k in range(KC)]).then_inc(psum_full, 1)
                for name in "bcuf":
                    for f in range(4):
                        dst = group(l, name, f)
                        w = arrived(l, name)
                        chain(dst[:, 0:n_tok], [(w[:, k, tile(f)], hT[:, k, 0:n_tok]) for k in range(KC)]).then_inc(psum_full, 1)
                pe.wait_ge(lat_ready[l], 1)
                for c in range(2):
                    dst = group(l, "ckvT", c)
                    for t in range(NTILE):
                        ins = nc.tensor.transpose(dst[:, tile(t)], kvlat[:, t, tile(c)], ident[:, :])
                    ins.then_inc(psum_full, 1)
                for c in range(3):
                    dst = group(l, "cqT", c)
                    for t in range(act):
                        ins = nc.tensor.transpose(dst[:, tile(t)], qlat[:, t, tile(c)], ident[:, :])
                    ins.then_inc(psum_full, 1)
                for t in range(NTILE):
                    for j in range(2):
                        dst = group(l, "kvup", t, j)
                        w = arrived(l, "ukv")
                        wait_emptied(pe, l, "ckvT", 1)
                        chain(dst, [(ckvT[:, c, tile(t)], w[:, c, 512 * j:512 * j + 512]) for c in range(2)]).then_inc(psum_full, 1)
                for t in range(act):
                    for j in range(2):
                        dst = group(l, "qup", t, j)
                        w = arrived(l, "uq")
                        wait_emptied(pe, l, "cqT", 2)
                        chain(dst[:, 0:4 * QK], [(cqT[:, c, tile(t)], w[:, c, 4 * QK * j:4 * QK * (j + 1)]) for c in range(3)])\
                            .then_inc(psum_full, 1)
                pe.wait_ge(dft_loaded[l], 16)
                for f in range(FG):
                    wait_emptied(pe, l, "f", f)
                    for s in range(act // 2):
                        dst = group(l, "four1", f, s)
                        for t in range(2):
                            ins = nc.tensor.matmul(dst[:, 256 * t:256 * t + 256], fT[:, f, tile(2 * s + t)], dft_c,
                                                   start=True, stop=True)
                        ins.then_inc(psum_full, 1)
                for f in range(FG):
                    dst = group(l, "four2", f)
                    for s in range(act // 2):
                        n = f * (act // 2) + s
                        wait_emptied(pe, l, "four1", f, s)
                        ab = four_ab[n].rearrange("p (t a c) -> p t a c", t=2, a=2)
                        ins = chain(dst[:, SEQ * s:SEQ * s + SEQ],
                                    [(ab[:, t, a, :], dft_n[:, a, t, :]) for t in range(2) for a in range(2)])
                    ins.then_inc(psum_full, 1)
                wait_emptied(pe, l, "kvup", NTILE - 1, 1)
                pe.wait_ge(kpe_ready[l], 1)
                pe.wait_ge(qrope_ready[l], 1)
                units = attention_units(l)
                for u in range(len(units) + 1):
                    if u < len(units):
                        h, s = units[u]
                        if s == 0:
                            dst = group(l, "kT", h)
                            for t in range(NTILE):
                                ins = nc.tensor.transpose(dst[0:QK, tile(t)], ktok[:, t, h, :], ident[:, :])
                            ins.then_inc(psum_full, 1)
                            dst = group(l, "qT", h)
                            for t in range(act):
                                ins = nc.tensor.transpose(dst[0:QK, tile(t)], qtok[:, t, h, :], ident[:, :])
                            ins.then_inc(psum_full, 1)
                            wait_emptied(pe, l, "kT", h)
                            wait_emptied(pe, l, "qT", h)
                        k0 = 0 if s == 0 else SEQ
                        for t in range(2):
                            dst = group(l, "S", h, s, t)
                            nc.tensor.matmul(dst[:, 0:512 - k0], headT[0:QK, h % 2, 0, tile(2 * s + t)],
                                             headT[0:QK, h % 2, 1, k0:512], start=True, stop=True).then_inc(psum_full, 1)
                    if u >= 1:
                        h, s = units[u - 1]
                        nk = 4 if s == 0 else 2
                        for t in range(2):
                            dst = group(l, "PT", h, s, t)
                            pe.wait_ge(prob_ready[l], 2 * (u - 1) + t + 1)
                            for k in range(nk):
                                ins = nc.tensor.transpose(dst[:, tile(k)], probs[:, (u - 1) % 2, t, tile(k)], ident[:, :])
                            ins.then_inc(psum_full, 1)
                        dst = group(l, "O", h, s)
                        for t in range(2):
                            wait_emptied(pe, l, "PT", h, s, t)
                        half = slice(VD * (h % 2), VD * (h % 2) + VD)
                        chain(dst[half, 0:SEQ], [(vtok[:, (NTILE - nk) + k, h, :], probsT[:, (u - 1) % 2, k, :]) for k in range(nk)])\
                            .then_inc(psum_full, 1)
                wait_emptied(pe, l, "O", *units[-1])
                branch = [oT, bT, fT]
                for b in range(3):
                    for dc in range(KC):
                        if b == 1 and dc == 0:
                            pe.wait_ge(conv_ready[l], 4)
                        if b == 2 and dc == 0:
                            wait_emptied(pe, l, "four2", FG - 1)
                        dst = group(l, "g", b, dc)
                        wo = arrived(l, "branch", b)
                        w = arrived(l, "gate", b, dc // 4)
                        chain(dst[:, 0:n_tok], [(w[:, k, tile(dc % 4)], hT[:, k, 0:n_tok]) for k in range(KC)]).then_inc(psum_full, 1)
                        dst = group(l, "y", b, dc)
                        chain(dst[:, 0:n_tok], [(wo[:, c, tile(dc)], branch[b][:, c, 0:n_tok]) for c in range(4)])\
                            .then_inc(psum_full, 1)
                pe.wait_ge(merged[l], 2 * KC)
                wo2 = [arrived(l, "out", j) for j in range(2)]
                for t in range(act):
                    for j in range(2):
                        dst = group(l, "out", t, j)
                        chain(dst, [(mT[:, k, tile(t)], wo2[j][:, k, :]) for k in range(KC)]).then_inc(psum_full, 1)
                transpose_h(2, act)
                wait_emptied(pe, l, "h", 2, KC - 2)
                wait_emptied(pe, l, "h", 2, KC - 1)
                for t in range(act):
                    dst = group(l, "rt", t)
                    chain(dst[:, 0:NE], [(hT[:, k, tile(t)], wr[:, k, :]) for k in range(KC)]).then_inc(psum_full, 1)
                for t in range(act):
                    for j in range(2):
                        dst = group(l, "hrow", t, j)
                        for k in range(4):
                            ins = nc.tensor.transpose(dst[:, tile(k)], hT[:, 4 * j + k, tile(t)], ident[:, :])
                        ins.then_inc(psum_full, 1)
                dst = group(l, "rank")
                pe.wait_ge(tri_loaded[l], 16)
                pe.wait_ge(mask_ready[l], 1)
                ones, above = tri[:, 0:P], tri[:, P:2 * P]
                for t in range(act):
                    chain(dst[:, NE * t:NE * t + NE], [(ones, mask[:, a, :]) for a in range(t)] + [(above, mask[:, t, :])])
                for r in range(ROUNDS):
                    for a in range(act):
                        ins = nc.tensor.matmul(dst[NE * r:NE * r + NE, P:P + 1], mask[:, a, :], ones[:, 0:1], start=a == 0,
                                               stop=a == act - 1, skip_group_check=True)
                ins.then_inc(psum_full, 1)
                dst = group(l, "turn")
                pe.wait_ge(needed_ready[l], 1)
                nc.tensor.matmul(dst[:, 0:1], above, needed, start=True, stop=True)
                nc.tensor.matmul(dst[:, 1:2], ones, needed, start=True, stop=True).then_inc(psum_full, 1)
                dst = group(l, "items")
                pe.wait_ge(turn_ready[l], 1)
                for a in range(2):
                    ins = nc.tensor.matmul(dst[0:1, MAX_ITEMS * a:MAX_ITEMS * (a + 1)], item_t[:, 2 + a:3 + a], turn,
                                           start=True, stop=True)
                ins.then_inc(psum_full, 1)
                pe.wait_ge(slot_loaded[SLOTS - 1], 16 * (item_at[(l, "shared")] // SLOTS + 1 + l) + 16)
                wait_emptied(pe, l, "items")
                wait_emptied(pe, l, "hrow", act - 1, 1)
                w = slot(l, "shared")
                for f in range(2):
                    for a in range(2):
                        b = f + 2 * a
                        ins = chain(ps[:, 512 * b:512 * b + n_tok],
                                    [(w[:, k, FE * a + P * f:FE * a + P * f + P], hT[:, k, 0:n_tok]) for k in range(KC)])
                    ins.then_inc(sgu_full[l], 1)
                pe.wait_ge(sdn_loaded[l], 16)
                pe.wait_ge(sact_ready[l], 2)
                for g in range(2 * act):
                    t, hf = g // 2, g % 2
                    b = 4 + g % 4
                    if g >= 4:
                        pe.wait_ge(sdn_taken[l], g - 3)
                    chain(ps[:, 512 * b:512 * b + 512],
                          [(act_s[:, f, tile(t)], dn_s[:, f, 512 * hf:512 * hf + 512]) for f in range(2)])\
                        .then_inc(sdn_full[l], 1)
                pe.wait_ge(sdn_taken[l], 2 * act)
                wait_emptied(pe, l, "items")
                more = nc.tensor.value_load(more_u[0:1, 0:1], min_val=0, max_val=4)

                narrow = CAP[l] < P

                def transpose_x(u, b, n=None):
                    pe.wait_ge(x_gathered[l][u], 16 * b + 16)
                    if n is None or n >= 1:
                        pe.wait_ge(xt_act[l], 4 * b + u)
                        pe.wait_ge(xt_dve[l], 4 * b + u)
                    for k in range(wide[l] // P):
                        c = 1024 + (P * k if not narrow else 512 * (k // 2) + P * (k % 2))
                        ins = nc.tensor.transpose(ps[:, c:c + P], xg[u][:, tile(k)], ident[:, :])
                    ins.then_inc(xt_full[l], 1)

                def gate_up(u, b):
                    pe.wait_ge(gu_loaded[l][u], 32 * b + 32)
                    pe.wait_ge(xt_act[l], 4 * b + u + 1)
                    pe.wait_ge(xt_dve[l], 4 * b + u + 1)
                    o = 512 * (u % 2)
                    x = xT[u % 2]
                    for k in range(KC):
                        if not narrow:
                            ins = nc.tensor.matmul(ps[:, o:o + 512], x[:, tile(k)], gu[u][:, k, :], start=k == 0, stop=k == KC - 1)
                        else:
                            xk = x[:, P * (k % 4) + 64 * (k // 4):P * (k % 4) + 64 * (k // 4) + 64]
                            for f in range(2):
                                w = gu[u][:, k, :].rearrange("p (a n) -> p a n", a=2)[:, :, P * f:P * f + P]
                                ins = nc.tensor.matmul(ps[64 * f:64 * f + 64, o:o + 256], xk, w, start=k == 0,
                                                       stop=k == KC - 1, skip_group_check=True)
                    ins.then_inc(gu_full[l], 1)

                def transpose_a(u, b, n=None):
                    pe.wait_ge(a_ready[l], 4 * b + u + 1)
                    if n is None or n >= 1:
                        pe.wait_ge(at_ready[l], 4 * b + u)
                    for f in range(1 if narrow else 2):
                        ins = nc.tensor.transpose(ps[:, 2048 + P * f:2048 + P * f + P], a_e[u % 2][:, tile(f)], ident[:, :])
                    ins.then_inc(at_full[l], 1)

                def down(u, b, n=None):
                    pe.wait_ge(at_ready[l], 4 * b + u + 1)
                    pe.wait_ge(dn_loaded[l][u], 16 * b + 16)
                    if n is None or n >= 1:
                        pe.wait_ge(y_act[l], 4 * b + u)
                        if not narrow:
                            pe.wait_ge(y_dve[l], 4 * b + u)
                    for f in range(2):
                        for c in range(2):
                            if not narrow:
                                ins = nc.tensor.matmul(ps[:, 2560 + 512 * c:3072 + 512 * c], aT_e[u % 2][:, tile(f)],
                                                       dn[u][:, f, 512 * c:512 * c + 512], start=f == 0, stop=f == 1)
                            else:
                                ins = nc.tensor.matmul(ps[64 * c:64 * c + 64, 2560:3072], aT_e[u % 2][:, 64 * f:64 * f + 64],
                                                       dn[u][:, f, 512 * c:512 * c + 512], start=f == 0, stop=f == 1,
                                                       skip_group_check=True)
                    ins.then_inc(y_full[l], 1)

                for n in range(UNROLL):
                    transpose_x(n, 0, n)
                    if n >= 2:
                        transpose_a(n - 2, 0, n - 2)
                    if n >= 1:
                        gate_up(n - 1, 0)
                    if n >= 2:
                        down(n - 2, 0, n - 2)
                with nc.tensor.Fori(1, more + BLOCKS) as b:
                    for u in range(UNROLL):
                        transpose_x(u, b)
                        transpose_a((u - 2) % 4, b - (u < 2))
                        gate_up((u - 1) % 4, b - (u < 1))
                        down((u - 2) % 4, b - (u < 2))
                last = more + (BLOCKS - 1)
                transpose_a(2, last)
                gate_up(3, last)
                down(2, last)
                transpose_a(3, last)
                down(3, last)

        @block.vector
        def _(dve):
            steps = [0]

            def link(ins):
                steps[0] += 1
                ins.then_inc(dve_step, 1)
                dve.wait_ge(dve_step, steps[0])

            V = nc.vector
            dve.wait_ge(consts_loaded, 96)
            for l in range(DEPTH):
                act = ACTIVE[l]
                n_tok = P * act
                counts = {"ssq": 0, "root": 0}

                def mean_square(count, pieces):
                    counts["ssq"] += count
                    dve.wait_ge(ssq_ready[l], counts["ssq"])
                    for c0, c1, width in pieces:
                        ins = V.tensor_scalar(ssq[:, c0:c1], ssq[:, c0:c1], 1.0 / width, EPS, ALU.mult, ALU.add)
                    ins.then_inc(ms_ready[l], 1)

                def inverse_root(c0, c1):
                    counts["root"] += 1
                    dve.wait_ge(root_ready[l], counts["root"])
                    link(V.reciprocal(rstd[:, c0:c1], rstd[:, c0:c1]))

                mean_square(NTILE, [(0, 4, DM)])
                inverse_root(0, 4)
                for t in range(NTILE):
                    V.tensor_scalar(xn[:, t, :], xres[:, t, :], rstd[:, t:t + 1], None, ALU.mult).then_inc(xn_ready[l], 1)
                dve.wait_ge(adab_loaded[l], 16 * 8)
                dve.wait_ge(params_loaded[l], 16 * 14)
                for r in range(3):
                    wait_full(dve, l, "ada", r)
                    V.tensor_tensor(ada_row[:, r, :], bank(l, "ada", r), ada_bias[:, r, :], ALU.add).then_inc(emptied["dve"], 1)
                wait_emptied(dve, l, "adaT")
                wait_emptied(dve, l, "adaP")
                for s in range(2):
                    V.scalar_tensor_tensor(scaleT[:, 0, s, :].rearrange("p (j b) -> p j b", j=2),
                                           adaT[:, :, 2:4, s].rearrange("p b j -> p j b"), 1.0,
                                           gains[:, 0, :].rearrange("p (j b) -> p j b", j=2), ALU.add, ALU.mult)
                    V.tensor_copy(shiftT[:, 0, s, :].rearrange("p (j b) -> p j b", j=2),
                                  adaT[:, :, 0:2, s].rearrange("p b j -> p j b"))
                    V.scalar_tensor_tensor(scaleT[:, 1, s, :], adaP[:, 1, :, s], 1.0, gains[:, 1, :], ALU.add, ALU.mult)
                    ins = V.tensor_copy(shiftT[:, 1, s, :], adaP[:, 0, :, s])
                ins.then_inc(coef_ready[l], 1)
                for n in (1, 2):
                    for s in range(act // 2):
                        for j in range(2):
                            wait_full(dve, l, "gaterow", n, s, j)
                            V.tensor_tensor(Grow[:, n - 1, s, 512 * j:512 * j + 512], bank(l, "gaterow", n, s, j),
                                            gpost[:, n - 1, 512 * j:512 * j + 512], ALU.mult).then_inc(emptied["dve"], 1)

                def modulate(n):
                    dve.wait_ge(coef_ready[l], 1)
                    for k in range(0, KC, 2):
                        wait_full(dve, l, "h", n, k)
                        for s in range(2 if n == 1 else act // 2):
                            ins = V.tensor_scalar(hT[:, k, SEQ * s:SEQ * s + SEQ], bank(l, "h", n, k)[:, SEQ * s:SEQ * s + SEQ],
                                                  scaleT[:, n - 1, s, k:k + 1], shiftT[:, n - 1, s, k:k + 1], ALU.mult, ALU.add)
                        ins.then_inc(emptied["dve"], 1)

                modulate(1)
                mean_square(NTILE + act, [(4, 8, KVR), (8, 8 + act, QR)])
                inverse_root(4, 8 + act)
                wait_emptied(dve, l, "kv", NTILE - 1)
                wait_emptied(dve, l, "q", act - 1)
                for t in range(NTILE):
                    V.tensor_scalar(kvlat[:, t, 0:KVR], kvlat[:, t, 0:KVR], rstd[:, 4 + t:5 + t], None, ALU.mult)
                for t in range(act):
                    ins = V.tensor_scalar(qlat[:, t, :], qlat[:, t, :], rstd[:, 8 + t:9 + t], None, ALU.mult)
                ins.then_inc(lat_ready[l], 1)
                cos, sin = rope_t[:, :, 0, :], rope_t[:, :, 1, :]
                x1, x2 = kvlat[:, 0:2, KVR:KVR + 16], kvlat[:, 0:2, KVR + 16:KV_END]
                t1, t2, t3, t4 = rt1[:, :, 0, :], rt1[:, :, 1, :], rt1[:, :, 2, :], rt1[:, :, 3, :]
                V.tensor_tensor(t1, x1, cos, ALU.mult)
                V.tensor_tensor(t2, x2, sin, ALU.mult)
                V.tensor_tensor(t3, x2, cos, ALU.mult)
                V.tensor_copy(ropek[:, 2:4, :], kvlat[:, 2:4, KVR:KV_END])
                link(V.tensor_tensor(t4, x1, sin, ALU.mult))
                V.tensor_tensor(ropek[:, 0:2, 0:16], t1, t2, ALU.subtract)
                link(V.tensor_tensor(ropek[:, 0:2, 16:32], t3, t4, ALU.add))
                wait_full(dve, l, "kv", 0)
                for t in range(NTILE):
                    ins = V.tensor_copy(ktok[:, t, :, NOPE:QK], ropek[:, t:t + 1, :].to_broadcast([P, H, ROPE]))
                ins.then_inc(kpe_ready[l], 1)
                for f in range(4):
                    wait_full(dve, l, "u", f)
                    wait_emptied(dve, l, "c", f)
                    V.tensor_tensor(cT[:, f, 0:n_tok], bank(l, "u", f)[:, 0:n_tok], cT[:, f, 0:n_tok], ALU.mult)\
                        .then_inc(emptied["dve"], 1)
                    wait_emptied(dve, l, "u", f)
                    inner = cT[:, f, 0:n_tok].rearrange("p (s n) -> p s n", n=SEQ)
                    y = tmp2[:, f % 2, 0:n_tok].rearrange("p (s n) -> p s n", n=SEQ)
                    link(V.tensor_scalar(y, inner, convw[:, 1, f:f + 1], None, ALU.mult))
                    link(V.scalar_tensor_tensor(y[:, :, 1:SEQ], inner[:, :, 0:SEQ - 1], convw[:, 0, f:f + 1],
                                                y[:, :, 1:SEQ], ALU.mult, ALU.add))
                    link(V.scalar_tensor_tensor(y[:, :, 0:SEQ - 1], inner[:, :, 1:SEQ], convw[:, 2, f:f + 1],
                                                y[:, :, 0:SEQ - 1], ALU.mult, ALU.add))
                    wait_emptied(dve, l, "b", f)
                    V.tensor_tensor(bT[:, f, 0:n_tok], bT[:, f, 0:n_tok], tmp2[:, f % 2, 0:n_tok], ALU.mult).then_inc(conv_ready[l], 1)
                for c in range(2):
                    wait_full(dve, l, "ckvT", c)
                    V.tensor_scalar(ckvT[:, c, :], bank(l, "ckvT", c), gqk[:, c:c + 1], None, ALU.mult).then_inc(emptied["dve"], 1)
                for t in range(act):
                    for j in range(2):
                        wait_full(dve, l, "qup", t, j)
                        V.tensor_copy(qtok[:, t, 4 * j:4 * j + 4, :], bank(l, "qup", t, j)[:, 0:4 * QK].rearrange("p (h d) -> p h d", h=4))\
                            .then_inc(emptied["dve"], 1)
                wait_emptied(dve, l, "qup", act - 1, 1)
                for t in range(2):
                    q1, q2 = qtok[:, t, :, NOPE:NOPE + 16], qtok[:, t, :, NOPE + 16:QK]
                    c_ = rope_t[:, t, 0:1, :].to_broadcast([P, H, 16])
                    s_ = rope_t[:, t, 1:2, :].to_broadcast([P, H, 16])
                    a1, a2 = rt1[:, 0], rt1[:, 1]
                    b1, b2 = rt2[:, 0], rt2[:, 1]
                    V.tensor_tensor(a1, q1, c_, ALU.mult)
                    V.tensor_tensor(a2, q2, s_, ALU.mult)
                    V.tensor_tensor(b1, q2, c_, ALU.mult)
                    link(V.tensor_tensor(b2, q1, s_, ALU.mult))
                    V.tensor_tensor(q1, a1, a2, ALU.subtract)
                    ins = V.tensor_tensor(q2, b1, b2, ALU.add)
                    if t == 0:
                        link(ins)
                ins.then_inc(qrope_ready[l], 1)
                for f in range(FG):
                    wait_full(dve, l, "four2", f)
                    V.tensor_copy(fT[:, f, 0:n_tok], bank(l, "four2", f)[:, 0:n_tok]).then_inc(emptied["dve"], 1)
                units = attention_units(l)
                for u in range(len(units) + 1):
                    if u < len(units):
                        h, s = units[u]
                        keys = 512 if s == 0 else 256
                        if s == 0:
                            wait_full(dve, l, "kT", h)
                            V.tensor_copy(headT[0:QK, h % 2, 1, :], bank(l, "kT", h)[0:QK, :]).then_inc(emptied["dve"], 1)
                        for t in range(2):
                            c = 2 * (u % 2) + t
                            wait_full(dve, l, "S", h, s, t)
                            link(V.reduce_max(smax[:, c:c + 1], bank(l, "S", h, s, t)[:, 0:keys], AX))
                            V.tensor_scalar(nmax[:, c:c + 1], smax[:, c:c + 1], -ATT_SCALE, None, ALU.mult).then_inc(max_ready[l], 1)
                    if u >= 1:
                        h, s = units[u - 1]
                        nk = 4 if s == 0 else 2
                        wait_full(dve, l, "PT", h, s, 0)
                        V.tensor_copy(probsT[:, (u - 1) % 2, 0:nk, 0:P],
                                      bank(l, "PT", h, s, 0)[:, 0:P * nk].rearrange("p (k q) -> p k q", q=P)).then_inc(emptied["dve"], 1)
                        wait_full(dve, l, "O", h, s)
                        half = slice(VD * (h % 2), VD * (h % 2) + VD)
                        V.tensor_copy(oT[half, h // 2, SEQ * s:SEQ * s + SEQ], bank(l, "O", h, s)[half, 0:SEQ]).then_inc(emptied["dve"], 1)
                    if u < len(units):
                        h, s = units[u]
                        keys = 512 if s == 0 else 256
                        for t in range(2):
                            c = 2 * (u % 2) + t
                            wait_emptied(dve, l, "S", h, s, t)
                            link(V.reciprocal(sinv[:, c:c + 1], ssum[:, c:c + 1]))
                            V.tensor_scalar(probs[:, u % 2, t, 0:keys], probs[:, u % 2, t, 0:keys], sinv[:, c:c + 1], None,
                                            ALU.mult).then_inc(prob_ready[l], 1)
                for b in range(3):
                    for dc in range(KC):
                        n = b * KC + dc
                        wait_full(dve, l, "y", b, dc)
                        wait_emptied(dve, l, "g", b, dc)
                        if b == 0:
                            dst = mT[:, dc, 0:n_tok]
                        else:
                            m = n - KC
                            if m >= 2:
                                dve.wait_ge(merged[l], m - 1)
                            dst = ytmp[:, m % 2, 0:n_tok]
                        V.tensor_tensor(dst, bank(l, "y", b, dc)[:, 0:n_tok], tmp2[:, n % 2, 0:n_tok], ALU.mult)\
                            .then_inc(emptied["dve"], 1)
                for t in range(act):
                    c = 12 + 2 * t
                    dve.wait_ge(ssq_ready[l], counts["ssq"] + 2)
                    link(V.tensor_tensor(ssq[:, c:c + 1], ssq[:, c:c + 1], ssq[:, c + 1:c + 2], ALU.add))
                    mean_square(2, [(c, c + 1, DM)])
                    inverse_root(c, c + 1)
                    wait_emptied(dve, l, "out", t, 1)
                    link(V.scalar_tensor_tensor(rows[:, t % 2, :], rows[:, t % 2, :], rstd[:, c:c + 1], Grow[:, 0, t // 2, :],
                                                ALU.mult, ALU.mult))
                    V.tensor_tensor(xres[:, t, :], xres[:, t, :], rows[:, t % 2, :], ALU.add).then_inc(x_updated[l], 1)
                mean_square(act, [(0, act, DM)])
                inverse_root(0, act)
                for t in range(act):
                    V.tensor_scalar(xn[:, t, :], xres[:, t, :], rstd[:, t:t + 1], None, ALU.mult).then_inc(xn_ready[l], 1)
                modulate(2)
                wait_emptied(dve, l, "rt", act - 1)
                sc, bi, mk, oh = score[:, 0:act], biased[:, 0:act], mask[:, 0:act], onehot[:, 0:act]
                tmp = oh_tmp[:, 0:act]
                link(V.tensor_tensor(bi, sc, brow.rearrange("p (a e) -> p a e", a=1).to_broadcast([P, act, NE]), ALU.add))
                for t in range(act):
                    link(V.max(m8[:, t, :], biased[:, t, :]))
                    link(V.max_index(idx8[:, t, :], m8[:, t, :], biased[:, t, :]))
                link(V.tensor_copy(idxf[:, 0:act, :], idx8[:, 0:act, :]))
                for t in range(act):
                    ins = V.tensor_tensor(oh[:, t], iota[:, 0:NE].rearrange("p (a e) -> p a e", a=1).to_broadcast([P, TOPK, NE]),
                                          idxf[:, t, 0:TOPK].rearrange("p (k a) -> p k a", a=1).to_broadcast([P, TOPK, NE]),
                                          ALU.is_equal)
                link(ins)
                V.tensor_reduce(mk, oh.rearrange("p t k e -> p t e k"), AX, ALU.add).then_inc(mask_ready[l], 1)

                def pick(dst, table):
                    for t in range(act):
                        ins = V.tensor_tensor(tmp[:, t], oh[:, t], table[:, t:t + 1, :].to_broadcast([P, TOPK, NE]), ALU.mult)
                    link(ins)
                    link(V.tensor_reduce(dst, tmp, AX, ALU.add))

                dve.wait_ge(ssq_ready[l], counts["ssq"])
                pick(pick_w[:, 0:act], score)
                link(V.tensor_reduce(rden[:, 0:act], pick_w[:, 0:act], AX, ALU.add))
                link(V.reciprocal(rden[:, 0:act], rden[:, 0:act]))
                for t in range(act):
                    V.tensor_scalar(pick_w[:, t, :], pick_w[:, t, :], rden[:, t:t + 1], ROUTED_SCALE, ALU.mult, ALU.mult)
                wait_full(dve, l, "rank")
                ranks = bank(l, "rank")
                V.tensor_tensor(needed, ranks[:, P:P + 1], item_t[:, l:l + 1], ALU.is_gt).then_inc(needed_ready[l], 1)
                V.scalar_tensor_tensor(place[:, 0:act], ranks[:, 0:NE * act].rearrange("p (t e) -> p t e", e=NE), float(NE),
                                       iota[:, 0:NE].rearrange("p (a e) -> p a e", a=1).to_broadcast([P, act, NE]),
                                       ALU.mult, ALU.add).then_inc(emptied["dve"], 1)
                wait_emptied(dve, l, "rank")
                pick(pos[:, 0:act], place)
                V.tensor_copy(posu[:, 0:act], pos[:, 0:act]).then_inc(pos_ready[l], 1)
                wait_full(dve, l, "turn")
                turns = bank(l, "turn")
                V.tensor_scalar(turn, iota, turns[:, 0:1], needed, ALU.is_equal, ALU.mult).then_inc(turn_ready[l], 1)
                link(V.tensor_scalar(over[0:1, :], item_t[0:1, 4:8], turns[0:1, 1:2], None, ALU.is_lt))
                link(V.tensor_reduce(more_f[0:1, :], over[0:1, :], AX, ALU.add))
                V.tensor_copy(more_u[0:1, :], more_f[0:1, :]).then_inc(emptied["dve"], 1)
                wait_full(dve, l, "items")
                V.tensor_scalar(item_col, bank(l, "items")[0:1, 0:MAX_ITEMS], float(P), None, ALU.add)
                V.tensor_copy(item_expert, bank(l, "items")[0:1, MAX_ITEMS:2 * MAX_ITEMS]).then_inc(emptied["dve"], 1)
                for f in range(2):
                    dve.wait_ge(ssilu_ready[l], f + 1)
                    V.tensor_tensor(act_s[:, f, 0:n_tok], ps[:, 512 * (2 + f):512 * (2 + f) + n_tok], silu_s[:, f, 0:n_tok], ALU.mult)\
                        .then_inc(sact_ready[l], 1)
                for g in range(2 * act):
                    b = 4 + g % 4
                    dve.wait_ge(sdn_full[l], g + 1)
                    V.tensor_copy(acc[:, g // 2, 512 * (g % 2):512 * (g % 2) + 512], ps[:, 512 * b:512 * b + 512])\
                        .then_inc(sdn_taken[l], 1)
                split = P // CAP[l]
                dve.wait_ge(table_read[l], 16 * split + 16)
                ins = V.tensor_scalar(row_g, row_y, 2, None, ALU.logical_shift_right)
                if split == 2:
                    link(ins)
                    link(V.tensor_scalar(row_g, row_g, 2.0, half_id, ALU.mult, ALU.add))
                    ins = V.tensor_scalar(row_y, row_y, 2.0, half_id, ALU.mult, ALU.add)
                ins.then_inc(rows_ready[l], 1)
                more = V.value_load(more_u[0:1, 0:1], min_val=0, max_val=4)
                half = wide[l] // 2
                fw = CAP[l] * 2

                def take_x(u, b, n=None):
                    dve.wait_ge(xt_full[l], 4 * b + u + 1)
                    if n is None or n >= 2:
                        dve.wait_ge(gu_full[l], 4 * b + u - 1)
                    V.tensor_copy(xT[u % 2][:, half:2 * half], ps[:, 1536:1536 + half]).then_inc(xt_dve[l], 1)

                def take_aT(u, b, n=None):
                    dve.wait_ge(at_full[l], 4 * b + u + 1)
                    if n is None or n >= 2:
                        dve.wait_ge(y_full[l], 4 * b + u - 1)
                    V.tensor_copy(aT_e[u % 2][:, 0:fw], ps[:, 2048:2048 + fw]).then_inc(at_ready[l], 1)

                def activate(u, b, n=None):
                    dve.wait_ge(silu_ready[l], 4 * b + u + 1)
                    if n is None or n >= 2:
                        dve.wait_ge(at_full[l], 4 * b + u - 1)
                    o = 512 * (u % 2) + fw
                    V.tensor_tensor(a_e[u % 2][:, 0:fw], ps[:, o:o + fw], silu_e[u % 2][:, 0:fw], ALU.mult).then_inc(a_ready[l], 1)

                def take_y(u, b, n=None):
                    if CAP[l] == P:
                        dve.wait_ge(y_full[l], 4 * b + u + 1)
                        if n is None or n >= 2:
                            dve.wait_ge(y_stored[l][(u - 2) % 4], 16 * b + (16 if u >= 2 else 0))
                        V.tensor_copy(y_e[u % 2][:, 512:1024], ps[:, 3072:3584]).then_inc(y_dve[l], 1)

                for n in range(UNROLL):
                    take_x(n, 0, n)
                    if n >= 2:
                        take_aT(n - 2, 0, n - 2)
                    if n >= 1:
                        activate(n - 1, 0, n - 1)
                    if n >= 2:
                        take_y(n - 2, 0, n - 2)
                with nc.vector.Fori(1, more + BLOCKS) as b:
                    for u in range(UNROLL):
                        take_x(u, b)
                        take_aT((u - 2) % 4, b - (u < 2))
                        activate((u - 1) % 4, b - (u < 1))
                        take_y((u - 2) % 4, b - (u < 2))
                last = more + (BLOCKS - 1)
                take_aT(2, last)
                activate(3, last)
                take_y(2, last)
                take_aT(3, last)
                take_y(3, last)
                for t in range(act):
                    dve.wait_ge(picked_loaded[t % 2][l], 16 * (t // 2 + 1))
                    dve.wait_ge(sdn_taken[l], 2 * t + 2)
                    rowsk = picked[t % 2].rearrange("p (k d) -> p k d", k=TOPK)
                    for k in range(TOPK):
                        ins = V.scalar_tensor_tensor(acc[:, t, :], rowsk[:, k, :], pick_w[:, t, k:k + 1], acc[:, t, :], ALU.mult, ALU.add)
                        if k < TOPK - 1:
                            link(ins)
                    ins.then_inc(combined[l], 1)
                mean_square(act, [(0, act, DM)])
                inverse_root(0, act)
                dve.wait_ge(combined[l], act)
                for t in range(act):
                    link(V.scalar_tensor_tensor(acc[:, t, :], acc[:, t, :], rstd[:, t:t + 1], Grow[:, 1, t // 2, :],
                                                ALU.mult, ALU.mult))
                    V.tensor_tensor(xres[:, t, :], xres[:, t, :], acc[:, t, :], ALU.add).then_inc(x_updated[l], 1)


_INS = ["x", "c", "ctx", "c_ctx", "w_ada", "b_ada", "g_pre_mix", "g_post_mix", "g_pre_ffn", "g_post_ffn", "w_in",
        "b_gate", "g_q", "w_uq", "g_kv", "w_ukv", "w_mla_out", "conv_w", "w_conv_out", "w_four_out", "w_out",
        "w_router", "b_router", "w_gate_e", "w_up_e", "w_down_e", "w_gate_s", "w_up_s", "w_down_s"]


def shape_tables():
    pos = np.arange(SEQ)
    pairs = ROPE // 4
    inv = (ROPE_BASE ** (-np.arange(pairs, dtype=np.float32) / pairs)).astype(np.float32)
    ang = np.concatenate([(pos // GRID_W)[:, None].astype(np.float32) * inv,
                          (pos % GRID_W)[:, None].astype(np.float32) * inv], axis=1).astype(np.float64)
    rope = np.stack([np.cos(ang), np.sin(ang)], axis=1).reshape(2, P, 2, ROPE // 2).transpose(1, 0, 2, 3)
    a = 2 * np.pi * (np.outer(np.arange(FC), np.arange(FC)) % FC) / FC
    chan = np.concatenate([np.cos(a), np.sin(a)], axis=1) / np.sqrt(FC)
    b = 2 * np.pi * (np.outer(pos, pos) % SEQ) / SEQ
    seq = (np.stack([np.cos(b), -np.sin(b)]) / np.sqrt(SEQ)).reshape(2, 2, P, SEQ).transpose(2, 0, 1, 3).reshape(P, 1024)
    return {"ident": np.eye(P, dtype=np.float32),
            "tri": np.concatenate([np.ones((P, P)), np.triu(np.ones((P, P)), 1)], axis=1).astype(np.float32),
            "pick_id": (TOPK * (P * np.arange(NTILE)[None, :, None] + np.arange(P)[:, None, None])
                        + np.arange(TOPK)[None, None, :]).astype(np.uint32),
            "item_t": item_tables(),
            "half_id": (np.arange(P)[:, None] // (P // 2)).astype(np.float32),
            "absent": np.full((P * NTILE * NE, 1), ABSENT, dtype=np.uint32),
            "iota": np.tile(np.arange(MAX_ITEMS, dtype=np.float32), (P, 1)),
            "rope": np.ascontiguousarray(rope, dtype=np.float32),
            "dft": np.ascontiguousarray(np.concatenate([chan, seq], axis=1), dtype=np.float32)}


def item_tables():
    column = np.arange(P)
    t = np.zeros((P, 8), dtype=np.float32)
    for l in range(DEPTH):
        t[:, l] = np.where(column < NE, -1, column // NE * CAP[l])
    t[:, 2], t[:, 3] = column - P, column % NE
    t[:, 4:8] = NE + UNROLL * np.arange(4)
    return t


def kernel(**inputs):
    import concourse.bacc as _bacc
    from concourse.bass_utils import run_bass_kernel_spmd as _run

    nc = _bacc.Bacc("TRN2", target_bir_lowering=False, num_devices=1)
    arrays, I, C = {}, {}, {}
    for group, into in (({n: inputs[n] for n in _INS}, I), (shape_tables(), C)):
        for name, a in group.items():
            a = np.ascontiguousarray(a)
            arrays[f"in_{name}"] = a
            into[name] = nc.dram_tensor(f"in_{name}", a.shape, mybir.dt.from_np(a.dtype), kind="ExternalInput").ap()
    out = nc.dram_tensor("out_0", (1, SEQ, DM), mybir.dt.float32, kind="ExternalOutput").ap()
    hybrid_layers(nc, I, C, out)
    r = _run(nc, [arrays], core_ids=[0])
    return r.results[0]["out_0"]
```

```python
import numpy as np
import concourse.bass as bass
from concourse import mybir
from concourse.alu_op_type import AluOpType as ALU
from contextlib import ExitStack

DM, DEPTH, GRID_W = 1024, 2, 64
H, NOPE, ROPE, VD = 8, 64, 32, 64
QK = NOPE + ROPE
QR, KVR = 384, 256
CONV = 512
FG, FC = 4, 128
NE, TOPK, FE = 32, 4, 256
ROUTED_SCALE, EPS = 2.5, 1e-6
ROPE_BASE = 10000.0
P = 128
KC = DM // P
NTILE = 4
SEQ = 256
KV_END = KVR + ROPE
Q_END = KV_END + QR
FOUR_END = Q_END + 3 * CONV + FG * FC
SLOTS = 4
BANKS = 8
ATT_SCALE = QK ** -0.5
ACTIVE = [NTILE, 2]
CAP = [P, P // 2]
ROUNDS = 4
ADA_CHUNKS = 12
MAX_ITEMS = 48
UNROLL = 4
BLOCKS = NE // UNROLL
SMALL = 536
VECTORS = [12, 8]
ABSENT = 65535


class Groups:

    def __init__(self):
        self.at, self.count, self.emptied_at = {}, {"act": 0, "dve": 0}, []

    def add(self, owner, *key):
        self.at[key] = len(self.emptied_at)
        self.count[owner] += 1
        self.emptied_at.append((owner, self.count[owner]))


def attention_units(l):
    return [(h, s) for h in range(H) for s in range(ACTIVE[l] // 2)]


def attention_steps(l):
    units = attention_units(l)
    steps = [("T", 0)]
    for u in range(len(units) + 2):
        if u < len(units):
            steps.append(("S", u))
        if u + 1 < len(units) and units[u + 1][1] == 0:
            steps.append(("T", u + 1))
        if 1 <= u <= len(units):
            steps.append(("PT", u - 1))
        if u >= 2:
            steps.append(("O", u - 2))
    return steps


def chunk_after(l, name, n):
    starts = {"kv": 4, "q": 8, "b": 12, "c": 16, "u": 20}
    return starts[name] + n if l == 0 and name in starts else None


def is_gate(c):
    return c in (4, 5, 10, 11)


def picks(a):
    lc, c = divmod(a, ADA_CHUNKS)
    return [("pick", a, s) for s in range(ACTIVE[lc] // 2 if is_gate(c) else 1)]


def plan():
    g = Groups()
    alternate = lambda k: "act" if k % 2 else "dve"
    for l in range(DEPTH):
        act = ACTIVE[l]

        def chunk_step(a):
            if a not in (0, 4):
                for key in picks(a - 1):
                    g.add("dve", *key)
            g.add("dve", "ada", a)

        if l == 0:
            for a in range(4):
                chunk_step(a)
            for key in picks(3):
                g.add("dve", *key)
        for k in range(KC):
            g.add(alternate(k), l, "h", 1, k)
        for name, owner, count in (("kv", "act", NTILE), ("q", "act", act), ("b", "act", 4), ("c", "act", 4),
                                   ("u", "dve", 4), ("f", "act", 4)):
            for n in range(count):
                g.add(owner, l, name, n)
                if chunk_after(l, name, n) is not None:
                    chunk_step(chunk_after(l, name, n))
        if l == 0:
            for key in picks(2 * ADA_CHUNKS - 1):
                g.add("dve", *key)
        for c in range(2):
            g.add("dve", l, "ckvT", c)
        for c in range(3):
            g.add("act", l, "cqT", c)
        for t in range(NTILE):
            for j in range(2):
                g.add("act", l, "kvup", t, j)
        for t in range(act):
            for j in range(2):
                g.add("dve", l, "qup", t, j)
        for f in range(FG):
            for s in range(act // 2):
                g.add("act", l, "four1", f, s)
        for f in range(FG):
            g.add("dve", l, "four2", f)
        for kind, u in attention_steps(l):
            h, s = attention_units(l)[u]
            if kind == "T":
                g.add("dve", l, "kT", h)
                g.add("act", l, "qT", h)
            elif kind == "O":
                g.add("dve", l, "O", h, s)
            else:
                for t in range(2):
                    g.add("act" if kind == "S" else alternate(t), l, kind, h, s, t)
        for b in range(3):
            for dc in range(KC):
                g.add("act", l, "g", b, dc)
                g.add("dve", l, "y", b, dc)
        for t in range(act):
            for j in range(2):
                g.add("act", l, "out", t, j)
        for k in range(KC):
            g.add(alternate(k), l, "h", 2, k)
        for t in range(act):
            g.add("act", l, "rt", t)
        for t in range(act):
            for j in range(2):
                g.add("act", l, "hrow", t, j)
        for name in ("rank", "turn", "items"):
            g.add("dve", l, name)
    return g


def hybrid_layers(nc, I, C, out):
    f32, f32r, u32 = mybir.dt.float32, mybir.dt.float32r, mybir.dt.uint32
    ACT, AX = mybir.ActivationFunctionType, mybir.AxisListType.X
    G = plan()
    ctx = ExitStack()

    def sb(name, shape, dt=f32):
        return ctx.enter_context(nc.sbuf_tensor(name, shape, dt))

    def sb_over(name, shape, first, views):
        with ExitStack() as lent:
            if first:
                lent.enter_context(nc.sbuf_tensor(name + "_skip", [P, first], f32))
            under = [lent.enter_context(nc.sbuf_tensor(n, size, f32r)) for n, size in views]
        return (sb(name, shape), *under)

    def one(name):
        return ctx.enter_context(nc.semaphore(name))

    def by_layer(name):
        return [one(f"{name}_{l}") for l in range(DEPTH)]

    with ctx:
        xres = sb("xres", [P, NTILE, DM])
        hT, h_lo = sb_over("hT", [P, KC, NTILE * P], 0, [("h_lo", [P, KC, NTILE * P])])
        ring, ring_lo = sb_over("ring", [P, SLOTS, 4096], 0, [("ring_lo", [P, SLOTS, 4096])])
        bT, bT_lo = sb_over("bT", [P, 4, 512], 0, [("bT_lo", [P, 4, 512])])
        cT, br_hi = sb_over("cT", [P, 4, 512], 0, [("br_hi", [P, 4, 512])])
        fT, fT_lo = sb_over("fT", [P, 4, 512], 0, [("fT_lo", [P, 4, 512])])
        tmp2 = sb("tmp2", [P, 2, 512])
        qkv, m_lo, h_hi = sb_over("qkv", [P, 8192], 0, [("m_lo", [P, KC, 512]), ("h_hi", [P, KC, NTILE * P])])
        head, v_hi, v_lo = sb_over("head", [P, 2048], 1024, [("v_hi", [P, 4, P]), ("v_lo", [P, 4, P])])
        probs_b, w_hi = sb_over("probs_b", [P, 2048], 0, [("w_hi", [P, 2, KC, P])])
        probsT_b, w_lo = sb_over("probsT_b", [P, 2048], 0, [("w_lo", [P, 2, KC, P])])
        oT_b, oT_lo = sb_over("oT_b", [P, 2048], 0, [("oT_lo", [P, 4, 512])])
        Grow = sb("Grow", [P, 2, 2, DM])
        ident = sb("ident", [P, P])
        rope_t = sb("rope_t", [P, 2, 2, 16])
        wr = sb("wr", [P, KC, NE])
        small = sb("small", [P, SMALL])
        used = [0]

        def part(n):
            used[0] += n
            assert used[0] <= SMALL
            return small[:, used[0] - n:used[0]]

        cs = part(16).rearrange("p (s k) -> p s k", s=2)
        gains = part(32).rearrange("p (l n k) -> p l n k", n=2, k=KC)
        streams = [[2, ACTIVE[l] // 2] for l in range(DEPTH)]
        scaleT, shiftT = ([[part(KC * n).rearrange("p (s k) -> p s k", k=KC) for n in streams[l]] for l in range(DEPTH)]
                          for _ in range(2))
        gqk = part(5)
        convw = part(12).rearrange("p (j f) -> p j f", j=3)
        bgate = part(24).rearrange("p (b k) -> p b k", b=3)
        ssq = part(24)
        rstd = part(24)
        brow = part(NE)
        iota = part(MAX_ITEMS)
        smax, nmax, ssum, sinv = part(4), part(4), part(4), part(4)
        rden = part(4)
        m8 = part(32).rearrange("p (t k) -> p t k", k=8)
        idx8 = part(32).bitcast(u32).rearrange("p (t k) -> p t k", k=8)
        idxf = part(32).rearrange("p (t k) -> p t k", k=8)
        pick_w = part(16).rearrange("p (t k) -> p t k", k=TOPK)
        pos = part(16).rearrange("p (t k) -> p t k", k=TOPK)
        posu = part(16).bitcast(u32).rearrange("p (t k) -> p t k", k=TOPK)
        pick_id = part(16).bitcast(u32).rearrange("p (t k) -> p t k", k=TOPK)
        item_t = part(10)
        sel = item_t[:, 8:10]
        needed, over = part(1), part(4)
        half_id = part(1)
        held = part(1)
        more_f, more_u = part(1), part(1).bitcast(u32)
        now_g, now_y = part(4).bitcast(u32), part(4).bitcast(u32)

        ca32 = oT_b[:, 1536:1792].rearrange("p (k c) -> p k c", c=32)
        stage = qkv[:, 1024:3072].rearrange("p (a c) -> p a c", c=512)
        grow_next = qkv[0:1, 6144:8192].rearrange("p (n d) -> p n d", n=2)
        dft_c = head[:, 0:256]
        dft_n = head[:, 256:1280].rearrange("p (a c n) -> p a c n", a=2, c=2)
        ropek = head[:, 1280:1408].rearrange("p (t d) -> p t d", t=NTILE)
        rt1 = head[:, 1408:1664].rearrange("p (t h d) -> p t h d", t=2, h=H)
        rt2 = head[:, 1664:1920].rearrange("p (t h d) -> p t h d", t=2, h=H)
        kvlat = probs_b[:, 0:4 * KV_END].rearrange("p (t c) -> p t c", t=4)
        qlat = probsT_b[:, 0:4 * QR].rearrange("p (t c) -> p t c", t=4)
        ckvT = qkv[:, 0:1024].rearrange("p (c t) -> p c t", c=2)
        cqT = oT_b[:, 0:1536].rearrange("p (c t) -> p c t", c=3)
        four_ab = [b[:, 512 * i:512 * i + 512] for b in (probs_b, probsT_b) for i in range(4)]
        qtok = qkv[:, 0:3072].rearrange("p (t h d) -> p t h d", t=4, h=H)
        ktok = qkv[:, 3072:6144].rearrange("p (t h d) -> p t h d", t=4, h=H)
        vtok = qkv[:, 6144:8192].rearrange("p (t h d) -> p t h d", t=4, h=H)
        headT = head[:, :].rearrange("p (b a t) -> p b a t", b=2, a=2)
        probs = probs_b[:, :].rearrange("p (b t k) -> p b t k", b=2, t=2)
        probsT = probsT_b[:, :].rearrange("p (b k t) -> p b k t", b=2, k=4)
        oT = oT_b[:, :].rearrange("p (c t) -> p c t", c=4)
        xn = qkv[:, 4096:8192].rearrange("p (t d) -> p t d", t=NTILE)
        mT = qkv[:, 0:4096].rearrange("p (k t) -> p k t", k=KC)
        ytmp = head[:, 0:1024].rearrange("p (b t) -> p b t", b=2)
        rows = oT_b[:, :].rearrange("p (n d) -> p n d", n=2)
        junk = tmp2[:, :, :].rearrange("p a b -> p (a b)")
        route = bT[:, 2:4, :].rearrange("p a b -> p (a b)")
        cols = lambda a, b: route[:, a:b].rearrange("p (t e) -> p t e", e=NE)
        score, biased, mask = cols(0, 128), cols(128, 256), cols(256, 384)
        onehot = route[:, 384:896].rearrange("p (t k e) -> p t k e", t=NTILE, k=TOPK)
        tri = qkv[:, 0:256]
        oh_tmp = tmp2[:, 0, :].rearrange("p (t k e) -> p t k e", t=NTILE, k=TOPK)
        turn = qkv[:, 384:384 + MAX_ITEMS]
        place = qkv[:, 256:384].rearrange("p (t e) -> p t e", e=NE)
        silu_s, act_s = tmp2, bT[:, 0:2, :]
        dn_s = head[:, :].rearrange("p (k n) -> p k n", k=2)
        acc = qkv[:, 0:4096].rearrange("p (t d) -> p t d", t=NTILE)
        hrow = [(probs_b if t < 2 else probsT_b)[:, DM * (t % 2):DM * (t % 2) + DM] for t in range(NTILE)]
        tab = wr[:, :, :].rearrange("p k e -> p (k e)").bitcast(u32)
        row_y = tab[:, 0:P + 1]
        row_g = [head[:, 1536:1537 + P].bitcast(u32), oT_b[:, 512:513 + P].bitcast(u32)]
        item_col, item_expert = tab[0:1, 136:136 + MAX_ITEMS], tab[0:1, 184:184 + MAX_ITEMS]
        wide = [DM, DM // 2]
        xg = [(probs_b if u < 2 else probsT_b)[:, DM * (u % 2):DM * (u % 2) + DM] for u in range(4)]
        xT = [oT_b[:, DM * j:DM * j + DM] for j in range(2)]
        silu_e = [head[:, 256 * j:256 * j + 256] for j in range(2)]
        a_e = [head[:, 512 + 256 * j:768 + 256 * j] for j in range(2)]
        aT_e = [head[:, 1024 + 256 * j:1280 + 256 * j] for j in range(2)]
        y_e = [bT[:, 2 * j:2 * j + 2, :].rearrange("p a b -> p (a b)") for j in range(2)]
        gu = [ring[:, u, :].rearrange("p (k n) -> p k n", k=KC) for u in range(UNROLL)]
        dn = [w.rearrange("p (k n) -> p k n", k=2) for w in
              (cT[:, :, :].rearrange("p a b -> p (a b)"), fT[:, :, :].rearrange("p a b -> p (a b)"),
               qkv[:, 4096:6144], qkv[:, 6144:8192])]
        picked = [hT[:, :, :].rearrange("p a b -> p (a b)"), qkv[:, 4096:8192]]
        scratch = lambda name, shape, dt: [nc.dram_tensor(f"{name}_{l}", shape(l), dt, kind="Internal").ap()
                                           for l in range(DEPTH)]
        grow_d = nc.dram_tensor("grow_next", (1, 2 * DM), f32, kind="Internal").ap()
        h_rows = scratch("h_rows", lambda l: (P * ACTIVE[l], DM), f32)
        slots_d = scratch("slot_table", lambda l: (P * ACTIVE[l] * NE, 1), u32)
        y_rows = scratch("y_rows", lambda l: (P * ACTIVE[l] * TOPK, DM), f32)
        ps = ctx.enter_context(nc.psum_tensor("ps", [P, BANKS * 512], f32))

        psum_full = one("psum_full")
        emptied = {"act": one("emptied_by_act"), "dve": one("emptied_by_dve")}
        x_loaded, consts_loaded, out_stored = one("x_loaded"), one("consts_loaded"), one("out_stored")
        slot_loaded = [one(f"slot_loaded_{i}") for i in range(SLOTS)]
        by_buffer = lambda name: [[one(f"{name}_{l}_{u}") for u in range(UNROLL)] for l in range(DEPTH)]
        gu_loaded, dn_loaded = by_buffer("gu_loaded"), by_buffer("dn_loaded")
        x_gathered, y_stored = by_buffer("x_gathered"), by_buffer("y_stored")
        params_loaded = by_layer("params_loaded")
        dft_loaded = by_layer("dft_loaded")
        cond_loaded = one("cond_loaded")
        gains_loaded = one("gains_loaded")
        zeroed = one("zeroed")
        ca_ready = one("ca_ready")
        gpost_loaded = one("gpost_loaded")
        grow_stored, grow_loaded = one("grow_stored"), one("grow_loaded")
        ssq_ready = by_layer("ssq_ready")
        ms_ready = by_layer("ms_ready")
        root_ready = by_layer("root_ready")
        xn_ready = by_layer("xn_ready")
        lat_ready = by_layer("lat_ready")
        conv_ready = by_layer("conv_ready")
        kpe_ready = by_layer("kpe_ready")
        qrope_ready = by_layer("qrope_ready")
        max_ready = by_layer("max_ready")
        prob_ready = by_layer("prob_ready")
        h_hi_ready, h_lo_ready = by_layer("h_hi_ready"), by_layer("h_lo_ready")
        w_hi_ready, w_lo_ready = by_layer("w_hi_ready"), by_layer("w_lo_ready")
        br_hi_ready, br_lo_ready = by_layer("br_hi_ready"), by_layer("br_lo_ready")
        v_hi_ready, v_lo_ready = by_layer("v_hi_ready"), by_layer("v_lo_ready")
        merged = by_layer("merged")
        x_updated = by_layer("x_updated")
        mask_ready = by_layer("mask_ready")
        tri_loaded = by_layer("tri_loaded")
        table_clear = by_layer("table_clear")
        pos_ready = by_layer("pos_ready")
        needed_ready = by_layer("needed_ready")
        turn_ready = by_layer("turn_ready")
        table_filled = by_layer("table_filled")
        table_read = by_layer("table_read")
        rows_ready = by_layer("rows_ready")
        now_ready = by_layer("now_ready")
        h_stored = by_layer("h_stored")
        sgu_full = by_layer("sgu_full")
        ssilu_ready = by_layer("ssilu_ready")
        sact_ready = by_layer("sact_ready")
        sdn_loaded = by_layer("sdn_loaded")
        sdn_full = by_layer("sdn_full")
        sdn_taken = by_layer("sdn_taken")
        xt_full = by_layer("xt_full")
        gu_full = by_layer("gu_full")
        at_full = by_layer("at_full")
        y_full = by_layer("y_full")
        xt_act, xt_dve = by_layer("xt_act"), by_layer("xt_dve")
        silu_ready = by_layer("silu_ready")
        a_ready = by_layer("a_ready")
        at_ready = by_layer("at_ready")
        y_act, y_dve = by_layer("y_act"), by_layer("y_dve")
        picked_loaded = [by_layer(f"picked_loaded_{i}") for i in range(2)]
        combined = by_layer("combined")
        held_set, dve_step = one("held_set"), one("dve_step")

        def wait_full(eng, *key):
            eng.wait_ge(psum_full, G.at[key] + 1)

        def wait_emptied(eng, *key):
            owner, n = G.emptied_at[G.at[key]]
            eng.wait_ge(emptied[owner], n)

        def bank(*key):
            b = G.at[key] % BANKS
            return ps[:, 512 * b:512 * b + 512]

        stream = []
        item_at, last_reader, loads, before = {}, [], [], []
        held_by, dmas = [None] * SLOTS, [0] * SLOTS

        def item(slot, reader, key, chunks, src, count=1):
            before.append(held_by[slot])
            item_at[key] = held_by[slot] = len(stream)
            dmas[slot] += count
            loads.append(dmas[slot])
            stream.append((key, chunks, src.shape[2] if src else 512, src, slot))
            last_reader.append(reader)

        def ada_item(slot, a):
            lc, c = divmod(a, ADA_CHUNKS)
            item(slot, ("ada", a), ("ada", a), KC, at(I["w_ada"][lc], 512 * c, 512 * c + 512), count=2)

        first_item, last_held = [], []
        for l in range(DEPTH):
            at = lambda w, k0, k1: w.rearrange("(k p) n -> p k n", p=P)[:, :, k0:k1]
            last = ACTIVE[l] - 1
            first_item.append(len(stream))
            w_in = I["w_in"][l]
            part_of = {"kv": (NTILE - 1, 0, KV_END), "q": (last, KV_END, Q_END)}
            part_of.update({name: (3, Q_END + CONV * n, Q_END + CONV * (n + 1)) for n, name in enumerate("bcuf")})

            def in_item(slot, name):
                n, c0, c1 = part_of[name]
                item(slot, (l, name, n), (l, name), KC, at(w_in, c0, c1))

            if l == 0:
                for a in range(4):
                    ada_item(a, a)
                in_item(0, "kv")
                in_item(1, "q")
                for a in range(4, 2 * ADA_CHUNKS):
                    ada_item(2 + a % 2, a)
                    if a in (8, 12, 16, 20):
                        n = a // 4 - 2
                        in_item(n % 2, "bcuf"[n])
            else:
                for n, name in enumerate(("kv", "q", "b", "c", "u", "f")):
                    in_item(n % SLOTS, name)
            item(2, (l, "kvup", NTILE - 1, 1), (l, "ukv"), 2, at(I["w_ukv"][l], 0, 1024))
            item(3, (l, "qup", last, 1), (l, "uq"), 3, at(I["w_uq"][l], 0, 768))
            branches = [(0, "w_mla_out"), (3, "w_conv_out"), (0, "w_four_out")]

            def branch_item(b):
                n, name = branches[b]
                item(n, (l, "y", b, KC - 1), (l, "branch", b), 4, at(I[name][l], 0, DM))

            branch_item(0)
            for b in range(3):
                for j in range(2):
                    c0 = FOUR_END + b * DM + 512 * j
                    item(1 + j, (l, "g", b, 4 * j + 3), (l, "gate", b, j), KC, at(w_in, c0, c0 + 512))
                if b < 2:
                    branch_item(b + 1)
            for j, n in ((0, 3), (1, 1)):
                item(n, (l, "out", last, 1), (l, "out", j), KC, at(I["w_out"][l], 512 * j, 512 * j + 512))
            last_held.append([held_by[slot] for slot in range(SLOTS)])
            item(SLOTS - 1, None, (l, "shared"), KC, None, count=2)
        first_item.append(len(stream))
        assert SLOTS == UNROLL

        def slot(*key):
            _, k, cols, _, n = stream[item_at[key]]
            return ring[:, n, 0:k * cols].rearrange("p (k n) -> p k n", k=k)

        def wait_arrived(eng, *key):
            n = item_at[key]
            eng.wait_ge(slot_loaded[stream[n][4]], 16 * loads[n])
            return slot(*key)

        def gate_columns(eng, l, n):
            b, dc = divmod(n, KC)
            return wait_arrived(eng, l, "gate", b, dc // 4)[:, :, P * (dc % 4):P * (dc % 4) + P]

        def branch_columns(eng, l, n):
            b, dc = divmod(n, KC)
            return wait_arrived(eng, l, "branch", b)[:, :, P * dc:P * dc + P]

        def out_weights(l, j, k):
            n = stream[item_at[(l, "out", j)]][4]
            flat = lambda w: w[:, :, :, :].rearrange("p a k n -> p (a k n)")[:, 512 * (k % 4):512 * (k % 4) + 512]
            high = h_lo[:, k, :] if j else flat(w_hi if k < 4 else w_lo)
            return slot(l, "out", j)[:, k, :], high, ring_lo[:, n, 512 * k:512 * k + 512]

        block = ctx.enter_context(nc.Block())

        @block.sync
        def _(sp):
            rows_of = lambda a: a.rearrange("(t p) d -> p t d", p=P)
            sp.dma_start(xres[:, 0:2, :], rows_of(I["x"][0])).then_inc(x_loaded, 16)
            sp.dma_start(xres[:, 2:4, :], rows_of(I["ctx"][0])).then_inc(x_loaded, 16)
            more = None
            for l in range(DEPTH):
                act = ACTIVE[l]
                for n in range(first_item[l], item_at[(l, "shared")]):
                    key, _, _, src, at_slot = stream[n]
                    m = n - first_item[l]
                    if l and m < SLOTS:
                        sp.wait_ge(gu_full[l - 1], more * UNROLL + (NE - SLOTS + 1 + m))
                    elif before[n] is not None:
                        wait_full(sp, *last_reader[before[n]])
                    sp.dma_start(slot(*key), src).then_inc(slot_loaded[at_slot], 16)
                    if key[0] == "ada":
                        lc, c = divmod(key[1], ADA_CHUNKS)
                        if key[1] < 4:
                            sp.wait_ge(zeroed, 2)
                        else:
                            wait_full(sp, *picks(key[1] - 4)[-1])
                        sp.dma_start(stage[2:3, key[1] % 4, :], I["b_ada"][lc:lc + 1, 512 * c:512 * c + 512])\
                            .then_inc(slot_loaded[at_slot], 16)

                def load_gate_up(u, b, e, first=False):
                    if not first:
                        sp.wait_ge(gu_full[l], 4 * b + u - 3)
                    elif u < 3:
                        wait_full(sp, *last_reader[last_held[l][u]])
                    else:
                        sp.wait_ge(sgu_full[l], 2)
                    src = lambda w: w[l][bass.ds(e, 1)].rearrange("a (p k) n -> p (a k) n", k=KC)
                    sp.dma_start(gu[u][:, :, 0:FE], src(I["w_gate_e"])).then_inc(gu_loaded[l][u], 16)
                    sp.dma_start(gu[u][:, :, FE:2 * FE], src(I["w_up_e"])).then_inc(gu_loaded[l][u], 16)

                def load_down(u, b, e, first=False):
                    if not first:
                        sp.wait_ge(y_full[l], 4 * b + u - 3)
                    elif u < 2:
                        wait_full(sp, l, "y", 2, KC - 1)
                    else:
                        wait_full(sp, l, "h", 2, KC - 1)
                    sp.dma_start(dn[u], I["w_down_e"][l][bass.ds(e, 1)].rearrange("a (k p) n -> p (a k) n", p=P))\
                        .then_inc(dn_loaded[l][u], 16)

                sp.wait_ge(merged[l], 2 * KC)
                sp.dma_start(dn_s, I["w_down_s"][l].rearrange("(k p) n -> p k n", p=P)).then_inc(sdn_loaded[l], 16)
                for u in (0, 2):
                    load_gate_up(u, 0, u, first=True)
                for u in (0, 1):
                    load_down(u, 0, u, first=True)
                wait_full(sp, l, "out", act - 1, 1)
                sp.dma_start(tri, C["tri"]).then_inc(tri_loaded[l], 16)
                by_p = lambda w: w.rearrange("(p k) n -> p k n", k=KC)
                w = slot(l, "shared")
                sp.dma_start(w[:, :, 0:FE], by_p(I["w_gate_s"][l])).then_inc(slot_loaded[SLOTS - 1], 16)
                sp.dma_start(w[:, :, FE:2 * FE], by_p(I["w_up_s"][l])).then_inc(slot_loaded[SLOTS - 1], 16)
                load_gate_up(1, 0, 1, first=True)
                for u in (2, 3):
                    load_down(u, 0, u, first=True)
                load_gate_up(3, 0, 3, first=True)
                wait_emptied(sp, l, "items")
                more = sp.value_load(more_u[0:1, 0:1], min_val=0, max_val=4)
                with nc.sync.Fori(1, more + BLOCKS) as b:
                    for u in range(UNROLL):
                        e = sp.value_load(item_expert[:, bass.ds(4 * b + u, 1)], min_val=0, max_val=NE - 1)
                        load_gate_up(u, b, e)
                        load_down(u, b, e)
                for u in range(UNROLL):
                    sp.wait_ge(y_stored[l][u], more * 16 + 16 * BLOCKS)
                for t in range(act):
                    if t >= 2:
                        sp.wait_ge(combined[l], t - 1)
                    sp.dma_start(picked[t % 2].rearrange("p (k d) -> p k d", k=TOPK),
                                 y_rows[l].rearrange("(t p k) d -> t p k d", p=P, k=TOPK)[t]).then_inc(picked_loaded[t % 2][l], 16)
            for t in range(2):
                sp.wait_ge(x_updated[DEPTH - 1], ACTIVE[DEPTH - 1] + t + 1)
                sp.dma_start(rows_of(out[0])[:, t, :], xres[:, t, :]).then_inc(out_stored, 16)
            sp.wait_ge(out_stored, 32)

        @block.gpsimd
        def _(pool):
            pool.dma_start(ident[:, :], C["ident"]).then_inc(consts_loaded, 16)
            pool.dma_start(rope_t[:, :, :, :], C["rope"]).then_inc(consts_loaded, 16)
            pool.dma_start(iota, C["iota"]).then_inc(consts_loaded, 16)
            pool.dma_start(pick_id, C["pick_id"]).then_inc(consts_loaded, 16)
            pool.dma_start(item_t, C["item_t"]).then_inc(consts_loaded, 16)
            pool.dma_start(half_id, C["half_id"]).then_inc(consts_loaded, 16)
            col = lambda a: a.rearrange("(k p) -> p k", p=P)
            nc.gpsimd.memset(held, 0.0).then_inc(held_set, 1)
            pool.wait_ge(held_set, 1)
            nc.gpsimd.memset(ca32, 0.0).then_inc(zeroed, 1)
            nc.gpsimd.memset(stage, 0.0).then_inc(zeroed, 1)
            for l in range(DEPTH):
                act = ACTIVE[l]
                with nc.allow_non_contiguous_dma("one small vector a partition"):
                    vectors = []
                    if l == 0:
                        for n, name in enumerate(("g_post_mix", "g_post_ffn")):
                            vectors += [(Grow[:, n, s, :], I[name][0:1, :].to_broadcast([P, DM])) for s in range(2)]
                    vectors += [(gqk[:, 0:2], col(I["g_kv"][l])), (gqk[:, 2:5], col(I["g_q"][l])),
                                (bgate, I["b_gate"][l].rearrange("(b k p) -> p b k", p=P, b=3)),
                                (wr[:, :, :], I["w_router"][l].rearrange("(p k) e -> p k e", k=KC)),
                                (brow, I["b_router"][l:l + 1, :].to_broadcast([P, NE]))]
                    vectors += [(convw[:, j, :], col(I["conv_w"][l][j])) for j in range(3)]
                    assert len(vectors) == VECTORS[l]
                    for dst, src in vectors:
                        pool.dma_start(dst, src).then_inc(params_loaded[l], 16)
                if l:
                    pool.wait_ge(x_updated[l - 1], 2 * ACTIVE[l - 1])
                pool.dma_start(head[:, 0:1280], C["dft"]).then_inc(dft_loaded[l], 16)
                if l == 0:
                    wait_full(pool, l, "h", 1, KC - 1)
                    for n, name in enumerate(("g_post_mix", "g_post_ffn")):
                        pool.dma_start(grow_next[:, n, :], I[name][1:2, :]).then_inc(gpost_loaded, 16)
                    wait_emptied(pool, *picks(2 * ADA_CHUNKS - 1)[-1])
                    pool.dma_start(grow_d, qkv[0:1, 6144:8192]).then_inc(grow_stored, 16)
                else:
                    pool.wait_ge(grow_stored, 16)
                    for n in range(2):
                        pool.dma_start(Grow[:, n, 0, :], grow_d[:, DM * n:DM * n + DM].to_broadcast([P, DM]))\
                            .then_inc(grow_loaded, 16)
                for b in (1, 2):
                    for dc in range(KC):
                        n = (b - 1) * KC + dc
                        wait_emptied(pool, l, "y", b, dc)
                        if b == 2:
                            pool.wait_ge(merged[l], n - KC + 1)
                        nc.gpsimd.tensor_tensor(mT[:, dc, 0:P * act], mT[:, dc, 0:P * act],
                                                ytmp[:, n % 2, 0:P * act], ALU.add).then_inc(merged[l], 1)
                pool.dma_start(slots_d[l], C["absent"][0:P * act * NE]).then_inc(table_clear[l], 16)
                pool.wait_ge(table_clear[l], 16)
                pool.wait_ge(pos_ready[l], 1)
                for t in range(act):
                    for k in range(TOPK):
                        pool.indirect_dma_start(out=slots_d[l], out_offset=bass.IndirectOffsetOnAxis(ap=posu[:, t, k:k + 1], axis=0),
                                                in_=pick_id[:, t, k:k + 1], in_offset=None,
                                                bounds_check=P * act * NE - 1, oob_is_err=False).then_inc(table_filled[l], 16)
                pool.wait_ge(table_filled[l], 16 * act * TOPK)
                for p0 in range(0, P, CAP[l]):
                    pool.dma_start(row_y[p0:p0 + CAP[l], 0:P], slots_d[l].rearrange("(r j e) a -> j r (e a)", e=NE, j=CAP[l]))\
                        .then_inc(table_read[l], 16)
                pool.dma_start(row_y[:, P:P + 1], C["absent"][0:P]).then_inc(table_read[l], 16)
                pool.wait_ge(h_stored[l], 16 * act)
                pool.wait_ge(rows_ready[l], 1)
                wait_emptied(pool, l, "items")
                more = pool.value_load(more_u[0:1, 0:1], min_val=0, max_val=4)
                split = P // CAP[l]
                source = h_rows[l].rearrange("t (a d) -> (t a) d", a=split)
                target = y_rows[l].rearrange("t (a d) -> (t a) d", a=split)
                n_g = P * act * split - 1
                n_y = P * act * TOPK * split - 1

                def column(u, b):
                    return pool.value_load(item_col[:, bass.ds(4 * b + u, 1)], min_val=0, max_val=P)

                def copied(count):
                    pool.wait_ge(now_ready[l], count)
                    nc.gpsimd.tensor_tensor(held, held, held, ALU.mult).then_inc(now_ready[l], 1)

                def gather(u, b, first=False):
                    n = u if first else column(u, b)
                    if not first:
                        pool.wait_ge(xt_full[l], 4 * b + u - 3)
                    pool.wait_ge(rows_ready[l], 1)
                    nc.gpsimd.tensor_copy(now_g[:, u:u + 1], row_g[l][:, bass.ds(n, 1)]).then_inc(now_ready[l], 1)
                    copied((16 * b + 4 * u - 7) if not first else 2 * u + 1)
                    pool.indirect_dma_start(out=xg[u][:, 0:wide[l]], out_offset=None, in_=source,
                                            in_offset=bass.IndirectOffsetOnAxis(ap=now_g[:, u:u + 1], axis=0),
                                            bounds_check=n_g, oob_is_err=False).then_inc(x_gathered[l][u], 16)

                def store(u, b, copies):
                    n = column(u, b)
                    pool.wait_ge(y_act[l], 4 * b + u + 1)
                    if l == 0:
                        pool.wait_ge(y_dve[l], 4 * b + u + 1)
                    nc.gpsimd.tensor_copy(now_y[:, u:u + 1], row_y[:, bass.ds(n, 1)]).then_inc(now_ready[l], 1)
                    copied(copies)
                    pool.indirect_dma_start(out=target, out_offset=bass.IndirectOffsetOnAxis(ap=now_y[:, u:u + 1], axis=0),
                                            in_=y_e[u % 2][:, 0:wide[l]], in_offset=None,
                                            bounds_check=n_y, oob_is_err=False).then_inc(y_stored[l][u], 16)

                for u in range(UNROLL):
                    gather(u, 0, first=True)
                with nc.gpsimd.Fori(1, more + BLOCKS) as b:
                    for u in range(UNROLL):
                        gather(u, b)
                        store(u, b - 1, 16 * b + 4 * u - 5)
                for u in range(UNROLL):
                    store(u, more + (BLOCKS - 1), more * (4 * UNROLL) + (4 * NE - 7 + 2 * u))

        @block.scalar
        def _(act_e):
            col = lambda a: a.rearrange("(k p) -> p k", p=P)
            with nc.allow_non_contiguous_dma("one small vector a partition"):
                act_e.dma_start(cs[:, 0, :], col(I["c"][0])).then_inc(cond_loaded, 16)
                act_e.dma_start(cs[:, 1, :], col(I["c_ctx"])).then_inc(cond_loaded, 16)
                for l in range(DEPTH):
                    act_e.dma_start(gains[:, l, 0, :], col(I["g_pre_mix"][l])).then_inc(gains_loaded, 16)
                    act_e.dma_start(gains[:, l, 1, :], I["g_pre_ffn"][l].rearrange("(p k) -> p k", k=KC)).then_inc(gains_loaded, 16)
            for l in range(DEPTH):
                act = ACTIVE[l]
                n_tok = P * act
                roots, squares = [0], [0]

                def square(src, into, width):
                    act_e.wait_ge(ssq_ready[l], squares[0])
                    squares[0] += 1
                    nc.scalar.activation(junk[:, 0:width], src, ACT.Square, accum_out=ssq[:, into:into + 1])\
                        .then_inc(ssq_ready[l], 1)

                def root(c0, c1):
                    roots[0] += 1
                    act_e.wait_ge(ms_ready[l], roots[0])
                    nc.scalar.activation(rstd[:, c0:c1], ssq[:, c0:c1], ACT.Sqrt).then_inc(root_ready[l], 1)

                if l:
                    act_e.wait_ge(ssq_ready[l - 1], last_squares)
                if l == 0:
                    act_e.wait_ge(cond_loaded, 32)
                    act_e.wait_ge(zeroed, 2)
                    nc.scalar.activation(ca32[:, :, 0:2], cs.rearrange("p s k -> p k s"), ACT.Silu).then_inc(ca_ready, 1)
                if l == 0:
                    act_e.wait_ge(x_loaded, 32)
                for t in range(NTILE):
                    if l:
                        act_e.wait_ge(x_updated[l - 1], ACTIVE[l - 1] + t + 1)
                    square(xres[:, t, :], t, DM)
                    root(t, t + 1)

                def modulate(n):
                    wait_emptied(act_e, "pick", ADA_CHUNKS * l + (3 if n == 1 else 9), 0)
                    for k in range(1, KC, 2):
                        wait_full(act_e, l, "h", n, k)
                        for s in range(2 if n == 1 else act // 2):
                            ins = nc.scalar.activation(hT[:, k, SEQ * s:SEQ * s + SEQ], bank(l, "h", n, k)[:, SEQ * s:SEQ * s + SEQ],
                                                       ACT.Identity, scale=scaleT[l][n - 1][:, s, k:k + 1],
                                                       bias=shiftT[l][n - 1][:, s, k:k + 1])
                        ins.then_inc(emptied["act"], 1)

                modulate(1)
                for t in range(NTILE):
                    wait_full(act_e, l, "kv", t)
                    square(bank(l, "kv", t)[:, 0:KVR], 4 + t, KVR)
                    nc.scalar.activation(kvlat[:, t, :], bank(l, "kv", t)[:, 0:KV_END], ACT.Copy).then_inc(emptied["act"], 1)
                for t in range(act):
                    wait_full(act_e, l, "q", t)
                    square(bank(l, "q", t)[:, 0:QR], 8 + t, QR)
                    nc.scalar.activation(qlat[:, t, :], bank(l, "q", t)[:, 0:QR], ACT.Copy).then_inc(emptied["act"], 1)
                root(4, 8 + act)
                for name, dst in (("b", bT), ("c", cT)):
                    for f in range(4):
                        wait_full(act_e, l, name, f)
                        nc.scalar.activation(dst[:, f, 0:n_tok], bank(l, name, f)[:, 0:n_tok], ACT.Copy).then_inc(emptied["act"], 1)
                for f in range(4):
                    wait_full(act_e, l, "f", f)
                    nc.scalar.activation(fT[:, f, 0:n_tok], bank(l, "f", f)[:, 0:n_tok], ACT.Copy).then_inc(emptied["act"], 1)
                act_e.wait_ge(params_loaded[l], 16 * VECTORS[l])
                for c in range(3):
                    wait_full(act_e, l, "cqT", c)
                    nc.scalar.activation(cqT[:, c, 0:n_tok], bank(l, "cqT", c)[:, 0:n_tok], ACT.Identity,
                                         scale=gqk[:, 2 + c:3 + c]).then_inc(emptied["act"], 1)
                act_e.wait_ge(grow_stored, 16)
                for t in range(NTILE):
                    for j in range(2):
                        wait_full(act_e, l, "kvup", t, j)
                        src = bank(l, "kvup", t, j).rearrange("p (h d) -> p h d", h=4)
                        nc.scalar.activation(ktok[:, t, 4 * j:4 * j + 4, 0:NOPE], src[:, :, 0:NOPE], ACT.Copy)
                        nc.scalar.activation(vtok[:, t, 4 * j:4 * j + 4, :], src[:, :, NOPE:], ACT.Copy).then_inc(emptied["act"], 1)
                n = 0
                for f in range(FG):
                    for s in range(act // 2):
                        wait_full(act_e, l, "four1", f, s)
                        nc.scalar.activation(four_ab[n], bank(l, "four1", f, s), ACT.Copy).then_inc(emptied["act"], 1)
                        n += 1
                units = attention_units(l)
                for kind, u in attention_steps(l):
                    h, s = units[u]
                    if kind == "T":
                        wait_full(act_e, l, "qT", h)
                        nc.scalar.activation(headT[0:QK, h % 2, 0, 0:n_tok], bank(l, "qT", h)[0:QK, 0:n_tok],
                                             ACT.Copy).then_inc(emptied["act"], 1)
                    elif kind == "S":
                        keys = 512 if s == 0 else 256
                        for t in range(2):
                            act_e.wait_ge(max_ready[l], 2 * u + t + 1)
                            if u >= 2:
                                wait_full(act_e, l, "PT", *units[u - 2], t)
                            c = 2 * (u % 2) + t
                            nc.scalar.activation(probs[:, u % 2, t, 0:keys], bank(l, "S", h, s, t)[:, 0:keys], ACT.Exp,
                                                 scale=ATT_SCALE, bias=nmax[:, c:c + 1],
                                                 accum_out=ssum[:, c:c + 1]).then_inc(emptied["act"], 1)
                    elif kind == "PT":
                        nk = 4 if s == 0 else 2
                        wait_full(act_e, l, "PT", h, s, 1)
                        nc.scalar.activation(probsT[:, u % 2, 0:nk, P:2 * P],
                                             bank(l, "PT", h, s, 1)[:, 0:P * nk].rearrange("p (k q) -> p k q", q=P),
                                             ACT.Copy).then_inc(emptied["act"], 1)

                def split_gate(n):
                    if n < 3 * KC:
                        if n >= 2:
                            wait_full(act_e, l, "g", *divmod(n - 2, KC))
                        nc.scalar.activation(w_hi[:, n % 2, :, :], gate_columns(act_e, l, n), ACT.Copy).then_inc(w_hi_ready[l], 1)

                split_gate(0)
                wait_full(act_e, l, "O", *units[-1])
                for k in range(KC):
                    nc.scalar.activation(h_hi[:, k, 0:n_tok], hT[:, k, 0:n_tok], ACT.Copy).then_inc(h_hi_ready[l], 1)
                split_gate(1)

                def split_branch(n):
                    b, dc = divmod(n, KC)
                    w = branch_columns(act_e, l, n)
                    if n:
                        wait_full(act_e, l, "y", *divmod(n - 1, KC))
                    nc.scalar.activation(v_hi[:, :, :], w, ACT.Copy).then_inc(v_hi_ready[l], 1)
                    if dc == 0:
                        if b == 0:
                            wait_emptied(act_e, l, "O", *units[-1])
                            act_e.wait_ge(conv_ready[l], 4)
                        if b == 2:
                            wait_emptied(act_e, l, "four2", FG - 1)
                        for c in range(4):
                            nc.scalar.activation(br_hi[:, c, 0:n_tok], (oT, bT, fT)[b][:, c, 0:n_tok], ACT.Copy)\
                                .then_inc(br_hi_ready[l], 1)

                split_branch(0)
                for b in range(3):
                    for dc in range(KC):
                        n = b * KC + dc
                        wait_full(act_e, l, "g", b, dc)
                        if n >= 2:
                            wait_emptied(act_e, l, "y", (n - 2) // KC, (n - 2) % KC)
                        nc.scalar.activation(tmp2[:, n % 2, 0:n_tok], bank(l, "g", b, dc)[:, 0:n_tok], ACT.Sigmoid,
                                             bias=bgate[:, b, dc:dc + 1]).then_inc(emptied["act"], 1)
                        split_gate(n + 2)
                        if n + 1 < 3 * KC:
                            split_branch(n + 1)

                def second_norm(t):
                    act_e.wait_ge(x_updated[l], t + 1)
                    square(xres[:, t, :], t, DM)
                    root(t, t + 1)

                for j in range(2):
                    wait_arrived(act_e, l, "out", j)
                    for k in range(KC):
                        if j == 0:
                            act_e.wait_ge(merged[l], KC + k + 1)
                            nc.scalar.activation(h_hi[:, k, 0:n_tok], mT[:, k, 0:n_tok], ACT.Copy).then_inc(h_hi_ready[l], 1)
                        w, high, _ = out_weights(l, j, k)
                        nc.scalar.activation(high, w, ACT.Copy).then_inc(w_hi_ready[l], 1)
                wait_emptied(act_e, l, "y", 2, KC - 1)
                for t in range(act):
                    if t >= 2:
                        act_e.wait_ge(x_updated[l], t - 1)
                    for j in range(2):
                        wait_full(act_e, l, "out", t, j)
                        square(bank(l, "out", t, j), 12 + 2 * t + j, 512)
                        nc.scalar.activation(rows[:, t % 2, 512 * j:512 * j + 512], bank(l, "out", t, j), ACT.Copy)\
                            .then_inc(emptied["act"], 1)
                    root(12 + 2 * t, 13 + 2 * t)
                    if t >= 1:
                        second_norm(t - 1)
                second_norm(act - 1)
                modulate(2)
                for t in range(act):
                    wait_full(act_e, l, "rt", t)
                    nc.scalar.activation(score[:, t, :], bank(l, "rt", t)[:, 0:NE], ACT.Sigmoid).then_inc(emptied["act"], 1)
                for t in range(act):
                    for j in range(2):
                        wait_full(act_e, l, "hrow", t, j)
                        nc.scalar.activation(hrow[t][:, 512 * j:512 * j + 512], bank(l, "hrow", t, j), ACT.Copy)\
                            .then_inc(emptied["act"], 1)
                    wait_emptied(act_e, l, "hrow", t, 1)
                    act_e.dma_start(h_rows[l].rearrange("(t p) d -> t p d", p=P)[t], hrow[t]).then_inc(h_stored[l], 16)
                act_e.wait_ge(pos_ready[l], 1)
                for f in range(2):
                    act_e.wait_ge(sgu_full[l], f + 1)
                    nc.scalar.activation(silu_s[:, f, 0:n_tok], ps[:, 512 * f:512 * f + n_tok], ACT.Silu).then_inc(ssilu_ready[l], 1)
                wait_emptied(act_e, l, "items")
                more = nc.scalar.value_load(more_u[0:1, 0:1], min_val=0, max_val=4)
                half = wide[l] // 2
                fw = CAP[l] * 2

                def take_x(u, b, n=None):
                    act_e.wait_ge(xt_full[l], 4 * b + u + 1)
                    if n is None or n >= 2:
                        act_e.wait_ge(gu_full[l], 4 * b + u - 1)
                    nc.scalar.activation(xT[u % 2][:, 0:half], ps[:, 1024:1024 + half], ACT.Copy).then_inc(xt_act[l], 1)

                def silus(u, b, n=None):
                    act_e.wait_ge(gu_full[l], 4 * b + u + 1)
                    if n is None or n >= 2:
                        act_e.wait_ge(a_ready[l], 4 * b + u - 1)
                    nc.scalar.activation(silu_e[u % 2][:, 0:fw], ps[:, 512 * (u % 2):512 * (u % 2) + fw], ACT.Silu)\
                        .then_inc(silu_ready[l], 1)

                def take_y(u, b, n=None):
                    act_e.wait_ge(y_full[l], 4 * b + u + 1)
                    if n is None or n >= 2:
                        act_e.wait_ge(y_stored[l][(u - 2) % 4], 16 * b + (16 if u >= 2 else 0))
                    nc.scalar.activation(y_e[u % 2][:, 0:512], ps[:, 2560:3072], ACT.Copy).then_inc(y_act[l], 1)

                for n in range(UNROLL):
                    take_x(n, 0, n)
                    if n >= 1:
                        silus(n - 1, 0, n - 1)
                    if n >= 2:
                        take_y(n - 2, 0, n - 2)
                with nc.scalar.Fori(1, more + BLOCKS) as b:
                    for u in range(UNROLL):
                        take_x(u, b)
                        silus((u - 1) % 4, b - (u < 1))
                        take_y((u - 2) % 4, b - (u < 2))
                silus(3, more + (BLOCKS - 1))
                take_y(2, more + (BLOCKS - 1))
                take_y(3, more + (BLOCKS - 1))
                for t in range(act):
                    act_e.wait_ge(combined[l], t + 1)
                    square(acc[:, t, :], t, DM)
                    root(t, t + 1)
                last_squares = squares[0]

        @block.tensor
        def _(pe):
            opened = [0]

            def group(*key):
                n = G.at[key]
                assert n == opened[0]
                opened[0] += 1
                if n >= BANKS:
                    owner, count = G.emptied_at[n - BANKS]
                    pe.wait_ge(emptied[owner], count)
                return bank(*key)

            def arrived(*key):
                return wait_arrived(pe, *key)

            def chain(dst, pairs):
                for n, (a, b) in enumerate(pairs):
                    ins = nc.tensor.matmul(dst, a, b, start=n == 0, stop=n == len(pairs) - 1)
                return ins

            for l in range(DEPTH):
                act = ACTIVE[l]
                n_tok = P * act
                tile = lambda t: slice(P * t, P * t + P)

                def ada(a):
                    dst = group("ada", a)
                    w = arrived("ada", a)
                    for k in range(KC):
                        g = 32 * (k % 4)
                        ins = nc.tensor.matmul(dst[g:g + 32, :], ca32[:, k, :], w[:, k, :], start=k < 4, stop=k >= 4,
                                               skip_group_check=True)
                    ins.then_inc(psum_full, 1)

                def pick(a):
                    lc, c = divmod(a, ADA_CHUNKS)
                    chunk = stage[:, a % 4, :]
                    wait_emptied(pe, "ada", a)
                    for key in picks(a):
                        dst = group(*key)
                        if is_gate(c):
                            rows_to = P if lc == 0 else 1
                            s = key[2]
                            ins = nc.tensor.matmul(dst[0:rows_to, :], sel[:, s:s + 1].to_broadcast([P, rows_to]), chunk,
                                                   start=True, stop=True)
                        elif c < 4:
                            for b in range(4):
                                ins = nc.tensor.matmul(dst[:, 2 * b:2 * b + 2], chunk[:, tile(b)], sel, start=True, stop=True)
                        else:
                            h0 = 64 * (c % 2)
                            for k in range(KC):
                                ins = nc.tensor.matmul(dst[h0:h0 + 64, 2 * k:2 * k + 2],
                                                       chunk.rearrange("p (q k) -> p k q", k=KC)[:, k, :], sel,
                                                       start=True, stop=True, skip_group_check=True)
                        ins.then_inc(psum_full, 1)

                def chunk_step(l, name, n):
                    a = chunk_after(l, name, n)
                    if a is not None:
                        if a != 4:
                            pick(a - 1)
                        ada(a)

                if l == 0:
                    pe.wait_ge(consts_loaded, 96)
                    pe.wait_ge(ca_ready, 1)
                    for a in range(4):
                        if a:
                            pick(a - 1)
                        ada(a)
                    pick(3)

                def transpose_h(n, tiles):
                    for k in range(KC):
                        dst = group(l, "h", n, k)
                        for t in range(tiles):
                            if k == 0:
                                pe.wait_ge(xn_ready[l], (0 if n == 1 else NTILE) + t + 1)
                            cols = xn[:, t, tile(k)] if n == 1 else xn[:, t, :].rearrange("p (q k) -> p k q", k=KC)[:, k, :]
                            ins = nc.tensor.transpose(dst[:, tile(t)], cols, ident[:, :])
                        ins.then_inc(psum_full, 1)

                transpose_h(1, NTILE)
                for t in range(NTILE):
                    dst = group(l, "kv", t)
                    w = arrived(l, "kv")
                    if t == 0:
                        wait_emptied(pe, l, "h", 1, KC - 2)
                        wait_emptied(pe, l, "h", 1, KC - 1)
                    chain(dst[:, 0:KV_END], [(hT[:, k, tile(t)], w[:, k, :]) for k in range(KC)]).then_inc(psum_full, 1)
                    chunk_step(l, "kv", t)
                for t in range(act):
                    dst = group(l, "q", t)
                    w = arrived(l, "q")
                    chain(dst[:, 0:QR], [(hT[:, k, tile(t)], w[:, k, :]) for k in range(KC)]).then_inc(psum_full, 1)
                    chunk_step(l, "q", t)
                for name in "bcuf":
                    for f in range(4):
                        dst = group(l, name, f)
                        w = arrived(l, name)
                        chain(dst[:, 0:n_tok], [(w[:, k, tile(f)], hT[:, k, 0:n_tok]) for k in range(KC)]).then_inc(psum_full, 1)
                        chunk_step(l, name, f)
                if l == 0:
                    pick(2 * ADA_CHUNKS - 1)
                pe.wait_ge(lat_ready[l], 1)
                for c in range(2):
                    dst = group(l, "ckvT", c)
                    for t in range(NTILE):
                        ins = nc.tensor.transpose(dst[:, tile(t)], kvlat[:, t, tile(c)], ident[:, :])
                    ins.then_inc(psum_full, 1)
                for c in range(3):
                    dst = group(l, "cqT", c)
                    for t in range(act):
                        ins = nc.tensor.transpose(dst[:, tile(t)], qlat[:, t, tile(c)], ident[:, :])
                    ins.then_inc(psum_full, 1)
                for t in range(NTILE):
                    for j in range(2):
                        dst = group(l, "kvup", t, j)
                        w = arrived(l, "ukv")
                        wait_emptied(pe, l, "ckvT", 1)
                        chain(dst, [(ckvT[:, c, tile(t)], w[:, c, 512 * j:512 * j + 512]) for c in range(2)]).then_inc(psum_full, 1)
                for t in range(act):
                    for j in range(2):
                        dst = group(l, "qup", t, j)
                        w = arrived(l, "uq")
                        wait_emptied(pe, l, "cqT", 2)
                        chain(dst[:, 0:4 * QK], [(cqT[:, c, tile(t)], w[:, c, 4 * QK * j:4 * QK * (j + 1)]) for c in range(3)])\
                            .then_inc(psum_full, 1)
                pe.wait_ge(dft_loaded[l], 16)
                for f in range(FG):
                    wait_emptied(pe, l, "f", f)
                    for s in range(act // 2):
                        dst = group(l, "four1", f, s)
                        for t in range(2):
                            ins = nc.tensor.matmul(dst[:, 256 * t:256 * t + 256], fT[:, f, tile(2 * s + t)], dft_c,
                                                   start=True, stop=True)
                        ins.then_inc(psum_full, 1)
                for f in range(FG):
                    dst = group(l, "four2", f)
                    for s in range(act // 2):
                        n = f * (act // 2) + s
                        wait_emptied(pe, l, "four1", f, s)
                        ab = four_ab[n].rearrange("p (t a c) -> p t a c", t=2, a=2)
                        ins = chain(dst[:, SEQ * s:SEQ * s + SEQ],
                                    [(ab[:, t, a, :], dft_n[:, a, t, :]) for t in range(2) for a in range(2)])
                    ins.then_inc(psum_full, 1)
                wait_emptied(pe, l, "kvup", NTILE - 1, 1)
                pe.wait_ge(kpe_ready[l], 1)
                pe.wait_ge(qrope_ready[l], 1)
                units = attention_units(l)
                for kind, u in attention_steps(l):
                    h, s = units[u]
                    nk = 4 if s == 0 else 2
                    if kind == "T":
                        for name, rows_of_head, dim in (("kT", ktok, NTILE), ("qT", qtok, act)):
                            dst = group(l, name, h)
                            for t in range(dim):
                                ins = nc.tensor.transpose(dst[0:QK, tile(t)], rows_of_head[:, t, h, :], ident[:, :])
                            ins.then_inc(psum_full, 1)
                    elif kind == "S":
                        wait_emptied(pe, l, "kT", h)
                        wait_emptied(pe, l, "qT", h)
                        k0 = P * (NTILE - nk)
                        for t in range(2):
                            dst = group(l, "S", h, s, t)
                            nc.tensor.matmul(dst[:, 0:512 - k0], headT[0:QK, h % 2, 0, tile(2 * s + t)],
                                             headT[0:QK, h % 2, 1, k0:512], start=True, stop=True).then_inc(psum_full, 1)
                    elif kind == "PT":
                        for t in range(2):
                            dst = group(l, "PT", h, s, t)
                            pe.wait_ge(prob_ready[l], 2 * u + t + 1)
                            for k in range(nk):
                                ins = nc.tensor.transpose(dst[:, tile(k)], probs[:, u % 2, t, tile(k)], ident[:, :])
                            ins.then_inc(psum_full, 1)
                    else:
                        dst = group(l, "O", h, s)
                        for t in range(2):
                            wait_emptied(pe, l, "PT", h, s, t)
                        half = slice(VD * (h % 2), VD * (h % 2) + VD)
                        chain(dst[half, 0:SEQ], [(vtok[:, (NTILE - nk) + k, h, :], probsT[:, u % 2, k, :]) for k in range(nk)])\
                            .then_inc(psum_full, 1)
                wait_emptied(pe, l, "O", *units[-1])
                branch_lo = [oT_lo, bT_lo, fT_lo]
                for b in range(3):
                    for dc in range(KC):
                        dst = group(l, "g", b, dc)
                        n = b * KC + dc
                        pe.wait_ge(w_lo_ready[l], n + 1)
                        for k in range(KC):
                            if n == 0:
                                pe.wait_ge(h_lo_ready[l], k + 1)
                            hi, lo = w_hi[:, n % 2, k, :], w_lo[:, n % 2, k, :]
                            nc.tensor.matmul(dst[:, 0:n_tok], hi, h_hi[:, k, 0:n_tok], start=k == 0, stop=False)
                            nc.tensor.matmul(dst[:, 0:n_tok], hi, h_lo[:, k, 0:n_tok], start=False, stop=False)
                            ins = nc.tensor.matmul(dst[:, 0:n_tok], lo, h_hi[:, k, 0:n_tok], start=False, stop=k == KC - 1)
                        ins.then_inc(psum_full, 1)
                        dst = group(l, "y", b, dc)
                        pe.wait_ge(v_lo_ready[l], n + 1)
                        for c in range(4):
                            if dc == 0:
                                pe.wait_ge(br_lo_ready[l], 4 * b + c + 1)
                            hi, lo = v_hi[:, c, :], v_lo[:, c, :]
                            nc.tensor.matmul(dst[:, 0:n_tok], hi, br_hi[:, c, 0:n_tok], start=c == 0, stop=False)
                            nc.tensor.matmul(dst[:, 0:n_tok], hi, branch_lo[b][:, c, 0:n_tok], start=False, stop=False)
                            ins = nc.tensor.matmul(dst[:, 0:n_tok], lo, br_hi[:, c, 0:n_tok], start=False, stop=c == 3)
                        ins.then_inc(psum_full, 1)
                for t in range(act):
                    for j in range(2):
                        dst = group(l, "out", t, j)
                        for k in range(KC):
                            if t == 0:
                                if j == 0:
                                    pe.wait_ge(h_lo_ready[l], KC + k + 1)
                                pe.wait_ge(w_lo_ready[l], 3 * KC + KC * j + k + 1)
                            _, high, low = out_weights(l, j, k)
                            hi, lo = h_hi[:, k, tile(t)], m_lo[:, k, tile(t)]
                            nc.tensor.matmul(dst, hi, high, start=k == 0, stop=False)
                            nc.tensor.matmul(dst, hi, low, start=False, stop=False)
                            ins = nc.tensor.matmul(dst, lo, high, start=False, stop=k == KC - 1)
                        ins.then_inc(psum_full, 1)
                transpose_h(2, act)
                wait_emptied(pe, l, "h", 2, KC - 2)
                wait_emptied(pe, l, "h", 2, KC - 1)
                for t in range(act):
                    dst = group(l, "rt", t)
                    chain(dst[:, 0:NE], [(hT[:, k, tile(t)], wr[:, k, :]) for k in range(KC)]).then_inc(psum_full, 1)
                for t in range(act):
                    for j in range(2):
                        dst = group(l, "hrow", t, j)
                        for k in range(4):
                            ins = nc.tensor.transpose(dst[:, tile(k)], hT[:, 4 * j + k, tile(t)], ident[:, :])
                        ins.then_inc(psum_full, 1)
                dst = group(l, "rank")
                pe.wait_ge(tri_loaded[l], 16)
                pe.wait_ge(mask_ready[l], 1)
                ones, above = tri[:, 0:P], tri[:, P:2 * P]
                for t in range(act):
                    chain(dst[:, NE * t:NE * t + NE], [(ones, mask[:, a, :]) for a in range(t)] + [(above, mask[:, t, :])])
                for r in range(ROUNDS):
                    for a in range(act):
                        ins = nc.tensor.matmul(dst[NE * r:NE * r + NE, P:P + 1], mask[:, a, :], ones[:, 0:1], start=a == 0,
                                               stop=a == act - 1, skip_group_check=True)
                ins.then_inc(psum_full, 1)
                dst = group(l, "turn")
                pe.wait_ge(needed_ready[l], 1)
                nc.tensor.matmul(dst[:, 0:1], above, needed, start=True, stop=True)
                nc.tensor.matmul(dst[:, 1:2], ones, needed, start=True, stop=True).then_inc(psum_full, 1)
                dst = group(l, "items")
                pe.wait_ge(turn_ready[l], 1)
                for a in range(2):
                    ins = nc.tensor.matmul(dst[0:1, MAX_ITEMS * a:MAX_ITEMS * (a + 1)], item_t[:, 2 + a:3 + a], turn,
                                           start=True, stop=True)
                ins.then_inc(psum_full, 1)
                arrived(l, "shared")
                wait_emptied(pe, l, "items")
                wait_emptied(pe, l, "hrow", act - 1, 1)
                w = slot(l, "shared")
                for f in range(2):
                    for a in range(2):
                        b = f + 2 * a
                        ins = chain(ps[:, 512 * b:512 * b + n_tok],
                                    [(w[:, k, FE * a + P * f:FE * a + P * f + P], hT[:, k, 0:n_tok]) for k in range(KC)])
                    ins.then_inc(sgu_full[l], 1)
                pe.wait_ge(sdn_loaded[l], 16)
                pe.wait_ge(sact_ready[l], 2)
                for g in range(2 * act):
                    t, hf = g // 2, g % 2
                    b = 4 + g % 4
                    if g >= 4:
                        pe.wait_ge(sdn_taken[l], g - 3)
                    chain(ps[:, 512 * b:512 * b + 512],
                          [(act_s[:, f, tile(t)], dn_s[:, f, 512 * hf:512 * hf + 512]) for f in range(2)])\
                        .then_inc(sdn_full[l], 1)
                pe.wait_ge(sdn_taken[l], 2 * act)
                wait_emptied(pe, l, "items")
                more = nc.tensor.value_load(more_u[0:1, 0:1], min_val=0, max_val=4)

                narrow = CAP[l] < P

                def transpose_x(u, b, n=None):
                    pe.wait_ge(x_gathered[l][u], 16 * b + 16)
                    if n is None or n >= 1:
                        pe.wait_ge(xt_act[l], 4 * b + u)
                        pe.wait_ge(xt_dve[l], 4 * b + u)
                    for k in range(wide[l] // P):
                        c = 1024 + (P * k if not narrow else 512 * (k // 2) + P * (k % 2))
                        ins = nc.tensor.transpose(ps[:, c:c + P], xg[u][:, tile(k)], ident[:, :])
                    ins.then_inc(xt_full[l], 1)

                def gate_up(u, b):
                    pe.wait_ge(gu_loaded[l][u], 32 * b + 32)
                    pe.wait_ge(xt_act[l], 4 * b + u + 1)
                    pe.wait_ge(xt_dve[l], 4 * b + u + 1)
                    o = 512 * (u % 2)
                    x = xT[u % 2]
                    for k in range(KC):
                        if not narrow:
                            ins = nc.tensor.matmul(ps[:, o:o + 512], x[:, tile(k)], gu[u][:, k, :], start=k == 0, stop=k == KC - 1)
                        else:
                            xk = x[:, P * (k % 4) + 64 * (k // 4):P * (k % 4) + 64 * (k // 4) + 64]
                            for f in range(2):
                                w = gu[u][:, k, :].rearrange("p (a n) -> p a n", a=2)[:, :, P * f:P * f + P]
                                ins = nc.tensor.matmul(ps[64 * f:64 * f + 64, o:o + 256], xk, w, start=k == 0,
                                                       stop=k == KC - 1, skip_group_check=True)
                    ins.then_inc(gu_full[l], 1)

                def transpose_a(u, b, n=None):
                    pe.wait_ge(a_ready[l], 4 * b + u + 1)
                    if n is None or n >= 1:
                        pe.wait_ge(at_ready[l], 4 * b + u)
                    for f in range(1 if narrow else 2):
                        ins = nc.tensor.transpose(ps[:, 2048 + P * f:2048 + P * f + P], a_e[u % 2][:, tile(f)], ident[:, :])
                    ins.then_inc(at_full[l], 1)

                def down(u, b, n=None):
                    pe.wait_ge(at_ready[l], 4 * b + u + 1)
                    pe.wait_ge(dn_loaded[l][u], 16 * b + 16)
                    if n is None or n >= 1:
                        pe.wait_ge(y_act[l], 4 * b + u)
                        if not narrow:
                            pe.wait_ge(y_dve[l], 4 * b + u)
                    for f in range(2):
                        for c in range(2):
                            if not narrow:
                                ins = nc.tensor.matmul(ps[:, 2560 + 512 * c:3072 + 512 * c], aT_e[u % 2][:, tile(f)],
                                                       dn[u][:, f, 512 * c:512 * c + 512], start=f == 0, stop=f == 1)
                            else:
                                ins = nc.tensor.matmul(ps[64 * c:64 * c + 64, 2560:3072], aT_e[u % 2][:, 64 * f:64 * f + 64],
                                                       dn[u][:, f, 512 * c:512 * c + 512], start=f == 0, stop=f == 1,
                                                       skip_group_check=True)
                    ins.then_inc(y_full[l], 1)

                for n in range(UNROLL):
                    transpose_x(n, 0, n)
                    if n >= 2:
                        transpose_a(n - 2, 0, n - 2)
                    if n >= 1:
                        gate_up(n - 1, 0)
                    if n >= 2:
                        down(n - 2, 0, n - 2)
                with nc.tensor.Fori(1, more + BLOCKS) as b:
                    for u in range(UNROLL):
                        transpose_x(u, b)
                        transpose_a((u - 2) % 4, b - (u < 2))
                        gate_up((u - 1) % 4, b - (u < 1))
                        down((u - 2) % 4, b - (u < 2))
                last = more + (BLOCKS - 1)
                transpose_a(2, last)
                gate_up(3, last)
                down(2, last)
                transpose_a(3, last)
                down(3, last)

        @block.vector
        def _(dve):
            steps = [0]

            def link(ins):
                steps[0] += 1
                ins.then_inc(dve_step, 1)
                dve.wait_ge(dve_step, steps[0])

            V = nc.vector
            dve.wait_ge(consts_loaded, 96)
            for l in range(DEPTH):
                act = ACTIVE[l]
                n_tok = P * act
                counts = {"ssq": 0, "root": 0}

                def mean_square(count, pieces):
                    counts["ssq"] += count
                    dve.wait_ge(ssq_ready[l], counts["ssq"])
                    for c0, c1, width in pieces:
                        ins = V.tensor_scalar(ssq[:, c0:c1], ssq[:, c0:c1], 1.0 / width, EPS, ALU.mult, ALU.add)
                    ins.then_inc(ms_ready[l], 1)

                def inverse_root(c0, c1):
                    counts["root"] += 1
                    dve.wait_ge(root_ready[l], counts["root"])
                    link(V.reciprocal(rstd[:, c0:c1], rstd[:, c0:c1]))

                def invert_norm(t):
                    mean_square(1, [(t, t + 1, DM)])
                    inverse_root(t, t + 1)

                def normalise_x(t):
                    V.tensor_scalar(xn[:, t, :], xres[:, t, :], rstd[:, t:t + 1], None, ALU.mult).then_inc(xn_ready[l], 1)

                for t in range(NTILE):
                    invert_norm(t)
                    normalise_x(t)

                def take_picks(a):
                    lc, c = divmod(a, ADA_CHUNKS)
                    for key in picks(a):
                        wait_full(dve, *key)
                        src = bank(*key)
                        if is_gate(c):
                            n, j, s = c // 10, c % 2 if c >= 10 else c - 4, key[2]
                            if lc == 0:
                                ins = V.tensor_tensor(Grow[:, n, s, 512 * j:512 * j + 512], src, Grow[:, n, s, 512 * j:512 * j + 512],
                                                      ALU.mult)
                            else:
                                dve.wait_ge(gpost_loaded, 32)
                                ins = V.tensor_tensor(grow_next[:, n, 512 * j:512 * j + 512], src[0:1, :],
                                                      grow_next[:, n, 512 * j:512 * j + 512], ALU.mult)
                        else:
                            n = c // 6
                            scale = c in (2, 3, 8, 9)
                            to = (scaleT if scale else shiftT)[lc][n]
                            S = to.shape[1]
                            if n == 0:
                                k0 = 4 * (c % 2)
                                to, rows_ = to[:, :, k0:k0 + 4], slice(0, P)
                                src = src[:, 0:8].rearrange("p (k s) -> p s k", s=2)
                                gain = gains[:, lc, 0:1, k0:k0 + 4].to_broadcast([P, S, 4])
                            else:
                                rows_ = slice(64 * (c % 2), 64 * (c % 2) + 64)
                                to = to[rows_]
                                src = src[rows_, 0:16].rearrange("p (k s) -> p s k", s=2)[:, 0:S, :]
                                gain = gains[rows_, lc, 1:2, :].to_broadcast([64, S, KC])
                            ins = V.scalar_tensor_tensor(to, src, 1.0, gain, ALU.add, ALU.mult) if scale else V.tensor_copy(to, src)
                        ins.then_inc(emptied["dve"], 1)

                def stage_chunk(a):
                    wait_full(dve, "ada", a)
                    if a >= 4:
                        wait_full(dve, *picks(a - 4)[-1])
                    for p0, p1 in ((0, 2), (32, 64), (64, 128)):
                        ins = V.tensor_copy(stage[p0:p1, a % 4, :], bank("ada", a)[p0:p1, :])
                    ins.then_inc(emptied["dve"], 1)

                def chunk_step(l, name, n):
                    a = chunk_after(l, name, n)
                    if a is not None:
                        if a != 4:
                            take_picks(a - 1)
                        stage_chunk(a)

                if l == 0:
                    dve.wait_ge(zeroed, 2)
                    for a in range(4):
                        if a == 1:
                            dve.wait_ge(gains_loaded, 16 * 2 * DEPTH)
                        if a:
                            take_picks(a - 1)
                        stage_chunk(a)
                    take_picks(3)

                def modulate(n):
                    wait_emptied(dve, "pick", ADA_CHUNKS * l + (3 if n == 1 else 9), 0)
                    for k in range(0, KC, 2):
                        wait_full(dve, l, "h", n, k)
                        for s in range(2 if n == 1 else act // 2):
                            ins = V.tensor_scalar(hT[:, k, SEQ * s:SEQ * s + SEQ], bank(l, "h", n, k)[:, SEQ * s:SEQ * s + SEQ],
                                                  scaleT[l][n - 1][:, s, k:k + 1], shiftT[l][n - 1][:, s, k:k + 1], ALU.mult, ALU.add)
                        ins.then_inc(emptied["dve"], 1)

                modulate(1)
                if l == 0:
                    dve.wait_ge(params_loaded[l], 16 * VECTORS[l])
                for name, count in (("kv", NTILE), ("q", act)):
                    for n in range(count):
                        chunk_step(l, name, n)
                mean_square(NTILE + act, [(4, 8, KVR), (8, 8 + act, QR)])
                inverse_root(4, 8 + act)
                wait_emptied(dve, l, "kv", NTILE - 1)
                wait_emptied(dve, l, "q", act - 1)
                for t in range(NTILE):
                    V.tensor_scalar(kvlat[:, t, 0:KVR], kvlat[:, t, 0:KVR], rstd[:, 4 + t:5 + t], None, ALU.mult)
                for t in range(act):
                    ins = V.tensor_scalar(qlat[:, t, :], qlat[:, t, :], rstd[:, 8 + t:9 + t], None, ALU.mult)
                ins.then_inc(lat_ready[l], 1)
                cos, sin = rope_t[:, :, 0, :], rope_t[:, :, 1, :]
                x1, x2 = kvlat[:, 0:2, KVR:KVR + 16], kvlat[:, 0:2, KVR + 16:KV_END]
                t1, t2, t3, t4 = rt1[:, :, 0, :], rt1[:, :, 1, :], rt1[:, :, 2, :], rt1[:, :, 3, :]
                V.tensor_tensor(t1, x1, cos, ALU.mult)
                V.tensor_tensor(t2, x2, sin, ALU.mult)
                V.tensor_tensor(t3, x2, cos, ALU.mult)
                V.tensor_copy(ropek[:, 2:4, :], kvlat[:, 2:4, KVR:KV_END])
                link(V.tensor_tensor(t4, x1, sin, ALU.mult))
                V.tensor_tensor(ropek[:, 0:2, 0:16], t1, t2, ALU.subtract)
                link(V.tensor_tensor(ropek[:, 0:2, 16:32], t3, t4, ALU.add))
                wait_full(dve, l, "kv", 0)
                for t in range(NTILE):
                    ins = V.tensor_copy(ktok[:, t, :, NOPE:QK], ropek[:, t:t + 1, :].to_broadcast([P, H, ROPE]))
                ins.then_inc(kpe_ready[l], 1)
                for name in "bc":
                    for f in range(4):
                        chunk_step(l, name, f)
                dve.wait_ge(params_loaded[l], 16 * VECTORS[l])
                for f in range(4):
                    wait_full(dve, l, "u", f)
                    wait_emptied(dve, l, "c", f)
                    V.tensor_tensor(cT[:, f, 0:n_tok], bank(l, "u", f)[:, 0:n_tok], cT[:, f, 0:n_tok], ALU.mult)\
                        .then_inc(emptied["dve"], 1)
                    wait_emptied(dve, l, "u", f)
                    inner = cT[:, f, 0:n_tok].rearrange("p (s n) -> p s n", n=SEQ)
                    y = tmp2[:, f % 2, 0:n_tok].rearrange("p (s n) -> p s n", n=SEQ)
                    link(V.tensor_scalar(y, inner, convw[:, 1, f:f + 1], None, ALU.mult))
                    link(V.scalar_tensor_tensor(y[:, :, 1:SEQ], inner[:, :, 0:SEQ - 1], convw[:, 0, f:f + 1],
                                                y[:, :, 1:SEQ], ALU.mult, ALU.add))
                    link(V.scalar_tensor_tensor(y[:, :, 0:SEQ - 1], inner[:, :, 1:SEQ], convw[:, 2, f:f + 1],
                                                y[:, :, 0:SEQ - 1], ALU.mult, ALU.add))
                    wait_emptied(dve, l, "b", f)
                    V.tensor_tensor(bT[:, f, 0:n_tok], bT[:, f, 0:n_tok], tmp2[:, f % 2, 0:n_tok], ALU.mult).then_inc(conv_ready[l], 1)
                    chunk_step(l, "u", f)
                if l == 0:
                    take_picks(2 * ADA_CHUNKS - 1)
                for c in range(2):
                    wait_full(dve, l, "ckvT", c)
                    V.tensor_scalar(ckvT[:, c, :], bank(l, "ckvT", c), gqk[:, c:c + 1], None, ALU.mult).then_inc(emptied["dve"], 1)
                for t in range(act):
                    for j in range(2):
                        wait_full(dve, l, "qup", t, j)
                        V.tensor_copy(qtok[:, t, 4 * j:4 * j + 4, :], bank(l, "qup", t, j)[:, 0:4 * QK].rearrange("p (h d) -> p h d", h=4))\
                            .then_inc(emptied["dve"], 1)
                wait_emptied(dve, l, "qup", act - 1, 1)
                for t in range(2):
                    q1, q2 = qtok[:, t, :, NOPE:NOPE + 16], qtok[:, t, :, NOPE + 16:QK]
                    c_ = rope_t[:, t, 0:1, :].to_broadcast([P, H, 16])
                    s_ = rope_t[:, t, 1:2, :].to_broadcast([P, H, 16])
                    a1, a2 = rt1[:, 0], rt1[:, 1]
                    b1, b2 = rt2[:, 0], rt2[:, 1]
                    V.tensor_tensor(a1, q1, c_, ALU.mult)
                    V.tensor_tensor(a2, q2, s_, ALU.mult)
                    V.tensor_tensor(b1, q2, c_, ALU.mult)
                    link(V.tensor_tensor(b2, q1, s_, ALU.mult))
                    V.tensor_tensor(q1, a1, a2, ALU.subtract)
                    ins = V.tensor_tensor(q2, b1, b2, ALU.add)
                    if t == 0:
                        link(ins)
                ins.then_inc(qrope_ready[l], 1)
                for f in range(FG):
                    wait_full(dve, l, "four2", f)
                    V.tensor_copy(fT[:, f, 0:n_tok], bank(l, "four2", f)[:, 0:n_tok]).then_inc(emptied["dve"], 1)
                units = attention_units(l)

                def normalise(u):
                    h, s = units[u]
                    keys = 512 if s == 0 else 256
                    for t in range(2):
                        c = 2 * (u % 2) + t
                        wait_emptied(dve, l, "S", h, s, t)
                        link(V.reciprocal(sinv[:, c:c + 1], ssum[:, c:c + 1]))
                        V.tensor_scalar(probs[:, u % 2, t, 0:keys], probs[:, u % 2, t, 0:keys], sinv[:, c:c + 1], None,
                                        ALU.mult).then_inc(prob_ready[l], 1)

                for kind, u in attention_steps(l):
                    h, s = units[u]
                    keys = 512 if s == 0 else 256
                    if kind == "T":
                        wait_full(dve, l, "kT", h)
                        V.tensor_copy(headT[0:QK, h % 2, 1, :], bank(l, "kT", h)[0:QK, :]).then_inc(emptied["dve"], 1)
                    elif kind == "S":
                        if u >= 1:
                            normalise(u - 1)
                        for t in range(2):
                            c = 2 * (u % 2) + t
                            wait_full(dve, l, "S", h, s, t)
                            link(V.reduce_max(smax[:, c:c + 1], bank(l, "S", h, s, t)[:, 0:keys], AX))
                            V.tensor_scalar(nmax[:, c:c + 1], smax[:, c:c + 1], -ATT_SCALE, None, ALU.mult).then_inc(max_ready[l], 1)
                    elif kind == "PT":
                        if u == len(units) - 1:
                            normalise(u)
                        nk = 4 if s == 0 else 2
                        wait_full(dve, l, "PT", h, s, 0)
                        V.tensor_copy(probsT[:, u % 2, 0:nk, 0:P],
                                      bank(l, "PT", h, s, 0)[:, 0:P * nk].rearrange("p (k q) -> p k q", q=P)).then_inc(emptied["dve"], 1)
                    else:
                        wait_full(dve, l, "O", h, s)
                        half = slice(VD * (h % 2), VD * (h % 2) + VD)
                        V.tensor_copy(oT[half, h // 2, SEQ * s:SEQ * s + SEQ], bank(l, "O", h, s)[half, 0:SEQ]).then_inc(emptied["dve"], 1)

                def split_gate(n):
                    if n < 3 * KC:
                        w = gate_columns(dve, l, n)
                        dve.wait_ge(w_hi_ready[l], n + 1)
                        if n >= 2:
                            wait_full(dve, l, "g", *divmod(n - 2, KC))
                        V.tensor_tensor(w_lo[:, n % 2, :, :], w, w_hi[:, n % 2, :, :].bitcast(f32), ALU.subtract)\
                            .then_inc(w_lo_ready[l], 1)

                split_gate(0)
                for k in range(KC):
                    dve.wait_ge(h_hi_ready[l], k + 1)
                    V.tensor_tensor(h_lo[:, k, 0:n_tok], hT[:, k, 0:n_tok], h_hi[:, k, 0:n_tok].bitcast(f32), ALU.subtract)\
                        .then_inc(h_lo_ready[l], 1)
                split_gate(1)

                def split_branch(n):
                    b, dc = divmod(n, KC)
                    w = branch_columns(dve, l, n)
                    dve.wait_ge(v_hi_ready[l], n + 1)
                    V.tensor_tensor(v_lo[:, :, :], w, v_hi[:, :, :].bitcast(f32), ALU.subtract).then_inc(v_lo_ready[l], 1)
                    if dc == 0:
                        for c in range(4):
                            dve.wait_ge(br_hi_ready[l], 4 * b + c + 1)
                            V.tensor_tensor((oT_lo, bT_lo, fT_lo)[b][:, c, 0:n_tok], (oT, bT, fT)[b][:, c, 0:n_tok],
                                            br_hi[:, c, 0:n_tok].bitcast(f32), ALU.subtract).then_inc(br_lo_ready[l], 1)

                split_branch(0)
                for b in range(3):
                    for dc in range(KC):
                        n = b * KC + dc
                        wait_full(dve, l, "y", b, dc)
                        wait_emptied(dve, l, "g", b, dc)
                        if b == 0:
                            dst = mT[:, dc, 0:n_tok]
                        else:
                            m = n - KC
                            if m >= 2:
                                dve.wait_ge(merged[l], m - 1)
                            dst = ytmp[:, m % 2, 0:n_tok]
                        V.tensor_tensor(dst, bank(l, "y", b, dc)[:, 0:n_tok], tmp2[:, n % 2, 0:n_tok], ALU.mult)\
                            .then_inc(emptied["dve"], 1)
                        if n + 1 < 3 * KC:
                            split_branch(n + 1)
                        split_gate(n + 2)
                for j in range(2):
                    wait_arrived(dve, l, "out", j)
                    for k in range(KC):
                        if j == 0:
                            dve.wait_ge(h_hi_ready[l], KC + k + 1)
                            V.tensor_tensor(m_lo[:, k, 0:n_tok], mT[:, k, 0:n_tok], h_hi[:, k, 0:n_tok].bitcast(f32), ALU.subtract)\
                                .then_inc(h_lo_ready[l], 1)
                        w, high, low = out_weights(l, j, k)
                        dve.wait_ge(w_hi_ready[l], 3 * KC + KC * j + k + 1)
                        V.tensor_tensor(low, w, high.bitcast(f32), ALU.subtract).then_inc(w_lo_ready[l], 1)
                if l:
                    dve.wait_ge(grow_loaded, 32)
                for t in range(act):
                    c = 12 + 2 * t
                    dve.wait_ge(ssq_ready[l], counts["ssq"] + 2)
                    link(V.tensor_tensor(ssq[:, c:c + 1], ssq[:, c:c + 1], ssq[:, c + 1:c + 2], ALU.add))
                    mean_square(2, [(c, c + 1, DM)])
                    inverse_root(c, c + 1)
                    wait_emptied(dve, l, "out", t, 1)
                    link(V.scalar_tensor_tensor(rows[:, t % 2, :], rows[:, t % 2, :], rstd[:, c:c + 1], Grow[:, 0, t // 2, :],
                                                ALU.mult, ALU.mult))
                    V.tensor_tensor(xres[:, t, :], xres[:, t, :], rows[:, t % 2, :], ALU.add).then_inc(x_updated[l], 1)
                    if t >= 1:
                        invert_norm(t - 1)
                wait_full(dve, l, "out", act - 1, 1)
                for t in range(act - 1):
                    normalise_x(t)
                invert_norm(act - 1)
                normalise_x(act - 1)
                modulate(2)
                wait_emptied(dve, l, "rt", act - 1)
                sc, bi, mk, oh = score[:, 0:act], biased[:, 0:act], mask[:, 0:act], onehot[:, 0:act]
                tmp = oh_tmp[:, 0:act]
                link(V.tensor_tensor(bi, sc, brow.rearrange("p (a e) -> p a e", a=1).to_broadcast([P, act, NE]), ALU.add))
                for t in range(act):
                    link(V.max(m8[:, t, :], biased[:, t, :]))
                    link(V.max_index(idx8[:, t, :], m8[:, t, :], biased[:, t, :]))
                link(V.tensor_copy(idxf[:, 0:act, :], idx8[:, 0:act, :]))
                for t in range(act):
                    ins = V.tensor_tensor(oh[:, t], iota[:, 0:NE].rearrange("p (a e) -> p a e", a=1).to_broadcast([P, TOPK, NE]),
                                          idxf[:, t, 0:TOPK].rearrange("p (k a) -> p k a", a=1).to_broadcast([P, TOPK, NE]),
                                          ALU.is_equal)
                link(ins)
                V.tensor_reduce(mk, oh.rearrange("p t k e -> p t e k"), AX, ALU.add).then_inc(mask_ready[l], 1)

                def pick(dst, table):
                    for t in range(act):
                        ins = V.tensor_tensor(tmp[:, t], oh[:, t], table[:, t:t + 1, :].to_broadcast([P, TOPK, NE]), ALU.mult)
                    link(ins)
                    link(V.tensor_reduce(dst, tmp, AX, ALU.add))

                dve.wait_ge(ssq_ready[l], counts["ssq"])
                pick(pick_w[:, 0:act], score)
                link(V.tensor_reduce(rden[:, 0:act], pick_w[:, 0:act], AX, ALU.add))
                link(V.reciprocal(rden[:, 0:act], rden[:, 0:act]))
                for t in range(act):
                    V.tensor_scalar(pick_w[:, t, :], pick_w[:, t, :], rden[:, t:t + 1], ROUTED_SCALE, ALU.mult, ALU.mult)
                wait_full(dve, l, "rank")
                ranks = bank(l, "rank")
                V.tensor_tensor(needed, ranks[:, P:P + 1], item_t[:, l:l + 1], ALU.is_gt).then_inc(needed_ready[l], 1)
                V.scalar_tensor_tensor(place[:, 0:act], ranks[:, 0:NE * act].rearrange("p (t e) -> p t e", e=NE), float(NE),
                                       iota[:, 0:NE].rearrange("p (a e) -> p a e", a=1).to_broadcast([P, act, NE]),
                                       ALU.mult, ALU.add).then_inc(emptied["dve"], 1)
                wait_emptied(dve, l, "rank")
                pick(pos[:, 0:act], place)
                V.tensor_copy(posu[:, 0:act], pos[:, 0:act]).then_inc(pos_ready[l], 1)
                wait_full(dve, l, "turn")
                turns = bank(l, "turn")
                V.tensor_scalar(turn, iota, turns[:, 0:1], needed, ALU.is_equal, ALU.mult).then_inc(turn_ready[l], 1)
                link(V.tensor_scalar(over[0:1, :], item_t[0:1, 4:8], turns[0:1, 1:2], None, ALU.is_lt))
                link(V.tensor_reduce(more_f[0:1, :], over[0:1, :], AX, ALU.add))
                V.tensor_copy(more_u[0:1, :], more_f[0:1, :]).then_inc(emptied["dve"], 1)
                wait_full(dve, l, "items")
                V.tensor_scalar(item_col, bank(l, "items")[0:1, 0:MAX_ITEMS], float(P), None, ALU.add)
                V.tensor_copy(item_expert, bank(l, "items")[0:1, MAX_ITEMS:2 * MAX_ITEMS]).then_inc(emptied["dve"], 1)
                for f in range(2):
                    dve.wait_ge(ssilu_ready[l], f + 1)
                    V.tensor_tensor(act_s[:, f, 0:n_tok], ps[:, 512 * (2 + f):512 * (2 + f) + n_tok], silu_s[:, f, 0:n_tok], ALU.mult)\
                        .then_inc(sact_ready[l], 1)
                def make_rows():
                    split = P // CAP[l]
                    dve.wait_ge(table_read[l], 16 * split + 16)
                    ins = V.tensor_scalar(row_g[l], row_y, 2, None, ALU.logical_shift_right)
                    if split == 2:
                        link(ins)
                        link(V.tensor_scalar(row_g[l], row_g[l], 2.0, half_id, ALU.mult, ALU.add))
                        ins = V.tensor_scalar(row_y, row_y, 2.0, half_id, ALU.mult, ALU.add)
                    ins.then_inc(rows_ready[l], 1)
                if l:
                    make_rows()
                for g in range(2 * act):
                    b = 4 + g % 4
                    dve.wait_ge(sdn_full[l], g + 1)
                    V.tensor_copy(acc[:, g // 2, 512 * (g % 2):512 * (g % 2) + 512], ps[:, 512 * b:512 * b + 512])\
                        .then_inc(sdn_taken[l], 1)
                if l == 0:
                    make_rows()
                more = V.value_load(more_u[0:1, 0:1], min_val=0, max_val=4)
                half = wide[l] // 2
                fw = CAP[l] * 2

                def take_x(u, b, n=None):
                    dve.wait_ge(xt_full[l], 4 * b + u + 1)
                    if n is None or n >= 2:
                        dve.wait_ge(gu_full[l], 4 * b + u - 1)
                    V.tensor_copy(xT[u % 2][:, half:2 * half], ps[:, 1536:1536 + half]).then_inc(xt_dve[l], 1)

                def take_aT(u, b, n=None):
                    dve.wait_ge(at_full[l], 4 * b + u + 1)
                    if n is None or n >= 2:
                        dve.wait_ge(y_full[l], 4 * b + u - 1)
                    V.tensor_copy(aT_e[u % 2][:, 0:fw], ps[:, 2048:2048 + fw]).then_inc(at_ready[l], 1)

                def activate(u, b, n=None):
                    dve.wait_ge(silu_ready[l], 4 * b + u + 1)
                    if n is None or n >= 2:
                        dve.wait_ge(at_full[l], 4 * b + u - 1)
                    o = 512 * (u % 2) + fw
                    V.tensor_tensor(a_e[u % 2][:, 0:fw], ps[:, o:o + fw], silu_e[u % 2][:, 0:fw], ALU.mult).then_inc(a_ready[l], 1)

                def take_y(u, b, n=None):
                    if CAP[l] == P:
                        dve.wait_ge(y_full[l], 4 * b + u + 1)
                        if n is None or n >= 2:
                            dve.wait_ge(y_stored[l][(u - 2) % 4], 16 * b + (16 if u >= 2 else 0))
                        V.tensor_copy(y_e[u % 2][:, 512:1024], ps[:, 3072:3584]).then_inc(y_dve[l], 1)

                for n in range(UNROLL):
                    take_x(n, 0, n)
                    if n >= 2:
                        take_aT(n - 2, 0, n - 2)
                    if n >= 1:
                        activate(n - 1, 0, n - 1)
                    if n >= 2:
                        take_y(n - 2, 0, n - 2)
                with nc.vector.Fori(1, more + BLOCKS) as b:
                    for u in range(UNROLL):
                        take_x(u, b)
                        take_aT((u - 2) % 4, b - (u < 2))
                        activate((u - 1) % 4, b - (u < 1))
                        take_y((u - 2) % 4, b - (u < 2))
                last = more + (BLOCKS - 1)
                take_aT(2, last)
                activate(3, last)
                take_y(2, last)
                take_aT(3, last)
                take_y(3, last)

                def combine(t):
                    dve.wait_ge(picked_loaded[t % 2][l], 16 * (t // 2 + 1))
                    dve.wait_ge(sdn_taken[l], 2 * t + 2)
                    rowsk = picked[t % 2].rearrange("p (k d) -> p k d", k=TOPK)
                    for k in range(TOPK):
                        ins = V.scalar_tensor_tensor(acc[:, t, :], rowsk[:, k, :], pick_w[:, t, k:k + 1], acc[:, t, :], ALU.mult, ALU.add)
                        if k < TOPK - 1:
                            link(ins)
                    ins.then_inc(combined[l], 1)

                def add_experts(t):
                    mean_square(1, [(t, t + 1, DM)])
                    inverse_root(t, t + 1)
                    dve.wait_ge(combined[l], t + 1)
                    link(V.scalar_tensor_tensor(acc[:, t, :], acc[:, t, :], rstd[:, t:t + 1], Grow[:, 1, t // 2, :],
                                                ALU.mult, ALU.mult))
                    V.tensor_tensor(xres[:, t, :], xres[:, t, :], acc[:, t, :], ALU.add).then_inc(x_updated[l], 1)

                for t in range(act):
                    combine(t)
                    if t >= 1:
                        add_experts(t - 1)
                add_experts(act - 1)


_INS = ["x", "c", "ctx", "c_ctx", "w_ada", "b_ada", "g_pre_mix", "g_post_mix", "g_pre_ffn", "g_post_ffn", "w_in",
        "b_gate", "g_q", "w_uq", "g_kv", "w_ukv", "w_mla_out", "conv_w", "w_conv_out", "w_four_out", "w_out",
        "w_router", "b_router", "w_gate_e", "w_up_e", "w_down_e", "w_gate_s", "w_up_s", "w_down_s"]


def shape_tables():
    pos = np.arange(SEQ)
    pairs = ROPE // 4
    inv = (ROPE_BASE ** (-np.arange(pairs, dtype=np.float32) / pairs)).astype(np.float32)
    ang = np.concatenate([(pos // GRID_W)[:, None].astype(np.float32) * inv,
                          (pos % GRID_W)[:, None].astype(np.float32) * inv], axis=1).astype(np.float64)
    rope = np.stack([np.cos(ang), np.sin(ang)], axis=1).reshape(2, P, 2, ROPE // 2).transpose(1, 0, 2, 3)
    a = 2 * np.pi * (np.outer(np.arange(FC), np.arange(FC)) % FC) / FC
    chan = np.concatenate([np.cos(a), np.sin(a)], axis=1) / np.sqrt(FC)
    b = 2 * np.pi * (np.outer(pos, pos) % SEQ) / SEQ
    seq = (np.stack([np.cos(b), -np.sin(b)]) / np.sqrt(SEQ)).reshape(2, 2, P, SEQ).transpose(2, 0, 1, 3).reshape(P, 1024)
    return {"ident": np.eye(P, dtype=np.float32),
            "tri": np.concatenate([np.ones((P, P)), np.triu(np.ones((P, P)), 1)], axis=1).astype(np.float32),
            "pick_id": (TOPK * (P * np.arange(NTILE)[None, :, None] + np.arange(P)[:, None, None])
                        + np.arange(TOPK)[None, None, :]).astype(np.uint32),
            "item_t": item_tables(),
            "half_id": (np.arange(P)[:, None] // (P // 2)).astype(np.float32),
            "absent": np.full((P * NTILE * NE, 1), ABSENT, dtype=np.uint32),
            "iota": np.tile(np.arange(MAX_ITEMS, dtype=np.float32), (P, 1)),
            "rope": np.ascontiguousarray(rope, dtype=np.float32),
            "dft": np.ascontiguousarray(np.concatenate([chan, seq], axis=1), dtype=np.float32)}


def item_tables():
    column = np.arange(P)
    t = np.zeros((P, 10), dtype=np.float32)
    for l in range(DEPTH):
        t[:, l] = np.where(column < NE, -1, column // NE * CAP[l])
    t[:, 2], t[:, 3] = column - P, column % NE
    t[:, 4:8] = NE + UNROLL * np.arange(4)
    for s in range(2):
        t[:, 8 + s] = (column % 32 == s) | (column == 2)
    return t


def kernel(**inputs):
    import concourse.bacc as _bacc
    from concourse.bass_utils import run_bass_kernel_spmd as _run

    nc = _bacc.Bacc("TRN2", target_bir_lowering=False, num_devices=1)
    arrays, I, C = {}, {}, {}
    for group, into in (({n: inputs[n] for n in _INS}, I), (shape_tables(), C)):
        for name, a in group.items():
            a = np.ascontiguousarray(a)
            arrays[f"in_{name}"] = a
            into[name] = nc.dram_tensor(f"in_{name}", a.shape, mybir.dt.from_np(a.dtype), kind="ExternalInput").ap()
    out = nc.dram_tensor("out_0", (1, SEQ, DM), mybir.dt.float32, kind="ExternalOutput").ap()
    hybrid_layers(nc, I, C, out)
    r = _run(nc, [arrays], core_ids=[0])
    return r.results[0]["out_0"]
```
